# Optimizing a Trainium2 kernel written in Bass

```python
import math
import jax, jax.numpy as jnp
from jax import lax
import numpy as np

D_MODEL = 1024
BATCH = 1
SEQ = 128
DEPTH = 1
DEC_BATCH = 1
DEC_SEQ = 512
PAST_LEN = 256

GRID_W = 64
HEAD_DIM = 64
HEADS_A = 8
KV_HEADS_A = 2
GROUP_A = HEADS_A // KV_HEADS_A
HEADS_B = 4
VDIM_B = 2 * HEAD_DIM
WIDTH_A = HEADS_A * HEAD_DIM
WIDTH_B = HEADS_B * VDIM_B
N_EXPERTS = 16
EXPERT_DIM = 1024
CAPACITY_FACTOR = 2
Q_BLOCK = 128
ROPE_THETA = 10000.0
EPS = 1e-6
SPLIT_SIZES = (HEADS_A * HEAD_DIM, KV_HEADS_A * HEAD_DIM, KV_HEADS_A * HEAD_DIM,
               HEADS_B * 2 * HEAD_DIM, HEADS_B * 2 * HEAD_DIM, HEADS_B * VDIM_B,
               D_MODEL, D_MODEL)
IN_WIDTH = sum(SPLIT_SIZES)

kernel_name = 'hybrid_diffusion_gqa_diffattn_ecmoe_step'

def rms_norm(x, g):
    xf = x.astype(jnp.float32)
    y = xf * lax.rsqrt(jnp.mean(xf * xf, axis=-1, keepdims=True) + EPS)
    return (y * g.astype(jnp.float32)).astype(x.dtype)

def rope_tables(n_tokens):
    n_rows = n_tokens // GRID_W
    row = jnp.repeat(jnp.arange(n_rows), GRID_W).astype(jnp.float32)
    col = jnp.tile(jnp.arange(GRID_W), n_rows).astype(jnp.float32)
    quarter = HEAD_DIM // 4
    freqs = ROPE_THETA ** (-jnp.arange(quarter, dtype=jnp.float32) / quarter)
    ang = jnp.stack([row[:, None] * freqs, col[:, None] * freqs], axis=1)
    return jnp.cos(ang)[:, None], jnp.sin(ang)[:, None]

def apply_rope_2d(x, cos, sin):
    shp = x.shape
    xf = x.astype(jnp.float32).reshape(shp[0], shp[1], -1, 2, 2, HEAD_DIM // 4)
    xa, xb = xf[..., 0, :], xf[..., 1, :]
    out = jnp.stack([xa * cos - xb * sin, xa * sin + xb * cos], axis=-2)
    return out.reshape(shp).astype(x.dtype)

def sweep_query_blocks(fn, q):
    b, s = q.shape[:2]
    nb = s // Q_BLOCK
    qb = jnp.moveaxis(q.reshape((b, nb, Q_BLOCK) + q.shape[2:]), 1, 0)
    out = lax.map(fn, qb)
    return jnp.moveaxis(out, 0, 1).reshape((b, s) + out.shape[3:])

def gqa_block(qb, k, v):
    s = jnp.einsum('bqhgd,bshd->bhgqs', qb, k).astype(jnp.float32) * (HEAD_DIM ** -0.5)
    p = jax.nn.softmax(s, axis=-1).astype(v.dtype)
    return jnp.einsum('bhgqs,bshd->bqhgd', p, v)

def diff_block(qb, k, v, lam):
    s = jnp.einsum('bqhmd,bshmd->bhmqs', qb, k).astype(jnp.float32) * (HEAD_DIM ** -0.5)
    p = jax.nn.softmax(s, axis=-1)
    a = p[:, :, 0] - lam[None, :, None, None] * p[:, :, 1]
    return jnp.einsum('bhqs,bshe->bqhe', a.astype(v.dtype), v)

def token_mixing(h, mix_w, rope, ctx, lam_init):
    (w_in, g_q, g_k, lq1, lk1, lq2, lk2, g_diff, w_ba, w_bb, w_out) = mix_w
    b, s, _ = h.shape
    offsets = np.cumsum(SPLIT_SIZES)[:-1].tolist()
    qa, ka, va, qb, kb, vb, ga, gb = jnp.split(h @ w_in, offsets, axis=-1)
    qa = rms_norm(qa.reshape(b, s, KV_HEADS_A, GROUP_A, HEAD_DIM), g_q)
    ka = rms_norm(ka.reshape(b, s, KV_HEADS_A, HEAD_DIM), g_k)
    va = va.reshape(b, s, KV_HEADS_A, HEAD_DIM)
    qb = qb.reshape(b, s, HEADS_B, 2, HEAD_DIM)
    kb = kb.reshape(b, s, HEADS_B, 2, HEAD_DIM)
    vb = vb.reshape(b, s, HEADS_B, VDIM_B)
    own_ctx = (ka, va, kb, vb)
    if rope is not None:
        cos, sin = rope
        qa, ka = apply_rope_2d(qa, cos, sin), apply_rope_2d(ka, cos, sin)
        qb, kb = apply_rope_2d(qb, cos, sin), apply_rope_2d(kb, cos, sin)
    if ctx is not None:
        ka = jnp.concatenate([ctx[0].astype(ka.dtype), ka], axis=1)
        va = jnp.concatenate([ctx[1].astype(va.dtype), va], axis=1)
        kb = jnp.concatenate([ctx[2].astype(kb.dtype), kb], axis=1)
        vb = jnp.concatenate([ctx[3].astype(vb.dtype), vb], axis=1)
    ya = sweep_query_blocks(lambda q: gqa_block(q, ka, va), qa).reshape(b, s, WIDTH_A)
    lam = (jnp.exp(jnp.sum(lq1.astype(jnp.float32) * lk1.astype(jnp.float32), axis=-1))
           - jnp.exp(jnp.sum(lq2.astype(jnp.float32) * lk2.astype(jnp.float32), axis=-1)) + lam_init)
    yb = sweep_query_blocks(lambda q: diff_block(q, kb, vb, lam), qb)
    yb = (rms_norm(yb, g_diff) * (1.0 - lam_init)).reshape(b, s, WIDTH_B)
    merged = jax.nn.sigmoid(ga) * (ya @ w_ba) + jax.nn.sigmoid(gb) * (yb @ w_bb)
    return merged @ w_out, own_ctx

def expert_choice_ffn(h, w_router, w_gate, w_up, w_down):
    b, n, d = h.shape
    cap = CAPACITY_FACTOR * n // N_EXPERTS
    aff = jax.nn.softmax(jnp.einsum('bnd,de->bne', h, w_router).astype(jnp.float32), axis=-1)
    gates, idx = lax.top_k(jnp.swapaxes(aff, 1, 2), cap)
    xe = jax.vmap(lambda hb, ib: hb[ib])(h, idx)
    a = jnp.einsum('becd,edf->becf', xe, w_gate)
    u = jnp.einsum('becd,edf->becf', xe, w_up)
    ye = jnp.einsum('becf,efd->becd', jax.nn.silu(a) * u, w_down) * gates[..., None].astype(h.dtype)
    return jax.vmap(lambda yb, ib: jnp.zeros((n, d), yb.dtype).at[ib.reshape(-1)].add(yb.reshape(-1, d)))(ye, idx)

def trunk_layer(x, mod, g_attn, g_ffn, mix_w, moe_w, rope, ctx, lam_init):
    shift1, scale1, gate1, shift2, scale2, gate2 = jnp.split(mod, 6, axis=-1)
    h = rms_norm(x, g_attn) * (1.0 + scale1) + shift1
    m, own_ctx = token_mixing(h, mix_w, rope, ctx, lam_init)
    x = x + gate1 * m
    h = rms_norm(x, g_ffn) * (1.0 + scale2) + shift2
    x = x + gate2 * expert_choice_ffn(h, *moe_w)
    return x, own_ctx

def setup_inputs(seed: int = 0) -> dict:
    key = jax.random.key(seed)
    ks = jax.random.split(key, 32)
    nrm = lambda k, shape, scale: jax.random.normal(k, shape, jnp.float32) * scale
    gain = lambda k, shape: 1.0 + 0.02 * jax.random.normal(k, shape, jnp.float32)
    return {
        'x_prompt': nrm(ks[0], (BATCH, SEQ, D_MODEL), 1.0),
        'x_sample': nrm(ks[1], (DEC_BATCH, DEC_SEQ, D_MODEL), 1.0),
        'cache_attn_k': nrm(ks[2], (DEC_BATCH, DEPTH, PAST_LEN, KV_HEADS_A, HEAD_DIM), 1.0),
        'cache_attn_v': nrm(ks[3], (DEC_BATCH, DEPTH, PAST_LEN, KV_HEADS_A, HEAD_DIM), 1.0),
        'cache_diff_k': nrm(ks[4], (DEC_BATCH, DEPTH, PAST_LEN, HEADS_B, 2, HEAD_DIM), 1.0),
        'cache_diff_v': nrm(ks[5], (DEC_BATCH, DEPTH, PAST_LEN, HEADS_B, VDIM_B), 1.0),
        'c': nrm(ks[6], (DEC_BATCH, D_MODEL), 1.0),
        'c_ctx': nrm(ks[7], (D_MODEL,), 1.0),
        'w_mod': nrm(ks[8], (DEPTH, D_MODEL, 6 * D_MODEL), 0.5 * D_MODEL ** -0.5),
        'b_mod': nrm(ks[9], (DEPTH, 6 * D_MODEL), 0.01),
        'g_attn_norm': gain(ks[10], (DEPTH, D_MODEL)),
        'g_ffn_norm': gain(ks[11], (DEPTH, D_MODEL)),
        'w_in': nrm(ks[12], (DEPTH, D_MODEL, IN_WIDTH), D_MODEL ** -0.5),
        'g_q_norm': gain(ks[13], (DEPTH, HEAD_DIM)),
        'g_k_norm': gain(ks[14], (DEPTH, HEAD_DIM)),
        'lambda_q1': nrm(ks[15], (DEPTH, HEADS_B, HEAD_DIM), 0.1),
        'lambda_k1': nrm(ks[16], (DEPTH, HEADS_B, HEAD_DIM), 0.1),
        'lambda_q2': nrm(ks[17], (DEPTH, HEADS_B, HEAD_DIM), 0.1),
        'lambda_k2': nrm(ks[18], (DEPTH, HEADS_B, HEAD_DIM), 0.1),
        'g_diff_norm': gain(ks[19], (DEPTH, VDIM_B)),
        'w_branch_a': nrm(ks[20], (DEPTH, WIDTH_A, D_MODEL), WIDTH_A ** -0.5),
        'w_branch_b': nrm(ks[21], (DEPTH, WIDTH_B, D_MODEL), WIDTH_B ** -0.5),
        'w_out': nrm(ks[22], (DEPTH, D_MODEL, D_MODEL), D_MODEL ** -0.5),
        'w_router': nrm(ks[23], (DEPTH, D_MODEL, N_EXPERTS), D_MODEL ** -0.5),
        'w_exp_gate': nrm(ks[24], (DEPTH, N_EXPERTS, D_MODEL, EXPERT_DIM), D_MODEL ** -0.5),
        'w_exp_up': nrm(ks[25], (DEPTH, N_EXPERTS, D_MODEL, EXPERT_DIM), D_MODEL ** -0.5),
        'w_exp_down': nrm(ks[26], (DEPTH, N_EXPERTS, EXPERT_DIM, D_MODEL), EXPERT_DIM ** -0.5),
        'g_final': gain(ks[27], (D_MODEL,)),
    }

def reference(x_prompt, x_sample, cache_attn_k, cache_attn_v, cache_diff_k, cache_diff_v, c,
              c_ctx, w_mod, b_mod, g_attn_norm, g_ffn_norm, w_in, g_q_norm, g_k_norm,
              lambda_q1, lambda_k1, lambda_q2, lambda_k2, g_diff_norm, w_branch_a, w_branch_b,
              w_out, w_router, w_exp_gate, w_exp_up, w_exp_down, g_final):
    rope = rope_tables(x_sample.shape[1])
    xp, xs = x_prompt, x_sample
    ak, av, dk, dv = [], [], [], []
    for l in range(DEPTH):
        lam_init = 0.8 - 0.6 * math.exp(-0.3 * l)
        mix_w = (w_in[l], g_q_norm[l], g_k_norm[l], lambda_q1[l], lambda_k1[l], lambda_q2[l],
                 lambda_k2[l], g_diff_norm[l], w_branch_a[l], w_branch_b[l], w_out[l])
        moe_w = (w_router[l], w_exp_gate[l], w_exp_up[l], w_exp_down[l])
        mod_ctx = (jax.nn.silu(c_ctx) @ w_mod[l] + b_mod[l])[None, None, :]
        mod_lat = (jax.nn.silu(c) @ w_mod[l] + b_mod[l])[:, None, :]
        xp, (ka, va, kb, vb) = trunk_layer(xp, mod_ctx, g_attn_norm[l], g_ffn_norm[l], mix_w, moe_w,
                                           None, None, lam_init)
        ak.append(ka); av.append(va); dk.append(kb); dv.append(vb)
        ctx = (cache_attn_k[:, l], cache_attn_v[:, l], cache_diff_k[:, l], cache_diff_v[:, l])
        xs, _ = trunk_layer(xs, mod_lat, g_attn_norm[l], g_ffn_norm[l], mix_w, moe_w,
                            rope, ctx, lam_init)
    y_prompt = rms_norm(xp, g_final)
    y_sample = rms_norm(xs, g_final)
    new_attn_k = jnp.stack(ak, axis=1)
    new_attn_v = jnp.stack(av, axis=1)
    new_diff_k = jnp.stack(dk, axis=1)
    new_diff_v = jnp.stack(dv, axis=1)
    return (y_prompt, y_sample, new_attn_k, new_attn_v, new_diff_k, new_diff_v)


_drawn_inputs = setup_inputs


def setup_inputs(seed=0):
    import zlib

    import numpy as np

    out = dict(_drawn_inputs(seed))
    spreads = {}
    factors = {'cache_attn_k': 8.0,
     'cache_attn_v': 8.0,
     'b_mod': 4.145,
     'g_attn_norm': 3.049,
     'g_ffn_norm': 8.0,
     'g_q_norm': 8.0,
     'g_k_norm': 2.912,
     'lambda_q1': 7.053,
     'lambda_k1': 6.104,
     'lambda_q2': 7.071,
     'lambda_k2': 5.793,
     'g_diff_norm': 8.0,
     'g_final': 9.783,
     'cache_diff_k': 8.0,
     'cache_diff_v': 8.0}
    for name, (base, spread) in spreads.items():
        noise = np.random.default_rng([zlib.crc32(name.encode()), seed]).standard_normal(out[name].shape)
        drawn = base * np.exp(spread * noise) if base else spread * noise
        out[name] = __import__('jax').numpy.asarray(drawn.astype(out[name].dtype))
    for name, factor in factors.items():
        out[name] = (out[name] * factor).astype(out[name].dtype)
    return out
```

```python
from contextlib import ExitStack

import concourse.bass as bass
from concourse import mybir

F32 = mybir.dt.float32
F32R = mybir.dt.float32r
ALU = mybir.AluOpType
ACT = mybir.ActivationFunctionType
AX = mybir.AxisListType

P = 128
D = 1024
KD = D // P
LAT, CTX = 512, 128
TOK = LAT + CTX
NT = TOK // P
NTL = LAT // P
PAST = 256
HD = 64
HA, KVA = 8, 2
HB = 4
MAPS = HA + 2 * HB
KMAPS = KVA + 2 * HB
KEYS = PAST + TOK
KT = KEYS // P
KTL = (PAST + LAT) // P
NE = 16
CAPL, CAPC = 2 * LAT // NE, 2 * CTX // NE
LAM_INIT = 0.8 - 0.6 * 1.0
EPS = 1e-6
SCALE = HD ** -0.5
NW = 512
CH = 2048
HALF = CH // 2
NRAW, NHL = 4, 3
EG = 4
NG = NE // EG
PITCH = 416

WIN = [0, 80, 208, 288]
LCOL = [0, 144, 208, 352]
CROW = [64, 0, 96, 32]
CCOL = [WIN[e] + CROW[e] for e in range(EG)]

GEMMS = [("qa", 512, 8), ("qb", 512, 8), ("kv", 256, 8), ("kb", 512, 8), ("vb", 512, 8),
         ("ga0", 512, 8), ("wa0", 512, 4), ("gb0", 512, 8), ("wb0", 512, 4),
         ("ga1", 512, 8), ("wa1", 512, 4), ("gb1", 512, 8), ("wb1", 512, 4),
         ("out0", 512, 8), ("out1", 512, 8)]
W_IN_COL = {"qa": 0, "kv": 512, "qb": 768, "kb": 1280, "vb": 1792, "ga0": 2304, "ga1": 2816,
            "gb0": 3328, "gb1": 3840}
GN = [g[0] for g in GEMMS]
FREED_BY = {"qa": "dve", "qb": "act", "kv": "dve", "kb": "act", "vb": "act"}
for _n in GN[5:]:
    FREED_BY[_n] = "act" if _n[0] == "g" else "dve"
STREAM = [("mod", j) for j in range(4)] + [("gemm", j) for j in range(13)] + \
         [("mod", j) for j in range(4, 12)] + [("gemm", j) for j in (13, 14)]
FIRST = {}
NHALF = {}
_h = 0
for _e in STREAM:
    _n = 4 if _e[0] == "mod" else (GEMMS[_e[1]][1] * GEMMS[_e[1]][2]) // HALF
    FIRST[_e], NHALF[_e] = _h, _n
    _h += _n
DENSE_HALVES = _h
HALVES_B = FIRST[("gemm", 5)]
GH = 24 * EG
NB6 = 6

UNITS = [(m, t) for m in range(HA) for t in range(NT)] + \
        [(HA + 2 * h + i, t) for h in range(HB) for t in range(NT) for i in range(2)]
NU = len(UNITS)
U_FIRST = {m: min(s for s, u in enumerate(UNITS) if u[0] == m) for m in range(MAPS)}
U_LAST = {m: max(s for s, u in enumerate(UNITS) if u[0] == m) for m in range(MAPS)}
PREP = {m: 0 if m == 0 else U_FIRST[m] - (2 if m <= HA else 1) for m in range(MAPS)}
PU_OF, PUS = {}, []
for _s, (_m, _t) in enumerate(UNITS):
    if _m < HA or (_m - HA) % 2 == 1:
        PU_OF[_s] = len(PUS)
        PUS.append((_m if _m < HA else HA + (_m - HA) // 2, _t, _s))
BLOCKS = [(h, b) for h in range(HA + HB) for b in range(3)]
BLK_OF = {i: BLOCKS.index((h, min(t // 2, 2))) for i, (h, t, _) in enumerate(PUS)}
BLK_END = {BLK_OF[i]: i for i in range(len(PUS))}
LAG = 2

T_ID, T_IOTA, T_SLAT, T_SCTX, T_EPS, T_NH, T_ONES = 0, 128, 192, 193, 194, 195, 196
T_KEPT = 200
T_SEL, T_SB, T_MEAN, T_COS, T_SIN = 200, 202, 458, 586, 842
T_W = 1098


def table_of_constants():
    import numpy as np
    t = np.zeros((P, T_W), np.float32)
    p = np.arange(P)
    t[:, T_ID:T_ID + P] = np.eye(P)
    t[:, T_IOTA:T_IOTA + 64] = np.arange(64)
    t[:, T_SLAT] = p % 64
    t[:, T_SCTX] = p % 32
    t[:, T_EPS] = EPS
    t[:, T_NH] = -0.5
    t[:, T_ONES] = 1.0
    t[0:4:2, T_SEL] = 1.0
    t[1:4:2, T_SEL + 1] = 1.0
    t[0:4:2, T_SB:T_SB + P] = 1.0
    t[1:4:2, T_SB + P:T_SB + 2 * P] = 1.0
    t[:, T_MEAN:T_MEAN + P] = 1.0 / P
    n = np.arange(LAT)
    freqs = np.float32(10000.0) ** (-np.arange(16, dtype=np.float32) / np.float32(16))
    ang = np.stack([(n // 64).astype(np.float32)[:, None] * freqs,
                    (n % 64).astype(np.float32)[:, None] * freqs], 1)
    c, s = np.cos(ang), np.sin(ang)
    cos = np.stack([c, c], 2).reshape(NTL, P, 64)
    sin = np.stack([-s, s], 2).reshape(NTL, P, 64)
    t[:, T_COS:T_COS + 256] = cos.transpose(1, 0, 2).reshape(P, 256)
    t[:, T_SIN:T_SIN + 256] = sin.transpose(1, 0, 2).reshape(P, 256)
    return t


def build(nc, x_prompt, x_sample, cache_attn_k, cache_attn_v, cache_diff_k, cache_diff_v, c, c_ctx,
          w_mod, b_mod, g_attn_norm, g_ffn_norm, w_in, g_q_norm, g_k_norm, lambda_q1, lambda_k1,
          lambda_q2, lambda_k2, g_diff_norm, w_branch_a, w_branch_b, w_out, w_router, w_exp_gate,
          w_exp_up, w_exp_down, g_final, constants,
          y_prompt, y_sample, new_attn_k, new_attn_v, new_diff_k, new_diff_v):
    ctx = ExitStack()
    with ctx:
        def sb(name, shape, dt=F32):
            return ctx.enter_context(nc.sbuf_tensor(name, shape, dt))

        def sem(name):
            return ctx.enter_context(nc.semaphore(name))


        raw = sb("raw", [P, NRAW, CH])
        tab = sb("tab", [P, T_KEPT])
        mod_t = sb("mod_t", [P, 6 * KD, 2])
        scale1 = sb("scale1", [P, KD, 2])
        scale2 = sb("scale2", [P, KD, 2])
        vec_t = sb("vec_t", [P, 81])
        c_hi = sb("c_hi", [P, KD, 4], F32R)
        c_lo = sb("c_lo", [P, KD, 4], F32R)
        g_qk = sb("g_qk", [P, 2, HD])
        ss = sb("ss", [P, NT])
        rs = sb("rs", [P, NT])
        q_ss = sb("q_ss", [P, NT, HA])
        q_rs = sb("q_rs", [P, NT, HA])
        neg_max = sb("neg_max", [P, 8])
        row_sum = sb("row_sum", [P, 8])
        row_inv = sb("row_inv", [P, 8])
        lam = sb("lam", [P, 3 * HB])
        g_dif = sb("g_dif", [P, 1])
        aff_n = sb("aff_n", [P, NT, NE])
        pos_n = sb("pos_n", [P, NT, NE])
        gate_p = sb("gate_p", [P, 3])
        gate_e = sb("gate_e", [P, EG])
        base = nc.sbuf_base + (-nc.sbuf_base) % 32
        room = nc.sbuf_usable_end - base

        def at(name, offset, shape, dt=F32):
            size = 4
            for n in shape[1:]:
                size *= n
            assert offset + size <= room, (name, offset + size, room)
            return nc.alloc_sbuf_tensor_at(name, shape, dt, offset=base + offset)

        ident = tab[:, T_ID:T_ID + P]
        eps = tab[:, T_EPS:T_EPS + 1]
        minus_half = tab[:, T_NH:T_NH + 1]
        one = tab[:, T_ONES:T_ONES + 1]

        RING = 151584
        w_hi = at("w_hi", RING, [P, NHL, HALF], F32R)
        w_lo = at("w_lo", RING + 12288, [P, NHL, HALF], F32R)
        ht_hi = at("ht_hi", 0, [P, KD, TOK], F32R)
        ht_lo = at("ht_lo", 20480, [P, KD, TOK], F32R)
        keys_t = at("keys_t", 40960, [P, KMAPS, KEYS], F32R)
        squares = at("squares", 40960, [P, D])
        va_hi = at("va_hi", 76800, [P, KT, P], F32R)
        va_lo = at("va_lo", 80384, [P, KT, P], F32R)
        vb_n = at("vb_n", 83968, [P, KT, HB * P])
        x_n = at("x_n", 98304, [P, NT, D])
        q_n = at("q_n", 98304, [P, NT, MAPS, HD])
        T0 = 118784
        q_sq = at("q_sq", T0, [P, 2, NW])
        mod_row = at("mod_row", T0, [4, 2, NW])
        h_tmp = at("h_tmp", T0 + 4096, [P, TOK])
        rope_a = at("rope_a", T0 + 4096, [P, NW])
        rope_b = at("rope_b", T0 + 6144, [P, NW])
        k_n = at("k_n", T0 + 8192, [P, NT, KMAPS, HD])
        vec = at("vec", T0 + 8192, [81, P])
        lam_w = at("lam_w", T0 + 8704, [P, 4, HB, HD])
        ka_parts = at("ka_parts", T0 + 20992, [P, KVA, 2, HD], F32R)
        kb_parts = at("kb_parts", T0 + 22016, [P, 2 * HB, 2, HD], F32R)
        k_cache = at("k_cache", T0 + 26112, [P, KMAPS, HD])
        va_cache = at("va_cache", T0 + 6656, [P, 2, P])
        va_ctx = at("va_ctx", T0 + 28672, [P, P])
        tab2 = at("tab2", T0 + 29184, [P, T_W - T_KEPT])
        probs = at("probs", 0, [P, 4, KTL * P])
        q_parts = at("q_parts", 12288, [P, NT, 4, HD], F32R)
        q_hi_t = at("q_hi_t", 17408, [P, 2, TOK], F32R)
        q_lo_t = at("q_lo_t", 22528, [P, 2, TOK], F32R)
        vb_hi = at("vb_hi", 27648, [P, KT, P], F32R)
        vb_lo = at("vb_lo", 31232, [P, KT, P], F32R)
        y_t = at("y_t", T0, [P, 8, TOK])
        p_hi = at("p_hi", RING, [P, 2, KTL, 2 * P], F32R)
        p_lo = at("p_lo", RING + 12288, [P, 2, KTL, 2 * P], F32R)
        y_sq = at("y_sq", 81920, [P, 2, TOK])
        y_rms = at("y_rms", 87040, [P, 2, TOK])
        yt_hi = at("yt_hi", 40960, [P, 8, TOK], F32R)
        yt_lo = at("yt_lo", 61440, [P, 8, TOK], F32R)
        mt_hi = at("mt_hi", 81920, [P, KD, TOK], F32R)
        mt_lo = at("mt_lo", 102400, [P, KD, TOK], F32R)
        sig = at("sig", 122880, [P, NT, NW])
        merged = at("merged", 133120, [P, NT, NW])
        gate1 = at("gate1", 0, [P, 2, D])
        gate2 = at("gate2", 8192, [P, 2, D])
        mod_row2 = at("mod_row2", 16384, [4, 2, NW])
        x_r = at("x_r", 40960, [P, NT, D])
        out_tmp = at("out_tmp", 61440, [P, 2, NW])
        xn_hi = at("xn_hi", 0, [P, NT, D], F32R)
        xn_lo = at("xn_lo", 20480, [P, NT, D], F32R)
        xn_f = at("xn_f", 122880, [P, NT, D])
        h2_t = at("h2_t", 61440, [P, KD, TOK])
        squares2 = at("squares2", 104448, [P, D])
        lg_t = at("lg_t", 81920, [NE, TOK])
        aff_t = at("aff_t", 84480, [NE, TOK])
        left = at("left", 87040, [NE, TOK])
        count = at("count", 89600, [NE, TOK])
        chosen = at("chosen", 92160, [NE, TOK])
        pos_t = at("pos_t", 94720, [NE, TOK])
        ones16 = at("ones16", 97280, [NE, LAT])
        soft = at("soft", 99328, [P, NT, NE])
        top8 = at("top8", 99648, [NE, 10, 8])
        router = at("router", 100352, [P, KD, NE])
        soft_s = at("soft_s", 100096, [P, 3, NT])
        acc = at("acc", 40960, [P, NT, D])
        xe_hi = at("xe_hi", 61440, [P, KD, PITCH], F32R)
        xe_lo = at("xe_lo", 74752, [P, KD, PITCH], F32R)
        xc_f = at("xc_f", 88064, [P, KD, NE * CAPC])
        xc_g = at("xc_g", 96256, [P, KD, EG * CAPC])
        ht2_hi = at("ht2_hi", 96256, [P, KD, P], F32R)
        ht2_lo = at("ht2_lo", 100352, [P, KD, P], F32R)
        h_act = at("h_act", 104448, [P, 2, NW])
        ye_hi = at("ye_hi", 108544, [P, 2, D], F32R)
        ye_lo = at("ye_lo", 116736, [P, 2, D], F32R)
        yc_hi = at("yc_hi", 124928, [P, D], F32R)
        yc_lo = at("yc_lo", 129024, [P, D], F32R)
        ye_f = at("ye_f", 133120, [P, D])
        sel_c = at("sel_c", 133120, [P, NE, CAPC], F32R)
        sel_g = at("sel_g", 137216, [P, NTL, EG * CAPL], F32R)
        pos_b = at("pos_b", 141312, [P, NW])
        aff_b = at("aff_b", 143360, [P, NW])
        sel_t = at("sel_t", 145408, [P, 2, LAT], F32R)
        sel_tc = at("sel_tc", 149504, [P, CTX], F32R)
        x_f = at("x_f", 0, [P, NT, D])
        gate2_f = at("gate2_f", 20480, [P, 2, D])
        g_fin = at("g_fin", 28672, [P, D])
        ge_tmp = at("ge_tmp", 32768, [P, D])

        ht_dram = nc.dram_tensor("ht_dram", [P, 2, KD * TOK], F32R).ap()
        x1_dram = nc.dram_tensor("x1_dram", [P, NT, D], F32).ap()
        g2_dram = nc.dram_tensor("g2_dram", [P, 2, D], F32).ap()
        pos_dram = nc.dram_tensor("pos_dram", [NE, TOK], F32).ap()
        aff_dram = nc.dram_tensor("aff_dram", [NE, TOK], F32).ap()

        ps = ctx.enter_context(nc.psum_tensor("ps", [P, 8 * 512], F32))

        def bank(b, lo=0, hi=512, rows=slice(None)):
            return ps[rows, 512 * b + lo:512 * b + hi]

        s_tab = sem("s_tab"); s_tab2 = sem("s_tab2"); s_vec = sem("s_vec"); s_x = [sem(f"s_tokens{t}") for t in range(NT)]
        s_bc = sem("s_bc"); s_router = sem("s_router")
        s_raw = [sem(f"s_raw{n}") for n in range(NRAW)]
        s_hi = sem("s_hi"); s_lo = sem("s_lo"); s_half = sem("s_half")
        s_silu = sem("s_silu"); s_vect = sem("s_vect"); s_vec_cp = sem("s_vec_cp"); s_csplit = sem("s_csplit")
        s_row = sem("s_row"); s_post = sem("s_post"); s_mod = sem("s_mod"); s_scale = sem("s_scale")
        s_lamw = sem("s_lamw"); s_lame = sem("s_lame"); s_lam = sem("s_lam")
        s_ss = sem("s_ss"); s_rs = sem("s_rs"); s_xn = sem("s_xn"); s_xt = sem("s_xt")
        s_hth = sem("s_hth"); s_htl = sem("s_htl"); s_spill = sem("s_spill"); s_refill = sem("s_refill")
        s_acc = sem("s_acc"); s_free_d = sem("s_free_d"); s_free_a = sem("s_free_a")
        s_qsq = sem("s_qsq"); s_qss = sem("s_qss"); s_qrs = sem("s_qrs"); s_vah = sem("s_vah")
        s_dve = sem("s_dve"); s_pool = sem("s_pool"); s_act = sem("s_act")
        s_qn = sem("s_qn"); s_kparts = sem("s_kparts"); s_ktr = sem("s_ktr"); s_kev = sem("s_kev")
        s_kc = [sem("s_kc0"), sem("s_kc1")]; s_vc = sem("s_vc"); s_vac = sem("s_vac")
        s_qp = sem("s_qp"); s_qtr = sem("s_qtr"); s_qh = sem("s_qh"); s_ql = sem("s_ql")
        s_sc = sem("s_sc"); s_max = sem("s_max"); s_exp = sem("s_exp"); s_rinv = sem("s_rinv")
        s_nrm = sem("s_nrm"); s_c1 = sem("s_c1"); s_comb = sem("s_comb"); s_ptr = sem("s_ptr")
        s_ph = sem("s_ph"); s_pl = sem("s_pl"); s_pv = sem("s_pv"); s_oev = sem("s_oev"); s_vb = sem("s_vb")
        s_ysq = sem("s_ysq"); s_yms = sem("s_yms"); s_yrt = sem("s_yrt"); s_yn = sem("s_yn")
        s_yh = sem("s_yh"); s_yl = sem("s_yl")
        s_mrg = sem("s_mrg"); s_mtr = sem("s_mtr"); s_mth = sem("s_mth"); s_mtl = sem("s_mtl")
        s_gb1 = sem("s_gb1"); s_gb2 = sem("s_gb2"); s_g2out = sem("s_g2out"); s_xr = sem("s_xr")
        s_x1 = sem("s_x1"); s_x1out = sem("s_x1out"); s_ss2 = sem("s_ss2"); s_rs2 = sem("s_rs2")
        s_xf = sem("s_xf"); s_xh = sem("s_xh"); s_xl = sem("s_xl"); s_x2t = sem("s_x2t"); s_h2 = sem("s_h2")
        s_lgt = sem("s_lgt"); s_lgc = sem("s_lgc"); s_lgn = sem("s_lgn"); s_sub = sem("s_sub")
        s_sexp = sem("s_sexp"); s_affn = sem("s_affn"); s_afft = sem("s_afft"); s_affc = sem("s_affc")
        s_pos = sem("s_pos"); s_post2 = sem("s_post2"); s_posn = sem("s_posn"); s_route = sem("s_route")
        s_clear = sem("s_clear"); s_selc = sem("s_selc"); s_gc = sem("s_gc"); s_xc = sem("s_xc")
        s_selg = sem("s_selg"); s_g = sem("s_g"); s_xeh = sem("s_xeh"); s_xel = sem("s_xel")
        s_xeclo = sem("s_xeclo"); s_pb = sem("s_pb"); s_selt = sem("s_selt"); s_gate = sem("s_gate")
        s_silu2 = sem("s_silu2"); s_hm = sem("s_hm"); s_htr = sem("s_htr"); s_h2h = sem("s_h2h")
        s_h2l = sem("s_h2l"); s_yef = sem("s_yef"); s_yeh = sem("s_yeh"); s_yel = sem("s_yel")
        s_yec = sem("s_yec"); s_cmb = sem("s_cmb"); s_add = sem("s_add")
        s_fin = sem("s_fin"); s_fx = sem("s_fx"); s_fss = sem("s_fss"); s_frs = sem("s_frs"); s_fy = sem("s_fy")
        s_out = sem("s_out"); s_kout = sem("s_kout"); s_gm = sem("s_gm"); s_xet = sem("s_xet")
        s_xech = sem("s_xech"); s_xcg = sem("s_xcg"); s_gep = sem("s_gep"); s_ych = sem("s_ych")

        block = ctx.enter_context(nc.Block())

        def columns(w, col, n, k0, kn):
            return w[k0 * P:(k0 + kn) * P, col:col + n].rearrange("(k p) n -> p k n", p=P)

        chunks = []
        for kind, j in STREAM:
            if kind == "mod":
                for q in range(2):
                    chunks.append([(slice(0, P), columns(w_mod[0], NW * j, NW, 4 * q, 4))])
                continue
            name, n, kt = GEMMS[j]
            if name in W_IN_COL:
                per = CH // n
                for q in range(kt // per):
                    chunks.append([(slice(0, P), columns(w_in[0], W_IN_COL[name], n, per * q, per))])
            elif name[:2] == "wa":
                w = w_branch_a[0].rearrange("(v i p) n -> v p i n", v=2, p=HD)
                c0 = NW * int(name[2])
                chunks.append([(slice(64 * v, 64 * v + 64), w[v][:, :, c0:c0 + NW]) for v in range(2)])
            elif name[:2] == "wb":
                chunks.append([(slice(0, P), columns(w_branch_b[0], NW * int(name[2]), NW, 0, 4))])
            else:
                for q in range(2):
                    chunks.append([(slice(0, P), columns(w_out[0], NW * int(name[3]), NW, 4 * q, 4))])
        NCH = len(chunks)
        assert 2 * NCH == DENSE_HALVES
        raw_count = [0] * NCH
        seen = [0] * NRAW
        for n, parts in enumerate(chunks):
            seen[n % NRAW] += 16 * len(parts)
            raw_count[n] = seen[n % NRAW]

        def half_of(tensor, h, n):
            return tensor[:, h % NHL, :].rearrange("p (k n) -> p k n", n=n)

        def split_hi(act, h):
            if h % 2 == 0:
                act.wait_ge(s_raw[(h // 2) % NRAW], raw_count[h // 2] if h < DENSE_HALVES else expert_raw(0, 0))
            if h >= NHL:
                act.wait_ge(s_half, h - NHL + 1)
            n, q = h // 2 % NRAW, h % 2
            act.activation(w_hi[:, h % NHL, :], raw[:, n, q * HALF:(q + 1) * HALF], ACT.Copy).then_inc(s_hi, 1)

        def split_lo(dve, h):
            dve.wait_ge(s_hi, h + 1)
            n, q = h // 2 % NRAW, h % 2
            dve.tensor_tensor(w_lo[:, h % NHL, :], raw[:, n, q * HALF:(q + 1) * HALF],
                              w_hi[:, h % NHL, :].bitcast(F32), ALU.subtract).then_inc(s_lo, 1)

        def prob_part(dst, i):
            _, t, _ = PUS[i]
            if t == NTL:
                return dst[:, BLK_OF[i] % 2, 0, 0:P], bank(4, 0, P)
            o = (t % 2) * P
            return (dst[:, BLK_OF[i] % 2, :, o:o + P].rearrange("p (a b) c -> p a b c", a=2),
                    ps[:, 2048:3072].rearrange("p (a b) -> p a b", a=2)[:, :, 0:384]
                    .rearrange("p a (b c) -> p a b c", c=P))

        def latent_slots(xe, k):
            v = xe[:, k, LCOL[0]:LCOL[0] + CAPL]
            return bass.AP(tensor=v.tensor, offset=v.offset,
                           ap=[v.ap[0], [LCOL[2] - LCOL[0], 2], [LCOL[1] - LCOL[0], 2], [1, CAPL]])

        def four(x):
            return x.rearrange("p (a b s) -> p a b s", a=2, b=2)

        def product_bank(j, t):
            return (NT * j + t) % NB6

        def wait_product(eng, j, t):
            if t < NT - 1:
                eng.wait_ge(s_acc, (NT - 1) * j + t + 1)
            else:
                eng.wait_ge(s_half, FIRST[("gemm", j)] + NHALF[("gemm", j)])

        def freed_before(owner, q):
            return sum(1 for r in range(q + 1) if FREED_BY[GN[r // NT]] == owner)

        def expert_chunk(e, n):
            if n < 8:
                w = (w_exp_gate, w_exp_up)[n // 2 % 2]
                return w[0, e, (n % 2) * NW:(n % 2 + 1) * NW,
                         (n // 4) * NW:(n // 4 + 1) * NW].rearrange("(k p) n -> p k n", p=P)
            k, d = (n - 8) // 2, (n - 8) % 2
            return w_exp_down[0, e, k * NW:(k + 1) * NW, d * NW:(d + 1) * NW].rearrange("(k p) n -> p k n", p=P)

        def groups(eng, body, count=NG):
            with eng.Fori(0, count - 1) as i:
                body(i, False)
            body(count - 1, True)

        EC = 12 * EG

        @block.sync
        def _(sp):
            sp.dma_start(tab[:, :], constants[:, 0:T_KEPT]).then_inc(s_tab, 16)
            xs = x_sample[0].rearrange("(t p) d -> t p d", p=P)
            for t in range(NTL):
                sp.dma_start(x_n[:, t, :], xs[t]).then_inc(s_x[t], 16)
            sp.dma_start(x_n[:, NTL, :], x_prompt[0]).then_inc(s_x[NTL], 16)
            for n, parts in enumerate(chunks):
                if n >= NRAW:
                    sp.wait_ge(s_lo, 2 * (n - NRAW) + 2)
                for rows, src in parts:
                    k = src.shape[1]
                    sp.dma_start(raw[rows, n % NRAW, :].rearrange("p (k n) -> p k n", k=k), src)\
                      .then_inc(s_raw[n % NRAW], 16)

            def body(i, last):
                for e in range(EG):
                    for n in range(12):
                        c = 12 * e + n
                        g = NCH + c
                        sp.wait_ge(s_lo, 2 * (g - NRAW) + 2 + GH * i)
                        sp.dma_start(raw[:, g % NRAW, :].rearrange("p (k n) -> p k n", n=NW),
                                     expert_chunk(i * EG + e, n)).then_inc(s_raw[g % NRAW], 16)
            groups(sp, body)

        def expert_raw(c, i):
            g = NCH + c
            before = seen[g % NRAW] + 16 * sum(1 for m in range(c + 1) if (NCH + m) % NRAW == g % NRAW)
            return before + 16 * (EC // NRAW) * i

        @block.tensor
        def _(pe):
            def product(j, stat_hi, stat_lo):
                h0, nh = FIRST[("gemm", j)], NHALF[("gemm", j)]
                _, n, kt = GEMMS[j]
                per = HALF // n
                for hh in range(nh):
                    h = h0 + hh
                    pe.wait_ge(s_lo, h + 1)
                    hi, lo = half_of(w_hi, h, n), half_of(w_lo, h, n)
                    for t in range(NT):
                        b = bank(product_bank(j, t), 0, n)
                        q = NT * j + t - NB6
                        if hh == 0 and q >= 0:
                            owner = FREED_BY[GN[q // NT]]
                            pe.wait_ge(s_free_d if owner == "dve" else s_free_a, freed_before(owner, q))
                        for kk in range(per):
                            k = per * hh + kk
                            first, last = k == 0, k == kt - 1
                            tt = slice(t * P, (t + 1) * P)
                            pe.matmul(b, stat_hi(k, tt), hi[:, kk, :], start=first, stop=False)
                            pe.matmul(b, stat_hi(k, tt), lo[:, kk, :], start=False, stop=False)
                            mm = pe.matmul(b, stat_lo(k, tt), hi[:, kk, :], start=False, stop=last)
                        if hh == nh - 1 and t < NT - 1:
                            mm.then_inc(s_acc, 1)
                    mm.then_inc(s_half, 1)

            def mod_product(j, b):
                for hh in range(4):
                    h = FIRST[("mod", j)] + hh
                    pe.wait_ge(s_lo, h + 1)
                    for kk in range(2):
                        k = 2 * hh + kk
                        pe.matmul(bank(b, rows=slice(0, 4)), c_hi[:, k, :], half_of(w_hi, h, NW)[:, kk, :],
                                  start=(k == 0), stop=False)
                        mm = pe.matmul(bank(b, rows=slice(0, 4)), c_lo[:, k, :], half_of(w_lo, h, NW)[:, kk, :],
                                       start=False, stop=(k == KD - 1))
                    mm.then_inc(s_half, 1)

            def mod_turn(j, n, rows):
                pe.wait_ge(s_row, n + 1)
                if n:
                    pe.wait_ge(s_mod, n)
                for i in range(4):
                    mm = pe.matmul(bank(6, 2 * i, 2 * i + 2), rows[0:4, n % 2, i * P:(i + 1) * P],
                                   tab2[0:4, T_SEL - T_KEPT:T_SEL - T_KEPT + 2], start=True, stop=True)
                mm.then_inc(s_post, 1)

            def mod_spread(j, n, rows):
                pe.wait_ge(s_row, n + 1)
                pe.wait_ge(s_mod, n)
                for i in range(2):
                    o = T_SB - T_KEPT + i * P
                    mm = pe.matmul(bank(6 + i), tab2[0:4, o:o + P], rows[0:4, n % 2, :], start=True, stop=True)
                mm.then_inc(s_post, 1)

            pe.wait_ge(s_tab, 16)
            pe.wait_ge(s_silu, 1)
            pe.transpose(bank(5, 0, 81), vec[:, :], ident[0:81, 0:81]).then_inc(s_vect, 1)
            pe.wait_ge(s_csplit, 1)
            pe.wait_ge(s_tab2, 16)
            for j in range(4):
                if j >= 2:
                    pe.wait_ge(s_row, j - 1)
                mod_product(j, j % 2)
                if j:
                    mod_turn(j - 1, j - 1, mod_row)
            mod_turn(3, 3, mod_row)
            pe.wait_ge(s_xn, NT)
            pe.wait_ge(s_mod, 4)
            for k in range(KD):
                if k >= 4:
                    pe.wait_ge(s_htl, k - 3)
                for t in range(NTL):
                    pe.transpose(bank(2 * (k % 4), t * P, (t + 1) * P), x_n[:, t, k * P:(k + 1) * P], ident)
                pe.transpose(bank(2 * (k % 4) + 1, 0, P),
                             x_n[:, NTL, k * P:(k + 1) * P], ident).then_inc(s_xt, 1)
            pe.wait_ge(s_htl, KD)

            def hth(k, tt):
                return ht_hi[:, k, tt]

            def htl(k, tt):
                return ht_lo[:, k, tt]

            turned = [0]

            def turn_keys(n, parts):
                pe.wait_ge(s_kparts, n + 1)
                maps = parts.shape[1]
                for g in range(0, maps, 4):
                    if turned[0] >= 2:
                        pe.wait_ge(s_kev, turned[0] - 1)
                    b = 6 + turned[0] % 2
                    for m in range(min(4, maps - g)):
                        mm = pe.transpose(bank(b, m * P, (m + 1) * P),
                                          parts[:, g + m, :, :].rearrange("p a b -> p (a b)").bitcast(F32), ident)
                    mm.then_inc(s_ktr, 1)
                    turned[0] += 1

            product(0, hth, htl)
            turn_keys(0, ka_parts)
            turn_keys(1, kb_parts)
            turn_keys(2, ka_parts)
            turn_keys(3, kb_parts)
            for j in (1, 2, 3):
                product(j, hth, htl)
            for n in range(NT):
                turn_keys(4 + n, ka_parts)
            product(4, hth, htl)
            for n in range(NT):
                turn_keys(4 + NT + n, kb_parts)

            turns = []

            def turn_banks_free():
                if not turns:
                    pe.wait_ge(s_kev, 3 * KT)
                    return
                kind, n, part = turns[-1]
                if kind == "p":
                    pe.wait_ge(s_pl, n + 1)
                elif part == 0:
                    pe.wait_ge(s_qh, n + 1)
                else:
                    pe.wait_ge(s_ql, n + 1)

            def turn_queries(m):
                pe.wait_ge(s_qp, m + 1)
                for part in range(2):
                    turn_banks_free()
                    for t in range(NT):
                        mm = pe.transpose(bank(4, t * P, (t + 1) * P),
                                          q_parts[:, t, 2 * part:2 * part + 2, :]
                                          .rearrange("p a b -> p (a b)").bitcast(F32), ident)
                    mm.then_inc(s_qtr, 1)
                    turns.append(("q", m, part))

            def scores(s):
                m, t = UNITS[s]
                x = m // (HA // KVA) if m < HA else KVA + m - HA
                if s == U_FIRST[m]:
                    pe.wait_ge(s_qh, m + 1)
                    pe.wait_ge(s_ql, m + 1)
                if s >= 2:
                    pe.wait_ge(s_exp, s - 1)
                b = 2 * (s % 2)
                cols = [(b, 0, 384), (b + 1, 384, 384)] if t < NTL else [(b, KTL * P, P)]
                for part, q in enumerate((q_hi_t, q_lo_t)):
                    for bb, c0, n in cols:
                        mm = pe.matmul(bank(bb, 0, n), q[:, m % 2, t * P:(t + 1) * P], keys_t[:, x, c0:c0 + n],
                                       start=(part == 0), stop=(part == 1))
                mm.then_inc(s_sc, 1)

            def turn_probs(i):
                h, t, s = PUS[i]
                if h < HA:
                    pe.wait_ge(s_nrm, i + 1)
                else:
                    pe.wait_ge(s_comb, i - HA * NT + 1)
                turn_banks_free()
                src = probs[:, (s if h < HA else s - 1) % 4, :]
                for kt in range(KTL if t < NTL else 1):
                    o = (kt % 3) * P
                    mm = pe.transpose(bank(4 + kt // 3, o, o + P), src[:, kt * P:(kt + 1) * P], ident)
                mm.then_inc(s_ptr, 1)
                turns.append(("p", i, 0))

            def values(blk):
                h, b = BLOCKS[blk]
                n = 2 * P if b < 2 else P
                pe.wait_ge(s_pl, BLK_END[blk] + 1)
                if blk >= 2:
                    pe.wait_ge(s_oev, blk - 1)
                if h >= HA and b == 0:
                    pe.wait_ge(s_vb, h - HA + 1)
                vh, vl = (va_hi, va_lo) if h < HA else (vb_hi, vb_lo)
                kts = range(KTL) if b < 2 else [KTL]
                for kt in kts:
                    src = kt if b < 2 else 0
                    o = bank(6 + blk % 2, 0, n)
                    pe.matmul(o, vh[:, kt, :], p_hi[:, blk % 2, src, 0:n], start=(kt == kts[0]), stop=False)
                    pe.matmul(o, vh[:, kt, :], p_lo[:, blk % 2, src, 0:n], start=False, stop=False)
                    mm = pe.matmul(o, vl[:, kt, :], p_hi[:, blk % 2, src, 0:n], start=False, stop=(kt == kts[-1]))
                mm.then_inc(s_pv, 1)

            for s in range(NU + LAG + 1):
                for m in range(MAPS):
                    if PREP[m] == s:
                        turn_queries(m)
                if s < NU:
                    scores(s)
                if s >= LAG and s - LAG in PU_OF:
                    turn_probs(PU_OF[s - LAG])
                if s - LAG - 1 in PU_OF and PU_OF[s - LAG - 1] in BLK_END.values():
                    values(BLK_OF[PU_OF[s - LAG - 1]])
            for h in range(HB):
                pe.wait_ge(s_ysq, h + 1)
                if h >= 2:
                    pe.wait_ge(s_yrt, h - 1)
                b = 2 * (h % 2)
                mean = tab2[:, T_MEAN - T_KEPT:T_MEAN - T_KEPT + P]
                pe.matmul(bank(b), mean, y_sq[:, h % 2, 0:512], start=True, stop=True)
                pe.matmul(bank(b + 1, 0, TOK - 512), mean, y_sq[:, h % 2, 512:TOK], start=True, stop=True)\
                  .then_inc(s_yms, 1)

            def turn_merged(nh):
                for t in range(NT):
                    n = nh * NT + t
                    pe.wait_ge(s_mrg, n + 1)
                    if n >= 2:
                        pe.wait_ge(s_mtl, n - 1)
                    for i in range(4):
                        mm = pe.transpose(bank(6 + n % 2, i * P, (i + 1) * P), merged[:, t, i * P:(i + 1) * P], ident)
                    mm.then_inc(s_mtr, 1)

            pe.wait_ge(s_refill, 32)
            for j in range(5, 13):
                name = GN[j]
                if name[0] == "g":
                    product(j, hth, htl)
                else:
                    if j == 6:
                        pe.wait_ge(s_yl, 8)
                    o = 0 if name[1] == "a" else 4
                    product(j, lambda k, tt: yt_hi[:, o + k, tt], lambda k, tt: yt_lo[:, o + k, tt])
                if j == 9:
                    turn_merged(0)
            for n in range(8):
                if n == 0:
                    pe.wait_ge(s_free_d, freed_before("dve", NT * 13 - 1))
                    pe.wait_ge(s_free_a, freed_before("act", NT * 13 - 1))
                if n >= 2:
                    pe.wait_ge(s_row, 4 + n - 1)
                mod_product(4 + n, n % 2)
                if n == 0:
                    turn_merged(1)
                    pe.wait_ge(s_mtl, 2 * NT)
                if n:
                    (mod_spread if n - 1 in (0, 1, 6, 7) else mod_turn)(4 + n - 1, 4 + n - 1, mod_row2)
            mod_spread(11, 11, mod_row2)
            for j in (13, 14):
                product(j, lambda k, tt: mt_hi[:, k, tt], lambda k, tt: mt_lo[:, k, tt])
            pe.wait_ge(s_free_d, freed_before("dve", NT * 15 - 1))
            for k in range(KD):
                if k == 0:
                    pe.wait_ge(s_xf, NT)
                if k >= 3:
                    pe.wait_ge(s_h2, k - 2)
                for t in range(NTL):
                    pe.transpose(bank(2 * (k % 3), t * P, (t + 1) * P), xn_f[:, t, k * P:(k + 1) * P], ident)
                pe.transpose(bank(2 * (k % 3) + 1, 0, P),
                             xn_f[:, NTL, k * P:(k + 1) * P], ident).then_inc(s_x2t, 1)
            pe.wait_ge(s_router, 16)
            e16 = slice(0, NE)
            for k in range(KD):
                pe.wait_ge(s_h2, k + 1)
                pe.matmul(bank(6, rows=e16), router[:, k, :], h2_t[:, k, 0:LAT], start=(k == 0), stop=(k == KD - 1))
                mm = pe.matmul(bank(7, 0, CTX, rows=e16), router[:, k, :], h2_t[:, k, LAT:TOK],
                               start=(k == 0), stop=(k == KD - 1))
            mm.then_inc(s_lgt, 1)
            pe.wait_ge(s_lgc, 1)
            for t in range(NT):
                mm = pe.transpose(bank(0, t * NE, (t + 1) * NE), lg_t[:, t * P:(t + 1) * P], ident[0:NE, 0:NE])
            mm.then_inc(s_lgn, 1)
            pe.wait_ge(s_affn, 1)
            for t in range(NT):
                mm = pe.transpose(ps[0:NE, 512 + t * P:512 + (t + 1) * P], aff_n[:, t, :], ident)
            mm.then_inc(s_afft, 1)
            pe.wait_ge(s_pos, 1)
            for t in range(NT):
                mm = pe.transpose(bank(3, t * NE, (t + 1) * NE), pos_t[:, t * P:(t + 1) * P], ident[0:NE, 0:NE])
            mm.then_inc(s_post2, 1)
            pe.wait_ge(s_selc, 1)
            pe.wait_ge(s_xl, NT)
            flat_c = sel_c[:, :, :].rearrange("p e s -> p (e s)")
            for k in range(KD):
                if k >= 2:
                    pe.wait_ge(s_xc, k - 1)
                b = bank(4 + k % 2, 0, NE * CAPC)
                pe.matmul(b, xn_hi[:, NTL, k * P:(k + 1) * P], flat_c, start=True, stop=False)
                pe.matmul(b, xn_lo[:, NTL, k * P:(k + 1) * P], flat_c, start=False, stop=True).then_inc(s_gc, 1)

            def gather(n):
                pe.wait_ge(s_selg, n * NTL + NTL)
                for k in range(KD):
                    if k >= 2:
                        pe.wait_ge(s_xel, n * KD + k - 1)
                    b = bank(6 + k % 2, 0, EG * CAPL)
                    for t in range(NTL):
                        pe.matmul(b, xn_hi[:, t, k * P:(k + 1) * P], sel_g[:, t, :], start=(t == 0), stop=False)
                        mm = pe.matmul(b, xn_lo[:, t, k * P:(k + 1) * P], sel_g[:, t, :],
                                       start=False, stop=(t == NTL - 1))
                    mm.then_inc(s_g, 1)

            gather(0)

            def body(i, last):
                H0 = DENSE_HALVES

                def hidden(e, b, hh0, n0):
                    for q in range(4):
                        h = H0 + 24 * e + hh0 + q
                        pe.wait_ge(s_lo, i * GH + h + 1)
                        hi, lo = half_of(w_hi, h, NW), half_of(w_lo, h, NW)
                        for kk in range(2):
                            k = 2 * q + kk
                            w = slice(WIN[e], WIN[e] + P)
                            pe.matmul(bank(b), xe_hi[:, k, w], hi[:, kk, :], start=(k == 0), stop=False)
                            pe.matmul(bank(b), xe_hi[:, k, w], lo[:, kk, :], start=False, stop=False)
                            mm = pe.matmul(bank(b), xe_lo[:, k, w], hi[:, kk, :], start=False, stop=(k == KD - 1))
                        mm.then_inc(s_half, 1)

                def turn_hidden(e, f):
                    pe.wait_ge(s_hm, i * 8 + 2 * e + f + 1)
                    if not (e == 0):
                        pe.wait_ge(s_h2l, i * 8 + 2 * e + f - 1)
                    for k in range(4):
                        mm = pe.transpose(bank(6 + f, k * P, (k + 1) * P), h_act[:, f, k * P:(k + 1) * P], ident)
                    mm.then_inc(s_htr, 1)

                def down(e, hh):
                    h = H0 + 24 * e + 16 + hh
                    d, k0 = (hh // 2) % 2, 4 * (hh // 4) + 2 * (hh % 2)
                    if hh % 4 == 0:
                        pe.wait_ge(s_h2l, i * 8 + 2 * e + hh // 4 + 1)
                    pe.wait_ge(s_lo, i * GH + h + 1)
                    hi, lo = half_of(w_hi, h, NW), half_of(w_lo, h, NW)
                    for kk in range(2):
                        k = k0 + kk
                        b = bank(4 + d)
                        pe.matmul(b, ht2_hi[:, k, :], hi[:, kk, :], start=(k == 0), stop=False)
                        pe.matmul(b, ht2_hi[:, k, :], lo[:, kk, :], start=False, stop=False)
                        mm = pe.matmul(b, ht2_lo[:, k, :], hi[:, kk, :], start=False, stop=(k == KD - 1))
                    mm.then_inc(s_half, 1)

                pe.wait_ge(s_xel, i * KD + KD)
                pe.wait_ge(s_xeclo, 2 * i + 2)
                for e in range(EG):
                    hidden(e, 0, 0, 0)
                    hidden(e, 2, 4, 0)
                    hidden(e, 1, 8, 0)
                    if e == 0:
                        pe.wait_ge(s_add, i * 2 * NT + 1)
                    turn_hidden(e, 0)
                    hidden(e, 3, 12, 0)
                    if e:
                        pe.wait_ge(s_yel, i * EG + e)
                    down(e, 0)
                    down(e, 1)
                    turn_hidden(e, 1)
                    for hh in range(2, 8):
                        down(e, hh)
                if not last:
                    pe.wait_ge(s_h2l, i * 8 + 8)
                    gather(i + 1)
                pe.wait_ge(s_yel, i * EG + EG)
                pe.wait_ge(s_yec, i * EG + EG + 1)
                pe.wait_ge(s_gate, i * 3 + 4)
                n = 0
                for t in range(NT):
                    for d in range(2):
                        if n >= 2:
                            pe.wait_ge(s_add, i * 2 * NT + n)
                        elif n == 0 and not last:
                            pe.wait_ge(s_xel, (i + 1) * KD + KD)
                        b = bank(6 + n % 2)
                        ds = slice(d * NW, (d + 1) * NW)
                        if t < NTL:
                            for pr in range(2):
                                st = sel_t[:, pr, t * P:(t + 1) * P]
                                pe.matmul(b, st, ye_hi[:, pr, ds], start=(pr == 0), stop=False)
                                mm = pe.matmul(b, st, ye_lo[:, pr, ds], start=False, stop=(pr == 1))
                        else:
                            pe.matmul(b, sel_tc[:, :], yc_hi[:, ds], start=True, stop=False)
                            mm = pe.matmul(b, sel_tc[:, :], yc_lo[:, ds], start=False, stop=True)
                        mm.then_inc(s_cmb, 1)
                        n += 1

            groups(pe, body)

        @block.scalar
        def _(act):
            act.wait_ge(s_vec, 16 * 6)
            act.activation(vec[0:16, :], vec[0:16, :], ACT.Silu).then_inc(s_silu, 1)
            for t in range(NT):
                act.wait_ge(s_x[t], 16)
                if t:
                    act.wait_ge(s_ss, t)
                act.activation(squares[:, :], x_n[:, t, :], ACT.Square, accum_out=ss[:, t:t + 1]).then_inc(s_ss, 1)
            act.wait_ge(s_lamw, 1)
            act.activation(lam[:, 0:2 * HB], lam[:, 0:2 * HB], ACT.Exp).then_inc(s_lame, 1)
            split_hi(act, 0)
            split_hi(act, 1)
            end_b = HALVES_B
            for j in range(4):
                for hh in range(4):
                    split_hi(act, FIRST[("mod", j)] + hh + 2)

            act.wait_ge(s_scale, 1)
            for k in range(KD):
                act.wait_ge(s_xt, k + 1)
                act.activation(ht_hi[:, k, 0:LAT], bank(2 * (k % 4)), ACT.Identity, scale=scale1[:, k, 0:1],
                               bias=mod_t[:, k, 0:1])
                act.activation(ht_hi[:, k, LAT:TOK], bank(2 * (k % 4) + 1, 0, P), ACT.Identity,
                               scale=scale1[:, k, 1:2], bias=mod_t[:, k, 1:2]).then_inc(s_hth, 1)
            act.wait_ge(s_htl, KD)
            act.dma_start(ht_dram[:, 0, :].bitcast(F32), ht_hi[:, :, :].rearrange("p k t -> p (k t)").bitcast(F32))\
               .then_inc(s_spill, 16)
            act.dma_start(ht_dram[:, 1, :].bitcast(F32), ht_lo[:, :, :].rearrange("p k t -> p (k t)").bitcast(F32))\
               .then_inc(s_spill, 16)

            turned = [0]

            def key_copies(maps, kt):
                for g in range(0, maps, 4):
                    n = min(4, maps - g)
                    x0 = 0 if maps == KVA else KVA + g
                    act.wait_ge(s_ktr, turned[0] + 1)
                    b = 6 + turned[0] % 2
                    act.activation(keys_t[:, x0:x0 + n, kt * P:(kt + 1) * P],
                                   bank(b, 0, n * P).rearrange("p (m c) -> p m c", c=P), ACT.Copy).then_inc(s_kev, 1)
                    turned[0] += 1

            def lead(j, stop):
                for hh in range(NHALF[("gemm", j)]):
                    h = FIRST[("gemm", j)] + hh + 2
                    if h < stop:
                        split_hi(act, h)

            n_sq = [0]

            def square_of(j, t, cols):
                wait_product(act, j, t)
                if n_sq[0] >= 2:
                    act.wait_ge(s_qss, n_sq[0] - 1)
                act.activation(q_sq[:, n_sq[0] % 2, 0:cols], bank(product_bank(j, t), 0, cols), ACT.Square)\
                   .then_inc(s_qsq, 1)
                n_sq[0] += 1

            lead(0, end_b)
            for t in range(NT):
                square_of(0, t, NW)
            key_copies(KVA, 0)
            key_copies(2 * HB, 0)
            key_copies(KVA, 1)
            key_copies(2 * HB, 1)
            lead(1, end_b)
            for t in range(NT):
                wait_product(act, 1, t)
                act.activation(q_n[:, t, HA:MAPS, :], bank(product_bank(1, t)).rearrange("p (m c) -> p m c", c=HD),
                               ACT.Copy).then_inc(s_free_a, 1)
            lead(2, end_b)
            for t in range(NT):
                square_of(2, t, P)
                act.activation(va_hi[:, 2 + t, :], bank(product_bank(2, t), P, 2 * P), ACT.Copy).then_inc(s_vah, 1)
            lead(3, end_b)
            for t in range(NT):
                wait_product(act, 3, t)
                act.activation(k_n[:, t, KVA:, :], bank(product_bank(3, t)).rearrange("p (m c) -> p m c", c=HD),
                               ACT.Copy).then_inc(s_free_a, 1)
            for t in range(NT):
                key_copies(KVA, 2 + t)
            lead(4, end_b)
            for t in range(NT):
                wait_product(act, 4, t)
                act.activation(vb_n[:, 2 + t, :], bank(product_bank(4, t)), ACT.Copy).then_inc(s_free_a, 1)
            for t in range(NT):
                key_copies(2 * HB, 2 + t)

            act.wait_ge(s_half, HALVES_B)
            act.wait_ge(s_spill, 32)
            for s in range(NU + LAG + 1):
                for m in range(MAPS):
                    if PREP[m] == s:
                        act.wait_ge(s_qtr, 2 * m + 1)
                        if m >= 2:
                            act.wait_ge(s_sc, U_LAST[m - 2] + 1)
                        act.activation(q_hi_t[:, m % 2, :], ps[:, 4 * 512:4 * 512 + TOK], ACT.Copy).then_inc(s_qh, 1)
                if s < NU:
                    _, t = UNITS[s]
                    act.wait_ge(s_max, s + 1)
                    if s >= 4:
                        if UNITS[s - 4][0] < HA:
                            act.wait_ge(s_ptr, PU_OF[s - 4] + 1)
                        elif s - 4 in PU_OF:
                            act.wait_ge(s_comb, PU_OF[s - 4] - HA * NT + 1)
                        else:
                            act.wait_ge(s_ptr, PU_OF[s - 3] + 1)
                    n = KTL * P if t < NTL else P
                    dst, src = probs[:, s % 4, 0:n], bank(2 * (s % 2), 0, n)
                    if t < NTL:
                        dst = dst.rearrange("p (a b) -> p a b", a=2)
                        src = ps[:, 1024 * (s % 2):1024 * (s % 2) + 1024].rearrange("p (a b) -> p a b", a=2)[:, :, 0:384]
                    act.activation(dst, src, ACT.Exp, bias=neg_max[:, s % 8:s % 8 + 1], scale=SCALE,
                                   accum_out=row_sum[:, s % 8:s % 8 + 1]).then_inc(s_exp, 1)
                if s >= LAG and s - LAG in PU_OF:
                    i = PU_OF[s - LAG]
                    act.wait_ge(s_ptr, i + 1)
                    dst, src = prob_part(p_hi, i)
                    if BLK_OF[i] >= 2:
                        act.wait_ge(s_pv, BLK_OF[i] - 1)
                    act.activation(dst, src, ACT.Copy).then_inc(s_ph, 1)
                if s - LAG - 1 in PU_OF and PU_OF[s - LAG - 1] in BLK_END.values():
                    blk = BLK_OF[PU_OF[s - LAG - 1]]
                    h, b = BLOCKS[blk]
                    n = 2 * P if b < 2 else P
                    act.wait_ge(s_pv, blk + 1)
                    rows = slice(0, P) if h >= HA else slice(64 * (h // 4), 64 * (h // 4) + 64)
                    y = 4 + h - HA if h >= HA else h % 4
                    act.activation(y_t[rows, y, 2 * P * b:2 * P * b + n], bank(6 + blk % 2, 0, n, rows), ACT.Copy)\
                       .then_inc(s_oev, 1)
            act.wait_ge(s_oev, len(BLOCKS))
            for h in range(HB + 1):
                if h < HB:
                    if h >= 2:
                        act.wait_ge(s_yms, h - 1)
                    act.activation(y_sq[:, h % 2, :], y_t[:, 4 + h, :], ACT.Square).then_inc(s_ysq, 1)
                if h:
                    act.wait_ge(s_yms, h)
                    if h >= 3:
                        act.wait_ge(s_yn, h - 2)
                    b = 1024 * ((h - 1) % 2)
                    act.activation(y_rms[:, (h - 1) % 2, :], ps[:, b:b + TOK], ACT.Sqrt, bias=eps).then_inc(s_yrt, 1)
            for i in range(8):
                if i >= 4:
                    act.wait_ge(s_yn, i - 3)
                act.activation(yt_hi[:, i, :], y_t[:, i, :], ACT.Copy).then_inc(s_yh, 1)
            act.wait_ge(s_pv, len(BLOCKS))
            for h in (HALVES_B, HALVES_B + 1):
                split_hi(act, h)
            act.wait_ge(s_yl, 8)
            def merged_hi(n):
                nh, t = n // NT, n % NT
                act.wait_ge(s_mtr, n + 1)
                act.activation(mt_hi[:, 4 * nh:4 * nh + 4, t * P:(t + 1) * P],
                               bank(6 + n % 2).rearrange("p (k c) -> p k c", c=P), ACT.Copy).then_inc(s_mth, 1)

            for j in range(5, 13):
                lead(j, DENSE_HALVES)
                if GN[j][0] == "g":
                    for t in range(NT):
                        wait_product(act, j, t)
                        if j > 5:
                            n = j // 2 - 3 + 1
                            act.wait_ge(s_mrg if GN[j][:2] == "ga" else s_free_d,
                                        t + 1 if GN[j][:2] == "ga" else freed_before("dve", NT * (j - 1) + t))
                        act.activation(sig[:, t, :], bank(product_bank(j, t)), ACT.Sigmoid).then_inc(s_free_a, 1)
                if j == 9:
                    for t in range(NT):
                        merged_hi(t)
            for n in range(8):
                for hh in range(4):
                    split_hi(act, FIRST[("mod", 4 + n)] + hh + 2)
                if n == 0:
                    for t in range(NT):
                        merged_hi(NT + t)
            for j in (13, 14):
                for hh in range(4):
                    split_hi(act, FIRST[("gemm", j)] + hh + 2)
            act.wait_ge(s_mod, 12)
            act.dma_start(g2_dram[:, :, :], gate2[:, :, :]).then_inc(s_g2out, 16)
            for t in range(NT):
                act.wait_ge(s_x1, t + 1)
                if t:
                    act.wait_ge(s_ss2, t)
                act.activation(squares2[:, :], x_r[:, t, :], ACT.Square, accum_out=ss[:, t:t + 1]).then_inc(s_ss2, 1)
            act.dma_start(x1_dram[:, :, :], x_r[:, :, :]).then_inc(s_x1out, 16)
            act.wait_ge(s_g2out, 16)
            for t in range(NT):
                act.wait_ge(s_xf, t + 1)
                act.activation(xn_hi[:, t, :], xn_f[:, t, :], ACT.Copy).then_inc(s_xh, 1)
            for k in range(KD):
                act.wait_ge(s_x2t, k + 1)
                act.activation(h2_t[:, k, 0:LAT], bank(2 * (k % 3)), ACT.Identity, scale=scale2[:, k, 0:1],
                               bias=mod_t[:, 24 + k, 0:1])
                act.activation(h2_t[:, k, LAT:TOK], bank(2 * (k % 3) + 1, 0, P), ACT.Identity,
                               scale=scale2[:, k, 1:2], bias=mod_t[:, 24 + k, 1:2]).then_inc(s_h2, 1)
            act.wait_ge(s_sub, 1)
            act.activation(soft[:, :, :], soft[:, :, :], ACT.Exp).then_inc(s_sexp, 1)
            act.wait_ge(s_route, 32)
            for k in range(KD):
                act.wait_ge(s_gc, k + 1)
                act.activation(xc_f[:, k, :], bank(4 + k % 2, 0, NE * CAPC), ACT.Identity,
                               scale=scale2[:, k, 1:2], bias=mod_t[:, 24 + k, 1:2]).then_inc(s_xc, 1)

            def gathered(n):
                for k in range(KD):
                    act.wait_ge(s_g, n * KD + k + 1)
                    act.activation(latent_slots(xe_hi, k), four(bank(6 + k % 2, 0, EG * CAPL)), ACT.Identity,
                                   scale=scale2[:, k, 0:1], bias=mod_t[:, 24 + k, 0:1]).then_inc(s_xeh, 1)

            act.wait_ge(s_clear, 1)
            gathered(0)

            def body(i, last):
                H0 = DENSE_HALVES

                def expert_split(h):
                    if last and h >= GH:
                        return
                    g = H0 + h
                    if h % 2 == 0:
                        act.wait_ge(s_raw[g // 2 % NRAW], expert_raw(h // 2, i))
                    act.wait_ge(s_half, i * GH + g - NHL + 1)
                    act.activation(w_hi[:, g % NHL, :], raw[:, g // 2 % NRAW, (g % 2) * HALF:(g % 2 + 1) * HALF],
                                   ACT.Copy).then_inc(s_hi, 1)

                def silu(e, f):
                    act.wait_ge(s_half, i * GH + H0 + 24 * e + 8 * f + 4)
                    if e:
                        act.wait_ge(s_htr, i * 8 + 2 * e + f - 1)
                    act.activation(h_act[:, f, :], bank(f), ACT.Silu).then_inc(s_silu2, 1)

                def hidden_hi(e, f):
                    act.wait_ge(s_htr, i * 8 + 2 * e + f + 1)
                    if e:
                        act.wait_ge(s_half, i * GH + H0 + 24 * e)
                    act.activation(ht2_hi[:, 4 * f:4 * f + 4, :], bank(6 + f).rearrange("p (k c) -> p k c", c=P),
                                   ACT.Copy).then_inc(s_h2h, 1)

                def output_hi(e):
                    act.wait_ge(s_yef, i * EG + e + 1)
                    rows = slice(64 * (e % 2), 64 * (e % 2) + 64)
                    act.activation(ye_hi[rows, e // 2, :], ye_f[rows, :], ACT.Copy).then_inc(s_yeh, 1)

                for e in range(EG):
                    for hh in range(24):
                        expert_split(24 * e + hh + 2)
                        if hh == 3:
                            silu(e, 0)
                        if hh == 1 and e:
                            output_hi(e - 1)
                        if hh == 11:
                            silu(e, 1)
                            hidden_hi(e, 0)
                        if hh == 17:
                            hidden_hi(e, 1)
                output_hi(EG - 1)
                if not last:
                    gathered(i + 1)

            act.wait_ge(s_selc, 1)
            groups(act, body)
            for t in range(NT):
                act.wait_ge(s_fx, t + 1)
                if t:
                    act.wait_ge(s_fss, t)
                act.activation(squares2[:, :], x_f[:, t, :], ACT.Square, accum_out=ss[:, t:t + 1]).then_inc(s_fss, 1)

        @block.vector
        def _(dve):
            n_own = [0]

            def own(n=1):
                n_own[0] += n
                return n_own[0]

            dve.wait_ge(s_vect, 1)
            dve.tensor_copy(vec_t[:, :], bank(5, 0, 81)).then_inc(s_dve, 1)
            dve.wait_ge(s_dve, own())
            cv = vec_t[:, 0:2 * KD].rearrange("p (v k) -> p k v", v=2)
            dve.memset(c_lo[:, :, :].bitcast(F32), 0.0).then_inc(s_dve, 1)
            dve.tensor_copy(c_hi[:, :, 0:2], cv).then_inc(s_dve, 1)
            dve.tensor_scalar(g_dif[:, :], vec_t[:, 80:81], 1.0 - LAM_INIT, None, ALU.mult).then_inc(s_dve, 1)
            dve.wait_ge(s_dve, own(3))
            dve.tensor_copy(c_lo[:, :, 0:2], cv).then_inc(s_dve, 1)
            dve.wait_ge(s_dve, own())
            dve.tensor_tensor(c_hi[:, :, 2:4], cv, c_hi[:, :, 0:2].bitcast(F32), ALU.subtract).then_inc(s_csplit, 1)
            dve.wait_ge(s_bc, 16 * 6)
            pairs = lam_w[:, :, :, :].rearrange("p (a b) h d -> p a b h d", b=2)
            dve.tensor_tensor(pairs[:, :, 0], pairs[:, :, 0], pairs[:, :, 1], ALU.mult).then_inc(s_dve, 1)
            dve.wait_ge(s_dve, own())
            dve.tensor_reduce(lam[:, 0:2 * HB].rearrange("p (a h) -> p a h", a=2), pairs[:, :, 0], AX.X, ALU.add)\
               .then_inc(s_lamw, 1)
            split_lo(dve, 0)
            split_lo(dve, 1)
            dve.wait_ge(s_lame, 1)
            dve.tensor_tensor(lam[:, 2 * HB:], lam[:, 0:HB], lam[:, HB:2 * HB], ALU.subtract).then_inc(s_dve, 1)
            dve.wait_ge(s_dve, own())
            dve.tensor_scalar(lam[:, 2 * HB:], lam[:, 2 * HB:], LAM_INIT, None, ALU.add).then_inc(s_dve, 1)
            dve.wait_ge(s_dve, own())
            dve.wait_ge(s_rs, 1)
            for t in range(NT):
                dve.tensor_scalar(x_n[:, t, :], x_n[:, t, :], rs[:, t:t + 1], None, ALU.mult).then_inc(s_xn, 1)

            def copy_row(j, b, rows):
                dve.wait_ge(s_half, FIRST[("mod", j)] + 4)
                if j >= 2:
                    dve.wait_ge(s_post, j - 1)
                dve.tensor_copy(rows[0:4, j % 2, :], bank(b, rows=slice(0, 4))).then_inc(s_row, 1)

            def add_bias(j):
                dve.wait_ge(s_post, j + 1)
                dve.tensor_tensor(mod_t[:, 4 * j:4 * j + 4, :], bank(6, 0, 8).rearrange("p (i v) -> p i v", v=2),
                                  vec_t[:, 32 + 4 * j:36 + 4 * j].unsqueeze(2).broadcast_to([P, 4, 2]), ALU.add)\
                   .then_inc(s_mod, 1)

            def scale_of(scale, k0, g):
                dve.scalar_tensor_tensor(scale[:, :, :], mod_t[:, k0:k0 + KD, :], 1.0,
                                         vec_t[:, g:g + KD].unsqueeze(2).broadcast_to([P, KD, 2]), ALU.add, ALU.mult)\
                   .then_inc(s_scale, 1)

            for j in range(4):
                for hh in range(4):
                    split_lo(dve, FIRST[("mod", j)] + hh + 2)
                copy_row(j, j % 2, mod_row)
                if j:
                    add_bias(j - 1)
            add_bias(3)
            dve.wait_ge(s_mod, 4)
            scale_of(scale1, 8, 16)
            dve.wait_ge(s_scale, 1)
            for k in range(KD):
                dve.wait_ge(s_xt, k + 1)
                if k:
                    dve.wait_ge(s_htl, k)
                dve.wait_ge(s_hth, k + 1)
                dve.tensor_scalar(h_tmp[:, 0:LAT], bank(2 * (k % 4)), scale1[:, k, 0:1], mod_t[:, k, 0:1],
                                  ALU.mult, ALU.add).then_inc(s_dve, 1)
                dve.tensor_scalar(h_tmp[:, LAT:TOK], bank(2 * (k % 4) + 1, 0, P),
                                  scale1[:, k, 1:2], mod_t[:, k, 1:2], ALU.mult, ALU.add).then_inc(s_dve, 1)
                dve.wait_ge(s_dve, own(2))
                dve.tensor_tensor(ht_lo[:, k, :], h_tmp[:, :], ht_hi[:, k, :].bitcast(F32), ALU.subtract)\
                   .then_inc(s_htl, 1)

            def lead(j, stop):
                for hh in range(NHALF[("gemm", j)]):
                    h = FIRST[("gemm", j)] + hh + 2
                    if h < stop:
                        split_lo(dve, h)

            n_sq = [0]

            def sums_of(t, heads):
                dve.wait_ge(s_qsq, n_sq[0] + 1)
                dve.tensor_reduce(q_ss[:, t, 0:heads],
                                  q_sq[:, n_sq[0] % 2, 0:heads * HD].rearrange("p (m c) -> p m c", c=HD),
                                  AX.X, ALU.add).then_inc(s_qss, 1)
                n_sq[0] += 1

            def over_rms(dst, j, t, heads):
                src = bank(product_bank(j, t), 0, heads * HD).rearrange("p (m c) -> p m c", c=HD)
                return dve.tensor_tensor(dst, src, q_rs[:, t, 0:heads].unsqueeze(2).broadcast_to([P, heads, HD]),
                                         ALU.mult)

            lead(0, HALVES_B)
            for t in range(NT):
                sums_of(t, HA)
            for t in range(NT):
                dve.wait_ge(s_qrs, t + 1)
                over_rms(q_n[:, t, 0:HA, :], 0, t, HA).then_inc(s_free_d, 1)
            lead(1, HALVES_B)
            lead(2, HALVES_B)
            for t in range(NT):
                sums_of(t, KVA)
            for t in range(NT):
                wait_product(dve, 2, t)
                dve.wait_ge(s_vah, t + 1)
                dve.wait_ge(s_qrs, NT + t + 1)
                over_rms(k_n[:, t, 0:KVA, :], 2, t, KVA).then_inc(s_dve, 1)
                own()
                v = bank(product_bank(2, t), P, 2 * P)
                if t == NTL:
                    dve.tensor_copy(va_ctx[:, :], v).then_inc(s_dve, 1)
                    own()
                dve.wait_ge(s_dve, own(0))
                dve.tensor_tensor(va_lo[:, 2 + t, :], v, va_hi[:, 2 + t, :].bitcast(F32), ALU.subtract)\
                   .then_inc(s_free_d, 1)
            lead(3, HALVES_B)
            lead(4, HALVES_B)

            for s in range(NU + LAG + 1):
                for m in range(MAPS):
                    if PREP[m] == s:
                        dve.wait_ge(s_qtr, 2 * m + 2)
                        if m >= 2:
                            dve.wait_ge(s_sc, U_LAST[m - 2] + 1)
                        dve.tensor_copy(q_lo_t[:, m % 2, :], ps[:, 4 * 512:4 * 512 + TOK]).then_inc(s_ql, 1)
                if s < NU:
                    _, t = UNITS[s]
                    dve.wait_ge(s_sc, s + 1)
                    nm = neg_max[:, s % 8:s % 8 + 1]
                    if t < NTL:
                        src = ps[:, 1024 * (s % 2):1024 * (s % 2) + 1024].rearrange("p (a b) -> p a b", a=2)
                        dve.tensor_reduce(nm, src[:, :, 0:384], AX.XY, ALU.max).then_inc(s_dve, 1)
                    else:
                        dve.tensor_reduce(nm, bank(2 * (s % 2), 0, P), AX.X, ALU.max).then_inc(s_dve, 1)
                    dve.wait_ge(s_dve, own())
                    dve.tensor_scalar(nm, nm, -SCALE, None, ALU.mult).then_inc(s_max, 1)
                if 1 <= s <= NU:
                    m, n = UNITS[s - 1][0], (s - 1) % 8
                    dve.wait_ge(s_exp, s)
                    if m >= HA and (m - HA) % 2 == 1:
                        h = (m - HA) // 2
                        dve.reciprocal(row_inv[:, n:n + 1], row_sum[:, n:n + 1]).then_inc(s_dve, 1)
                        dve.wait_ge(s_dve, own())
                        dve.tensor_tensor(row_inv[:, n:n + 1], row_inv[:, n:n + 1],
                                          lam[:, 2 * HB + h:2 * HB + h + 1], ALU.mult).then_inc(s_rinv, 1)
                    else:
                        dve.reciprocal(row_inv[:, n:n + 1], row_sum[:, n:n + 1]).then_inc(s_rinv, 1)
                if s >= LAG and s - LAG in PU_OF:
                    i = PU_OF[s - LAG]
                    h, t, _ = PUS[i]
                    if h >= HA:
                        dve.wait_ge(s_c1, i - HA * NT + 1)
                        dve.wait_ge(s_rinv, s - LAG)
                        n = KTL * P if t < NTL else P
                        u = s - LAG - 1
                        dve.scalar_tensor_tensor(probs[:, u % 4, 0:n], probs[:, u % 4, 0:n],
                                                 row_inv[:, u % 8:u % 8 + 1], probs[:, (u + 1) % 4, 0:n],
                                                 ALU.mult, ALU.subtract).then_inc(s_comb, 1)
                    dve.wait_ge(s_ph, i + 1)
                    dst, src = prob_part(p_lo, i)
                    hi, _ = prob_part(p_hi, i)
                    dve.tensor_tensor(dst, src, hi.bitcast(F32), ALU.subtract).then_inc(s_pl, 1)
            for h in range(HB):
                dve.wait_ge(s_yrt, h + 1)
                dve.reciprocal(y_rms[:, h % 2, :], y_rms[:, h % 2, :]).then_inc(s_dve, 1)
                dve.wait_ge(s_dve, own())
                dve.scalar_tensor_tensor(y_t[:, 4 + h, :], y_t[:, 4 + h, :], g_dif[:, 0:1], y_rms[:, h % 2, :],
                                         ALU.mult, ALU.mult).then_inc(s_yn, 1)
            dve.wait_ge(s_yn, HB)
            for i in range(8):
                dve.wait_ge(s_yh, i + 1)
                dve.tensor_tensor(yt_lo[:, i, :], y_t[:, i, :], yt_hi[:, i, :].bitcast(F32), ALU.subtract)\
                   .then_inc(s_yl, 1)
            for h in (HALVES_B, HALVES_B + 1):
                split_lo(dve, h)

            def merged_lo(n):
                nh, t = n // NT, n % NT
                dve.wait_ge(s_mth, n + 1)
                o = (slice(None), slice(4 * nh, 4 * nh + 4), slice(t * P, (t + 1) * P))
                dve.tensor_tensor(mt_lo[o], bank(6 + n % 2).rearrange("p (k c) -> p k c", c=P),
                                  mt_hi[o].bitcast(F32), ALU.subtract).then_inc(s_mtl, 1)

            for j in range(5, 13):
                lead(j, DENSE_HALVES)
                name = GN[j]
                for t in range(NT):
                    if name[0] == "w":
                        wait_product(dve, j, t)
                        b = bank(product_bank(j, t))
                        if j == 10:
                            dve.wait_ge(s_mtr, t + 1)
                        if name[1] == "a":
                            dve.tensor_tensor(merged[:, t, :], b, sig[:, t, :], ALU.mult).then_inc(s_free_d, 1)
                        else:
                            dve.tensor_tensor(sig[:, t, :], b, sig[:, t, :], ALU.mult).then_inc(s_free_d, 1)
                            dve.wait_ge(s_free_d, freed_before("dve", NT * j + t))
                            dve.tensor_tensor(merged[:, t, :], merged[:, t, :], sig[:, t, :], ALU.add)\
                               .then_inc(s_mrg, 1)
                if j == 9:
                    for t in range(NT):
                        merged_lo(t)
            for n in range(8):
                for hh in range(4):
                    split_lo(dve, FIRST[("mod", 4 + n)] + hh + 2)
                if n == 0:
                    for t in range(NT):
                        merged_lo(NT + t)
                copy_row(4 + n, n % 2, mod_row2)
                for i in ([n - 1] if n else []) + ([7] if n == 7 else []):
                    if i in (0, 1, 6, 7):
                        gate, g = (gate1, s_gb1) if i < 4 else (gate2, s_gb2)
                        dve.wait_ge(s_post, 4 + i + 1)
                        dve.wait_ge(g, 32)
                        cols = slice((i % 2) * NW, (i % 2 + 1) * NW)
                        dve.tensor_tensor(gate[:, :, cols], gate[:, :, cols],
                                          ps[:, 6 * 512:8 * 512].rearrange("p (v c) -> p v c", v=2), ALU.add)\
                           .then_inc(s_mod, 1)
                    else:
                        add_bias(4 + i)
                    if i == 5:
                        dve.wait_ge(s_mod, 10)
                        scale_of(scale2, 32, 24)
                        dve.wait_ge(s_scale, 2)
            dve.wait_ge(s_mod, 12)
            for j in (13, 14):
                for hh in range(4):
                    h = FIRST[("gemm", j)] + hh + 2
                    if h < DENSE_HALVES:
                        split_lo(dve, h)
                    else:
                        split_lo(dve, h)
                dve.wait_ge(s_xr, 32)
                cols = slice((j - 13) * NW, (j - 12) * NW)
                for t in range(NT):
                    wait_product(dve, j, t)
                    dve.tensor_tensor(out_tmp[:, t % 2, :], bank(product_bank(j, t)), gate1[:, t // NTL, cols],
                                      ALU.mult).then_inc(s_free_d, 1)
                    dve.wait_ge(s_free_d, freed_before("dve", NT * j + t))
                    dve.tensor_tensor(x_r[:, t, cols], x_r[:, t, cols], out_tmp[:, t % 2, :], ALU.add)\
                       .then_inc(s_x1 if j == 14 else s_dve, 1)
                if j == 13:
                    dve.wait_ge(s_dve, own(NT))

            dve.wait_ge(s_x1, NT)
            dve.wait_ge(s_rs2, 1)
            for t in range(NT):
                dve.tensor_scalar(xn_f[:, t, :], x_r[:, t, :], rs[:, t:t + 1], None, ALU.mult).then_inc(s_xf, 1)
            dve.wait_ge(s_xf, NT)
            for t in range(NT):
                dve.wait_ge(s_xh, t + 1)
                dve.tensor_tensor(xn_lo[:, t, :], xn_f[:, t, :], xn_hi[:, t, :].bitcast(F32), ALU.subtract)\
                   .then_inc(s_xl, 1)
            e16 = slice(0, NE)
            dve.wait_ge(s_lgt, 1)
            dve.tensor_copy(lg_t[:, 0:LAT], bank(6, rows=e16)).then_inc(s_dve, 1)
            dve.tensor_copy(lg_t[:, LAT:TOK], bank(7, 0, CTX, rows=e16)).then_inc(s_lgc, 1)
            dve.wait_ge(s_dve, own())
            dve.wait_ge(s_lgn, 1)
            logits = bank(0, 0, NT * NE).rearrange("p (t e) -> p t e", e=NE)

            def over_experts(i):
                return soft_s[:, i, :].unsqueeze(2).broadcast_to([P, NT, NE])

            dve.tensor_reduce(soft_s[:, 0, :], logits, AX.X, ALU.max).then_inc(s_dve, 1)
            dve.wait_ge(s_dve, own())
            dve.tensor_tensor(soft[:, :, :], logits, over_experts(0), ALU.subtract).then_inc(s_sub, 1)
            dve.wait_ge(s_sexp, 1)
            dve.tensor_reduce(soft_s[:, 1, :], soft[:, :, :], AX.X, ALU.add).then_inc(s_dve, 1)
            dve.wait_ge(s_dve, own())
            dve.reciprocal(soft_s[:, 2, :], soft_s[:, 1, :]).then_inc(s_dve, 1)
            dve.wait_ge(s_dve, own())
            dve.tensor_tensor(aff_n[:, :, :], soft[:, :, :], over_experts(2), ALU.mult).then_inc(s_affn, 1)
            dve.wait_ge(s_afft, 1)
            dve.tensor_copy(aff_t[:, :], ps[e16, 512:512 + TOK]).then_inc(s_affc, 1)
            dve.wait_ge(s_affc, 1)
            dve.memset(ones16[:, :], 1.0).then_inc(s_dve, 1)
            dve.tensor_copy(left[:, :], aff_t[:, :]).then_inc(s_dve, 1)
            dve.wait_ge(s_dve, own(2))
            sets = ((slice(0, LAT), CAPL), (slice(LAT, TOK), CAPC))
            n_top = 0
            for cols, cap in sets:
                for _ in range(cap // 8):
                    dve.max(top8[:, n_top, :], left[:, cols]).then_inc(s_dve, 1)
                    dve.wait_ge(s_dve, own())
                    dve.match_replace(left[:, cols], top8[:, n_top, :], left[:, cols], -1.0).then_inc(s_dve, 1)
                    dve.wait_ge(s_dve, own())
                    n_top += 1
            dve.tensor_scalar(chosen[:, :], left[:, :], 0.0, None, ALU.is_lt).then_inc(s_dve, 1)
            dve.wait_ge(s_dve, own())
            for cols, cap in sets:
                n = cols.stop - cols.start
                dve.tensor_tensor_scan(count[:, cols], ones16[:, 0:n], chosen[:, cols], 0.0, ALU.mult, ALU.add)\
                   .then_inc(s_dve, 1)
            dve.wait_ge(s_dve, own(2))
            dve.tensor_tensor(count[:, :], count[:, :], chosen[:, :], ALU.mult).then_inc(s_dve, 1)
            dve.wait_ge(s_dve, own())
            dve.tensor_scalar(pos_t[:, :], count[:, :], -1.0, None, ALU.add).then_inc(s_pos, 1)
            dve.wait_ge(s_post2, 1)
            dve.tensor_copy(pos_n[:, :, :], bank(3, 0, NT * NE).rearrange("p (t e) -> p t e", e=NE))\
               .then_inc(s_posn, 1)
            dve.wait_ge(s_posn, 1)
            dve.wait_ge(s_x2t, KD)
            dve.tensor_tensor(sel_c[:, :, :], tab[:, T_IOTA:T_IOTA + CAPC].unsqueeze(1).broadcast_to([P, NE, CAPC]),
                              pos_n[:, NTL, :].unsqueeze(2).broadcast_to([P, NE, CAPC]), ALU.is_equal)\
               .then_inc(s_selc, 1)

            def select_group(n):
                for t in range(NTL):
                    dve.tensor_tensor(sel_g[:, t, :].rearrange("p (e s) -> p e s", s=CAPL),
                                      tab[:, T_IOTA:T_IOTA + CAPL].unsqueeze(1).broadcast_to([P, EG, CAPL]),
                                      pos_n[:, t, bass.ds(n * EG, EG)].unsqueeze(2).broadcast_to([P, EG, CAPL]),
                                      ALU.is_equal).then_inc(s_selg, 1)

            def gathered(n):
                for k in range(KD):
                    dve.wait_ge(s_g, n * KD + k + 1)
                    dve.wait_ge(s_xeh, n * KD + k + 1)
                    tmp = h_act[:, k % 2, 0:EG * CAPL]
                    dve.tensor_scalar(tmp, bank(6 + k % 2, 0, EG * CAPL), scale2[:, k, 0:1], mod_t[:, 24 + k, 0:1],
                                      ALU.mult, ALU.add).then_inc(s_xet, 1)
                    dve.wait_ge(s_xet, n * KD + k + 1)
                    dve.tensor_tensor(latent_slots(xe_lo, k), four(tmp), latent_slots(xe_hi, k).bitcast(F32),
                                      ALU.subtract).then_inc(s_xel, 1)

            select_group(0)
            dve.wait_ge(s_clear, 1)
            gathered(0)

            def body(i, last):
                H0 = DENSE_HALVES

                def expert_split(h):
                    if last and h >= GH:
                        return
                    g = H0 + h
                    dve.wait_ge(s_hi, i * GH + g + 1)
                    dve.tensor_tensor(w_lo[:, g % NHL, :], raw[:, g // 2 % NRAW, (g % 2) * HALF:(g % 2 + 1) * HALF],
                                      w_hi[:, g % NHL, :].bitcast(F32), ALU.subtract).then_inc(s_lo, 1)

                def select_slots(q):
                    dve.wait_ge(s_pb, 256 * i + (64, 128, 256)[q])
                    n = LAT if q < 2 else CTX
                    dst = sel_t[:, q, :] if q < 2 else sel_tc[:, :]
                    slot = T_SLAT if q < 2 else T_SCTX
                    dve.tensor_scalar(dst, pos_b[:, 0:n], tab[:, slot:slot + 1], None, ALU.is_equal)\
                       .then_inc(s_selt, 1)
                    dve.wait_ge(s_selt, 3 * i + q + 1)
                    dve.tensor_tensor(aff_b[:, 0:n], aff_b[:, 0:n], dst.bitcast(F32), ALU.mult).then_inc(s_gm, 1)
                    dve.wait_ge(s_gm, 3 * i + q + 1)
                    dve.tensor_reduce(gate_p[:, q:q + 1], aff_b[:, 0:n], AX.X, ALU.add).then_inc(s_gate, 1)

                def gates_of_rows():
                    dve.wait_ge(s_gate, 3 * i + 4)
                    dve.wait_ge(s_clear, 1)
                    for v in range(2):
                        rows = slice(64 * v, 64 * v + 64)
                        by_pair = gate_e[rows, :].rearrange("p (a b) -> p b a", b=2)
                        dve.tensor_copy(by_pair[:, v, :], gate_p[rows, 0:2]).then_inc(s_gep, 1)
                    for e in range(EG):
                        rows = slice(CROW[e], CROW[e] + 32)
                        dve.tensor_copy(gate_e[rows, e:e + 1], gate_p[rows, 2:3]).then_inc(s_gep, 1)

                def hidden(e, f):
                    dve.wait_ge(s_half, i * GH + H0 + 24 * e + 8 * f + 8)
                    dve.wait_ge(s_silu2, i * 8 + 2 * e + f + 1)
                    dve.tensor_tensor(h_act[:, f, :], h_act[:, f, :], bank(2 + f), ALU.mult).then_inc(s_hm, 1)

                def hidden_lo(e, f):
                    dve.wait_ge(s_h2h, i * 8 + 2 * e + f + 1)
                    o = slice(4 * f, 4 * f + 4)
                    dve.tensor_tensor(ht2_lo[:, o, :], bank(6 + f).rearrange("p (k c) -> p k c", c=P),
                                      ht2_hi[:, o, :].bitcast(F32), ALU.subtract).then_inc(s_h2l, 1)

                def output(e):
                    dve.wait_ge(s_half, i * GH + H0 + 24 * e + 24)
                    dve.wait_ge(s_gep, 6 * i + 6)
                    dve.wait_ge(s_yec, i * EG + e + 1)
                    dve.tensor_scalar(ye_f[:, :], ps[:, 4 * 512:6 * 512], gate_e[:, e:e + 1], None, ALU.mult)\
                       .then_inc(s_yef, 1)

                def output_lo(e):
                    rows = slice(64 * (e % 2), 64 * (e % 2) + 64)
                    dve.wait_ge(s_yef, i * EG + e + 1)
                    dve.wait_ge(s_yeh, i * EG + e + 1)
                    dve.tensor_tensor(ye_lo[rows, e // 2, :], ye_f[rows, :], ye_hi[rows, e // 2, :].bitcast(F32),
                                      ALU.subtract).then_inc(s_yel, 1)

                for e in range(EG):
                    for hh in range(24):
                        expert_split(24 * e + hh + 2)
                        if e == 0 and hh in (2, 8, 14):
                            select_slots((hh - 2) // 6)
                        if e == 0 and hh == 16:
                            gates_of_rows()
                        if e == 0 and hh == 4 and not last:
                            select_group(i + 1)
                        if e and hh == 0:
                            output(e - 1)
                        if e and hh == 2:
                            output_lo(e - 1)
                        if hh in (7, 15):
                            hidden(e, hh // 8)
                        if hh in (11, 17):
                            hidden_lo(e, hh // 17)
                output(EG - 1)
                output_lo(EG - 1)
                if not last:
                    gathered(i + 1)
                dve.wait_ge(s_add, i * 2 * NT + 1)
                n = 0
                for t in range(NT):
                    for d in range(2):
                        cols = slice(d * NW, (d + 1) * NW)
                        dve.wait_ge(s_cmb, i * 2 * NT + n + 1)
                        dve.tensor_tensor(acc[:, t, cols], acc[:, t, cols], bank(6 + n % 2), ALU.add)\
                           .then_inc(s_add, 1)
                        n += 1

            groups(dve, body)
            dve.wait_ge(s_add, NG * 2 * NT + 1)
            dve.wait_ge(s_fin, 48)
            for t in range(NT):
                if t:
                    dve.wait_ge(s_fx, t)
                dve.tensor_tensor(ge_tmp[:, :], acc[:, t, :], gate2_f[:, t // NTL, :], ALU.mult).then_inc(s_dve, 1)
                dve.wait_ge(s_dve, own())
                dve.tensor_tensor(x_f[:, t, :], x_f[:, t, :], ge_tmp[:, :], ALU.add).then_inc(s_fx, 1)
            dve.wait_ge(s_frs, 1)
            dve.wait_ge(s_fx, NT)
            for t in range(NT):
                dve.scalar_tensor_tensor(x_f[:, t, :], x_f[:, t, :], rs[:, t:t + 1], g_fin[:, :], ALU.mult, ALU.mult)\
                   .then_inc(s_fy, 1)

        @block.gpsimd
        def _(pool):
            n_own = [0]

            def own(n=1):
                n_own[0] += n
                return n_own[0]

            vd = [(0, c[0], 8), (8, c_ctx, 8), (16, g_attn_norm[0], 8), (24, g_ffn_norm[0], 8), (32, b_mod[0], 48),
                  (80, g_diff_norm[0], 1)]
            for r, src, n in vd:
                pool.dma_start(vec[r:r + n, :], src.rearrange("(r n) -> r n", n=P)).then_inc(s_vec, 16)
            pool.dma_start(tab2[:, :], constants[:, T_KEPT:T_W]).then_inc(s_tab2, 16)
            for n, src in enumerate((lambda_q1, lambda_k1, lambda_q2, lambda_k2)):
                flat = src.rearrange("a h d -> a (h d)")
                pool.dma_start(lam_w[:, n, :, :].rearrange("p h d -> p (h d)"), flat.to_broadcast([P, HB * HD]))\
                    .then_inc(s_bc, 16)
            pool.dma_start(g_qk[:, 0, :], g_q_norm.to_broadcast([P, HD])).then_inc(s_bc, 16)
            pool.dma_start(g_qk[:, 1, :], g_k_norm.to_broadcast([P, HD])).then_inc(s_bc, 16)

            def load_key_cache(n):
                rows = slice(n * P, (n + 1) * P)
                pool.dma_start(k_cache[:, 0:KVA, :], cache_attn_k[0, 0, rows]).then_inc(s_kc[n], 16)
                pool.dma_start(k_cache[:, KVA:, :].rearrange("p m d -> p (m d)"),
                               cache_diff_k[0, 0, rows].rearrange("p h i d -> p (h i d)")).then_inc(s_kc[n], 16)

            load_key_cache(0)
            pool.dma_start(va_cache[:, :, :], cache_attn_v[0, 0].rearrange("(t p) h d -> p t (h d)", p=P))\
                .then_inc(s_vac, 16)
            pool.dma_start(vb_n[:, 0:2, :], cache_diff_v[0, 0].rearrange("(t p) h d -> p t (h d)", p=P))\
                .then_inc(s_vc, 16)

            def one_over_rms(dst, sums, count_of, semaphore):
                pool.tensor_scalar(dst, sums, 1.0 / count_of, EPS, ALU.mult, ALU.add).then_inc(s_pool, 1)
                pool.wait_ge(s_pool, own())
                n = dst.shape[1]
                pool.tensor_tensor(dst, dst, minus_half.broadcast_to([P, n]), ALU.pow).then_inc(semaphore, 1)

            pool.wait_ge(s_ss, NT)
            pool.wait_ge(s_tab, 16)
            pool.wait_ge(s_tab2, 16)
            one_over_rms(rs[:, :], ss[:, :], D, s_rs)
            pool.wait_ge(s_vac, 16)
            pool.tensor_copy(va_hi[:, 0:2, :], va_cache[:, :, :]).then_inc(s_pool, 1)
            pool.wait_ge(s_pool, own())
            pool.tensor_tensor(va_lo[:, 0:2, :], va_cache[:, :, :], va_hi[:, 0:2, :].bitcast(F32), ALU.subtract)\
                .then_inc(s_pool, 1)
            pool.wait_ge(s_pool, own())

            turned = [0, 0]

            def make_parts(kind, src):
                parts = (ka_parts, kb_parts)[kind]
                if turned[kind]:
                    pool.wait_ge(s_ktr, turned[kind])
                turned[kind] = max(turned) + 1 + kind
                pool.tensor_copy(parts[:, :, 0, :], src).then_inc(s_pool, 1)
                pool.wait_ge(s_pool, own())
                pool.tensor_tensor(parts[:, :, 1, :], src, parts[:, :, 0, :].bitcast(F32), ALU.subtract)\
                    .then_inc(s_kparts, 1)

            pool.wait_ge(s_kc[0], 32)
            make_parts(0, k_cache[:, 0:KVA, :])
            make_parts(1, k_cache[:, KVA:, :])
            pool.wait_ge(s_kparts, 2)
            load_key_cache(1)
            for t in range(NT):
                pool.wait_ge(s_qss, t + 1)
                one_over_rms(q_rs[:, t, :], q_ss[:, t, :], HD, s_qrs)
            pool.wait_ge(s_kc[1], 32)
            make_parts(0, k_cache[:, 0:KVA, :])
            make_parts(1, k_cache[:, KVA:, :])

            def rope(x, heads, t):
                cos = tab2[:, T_COS - T_KEPT + 64 * t:T_COS - T_KEPT + 64 * t + 64]
                sin = tab2[:, T_SIN - T_KEPT + 64 * t:T_SIN - T_KEPT + 64 * t + 64]
                n = heads * HD
                a = rope_a[:, 0:n].rearrange("p (h d) -> p h d", d=HD)
                pool.tensor_tensor(a, x, cos.unsqueeze(1).broadcast_to([P, heads, HD]), ALU.mult).then_inc(s_pool, 1)
                b = rope_b[:, 0:n].rearrange("p (h a f c) -> p h a f c", a=2, f=2, c=16)
                x4 = x.rearrange("p h (a f c) -> p h a f c", a=2, f=2)
                s4 = sin.rearrange("p (a f c) -> p a f c", a=2, f=2)
                for f in range(2):
                    pool.tensor_tensor(b[:, :, :, f, :], x4[:, :, :, 1 - f, :],
                                       s4[:, :, f, :].unsqueeze(1).broadcast_to([P, heads, 2, 16]), ALU.mult)\
                        .then_inc(s_pool, 1)
                pool.wait_ge(s_pool, own(3))
                pool.tensor_tensor(x, a, rope_b[:, 0:n].rearrange("p (h d) -> p h d", d=HD), ALU.add)\
                    .then_inc(s_pool, 1)
                pool.wait_ge(s_pool, own())

            def gain(x, heads, which):
                pool.tensor_tensor(x, x, g_qk[:, which, :].unsqueeze(1).broadcast_to([P, heads, HD]), ALU.mult)\
                    .then_inc(s_pool, 1)
                pool.wait_ge(s_pool, own())

            pool.wait_ge(s_bc, 16 * 6)
            pool.wait_ge(s_htl, KD)
            for t in range(NT):
                pool.wait_ge(s_free_d, t + 1)
                gain(q_n[:, t, 0:HA, :], HA, 0)
                if t < NTL:
                    rope(q_n[:, t, 0:HA, :], HA, t)
            for t in range(NT):
                pool.wait_ge(s_qss, NT + t + 1)
                one_over_rms(q_rs[:, t, 0:KVA], q_ss[:, t, 0:KVA], HD, s_qrs)
            for t in range(NT):
                pool.wait_ge(s_free_d, NT + t + 1)
                gain(k_n[:, t, 0:KVA, :], KVA, 1)
                if t < NTL:
                    rope(k_n[:, t, 0:KVA, :], KVA, t)
                make_parts(0, k_n[:, t, 0:KVA, :])
            for t in range(NT):
                pool.wait_ge(s_free_a, NT + t + 1)
                if t < NTL:
                    rope(k_n[:, t, KVA:, :], 2 * HB, t)
                make_parts(1, k_n[:, t, KVA:, :])
            pool.dma_start(new_attn_k[0, 0], k_n[:, NTL, 0:KVA, :]).then_inc(s_kout, 16)
            pool.dma_start(new_diff_k[0, 0].rearrange("p h i d -> p (h i d)"),
                           k_n[:, NTL, KVA:, :].rearrange("p m d -> p (m d)")).then_inc(s_kout, 16)
            pool.dma_start(new_attn_v[0, 0].rearrange("p h d -> p (h d)"), va_ctx[:, :]).then_inc(s_out, 16)
            for t in range(NTL):
                rope(q_n[:, t, HA:MAPS, :], 2 * HB, t)

            def query_parts(m):
                if m:
                    pool.wait_ge(s_qtr, 2 * m)
                q = q_n[:, :, m, :].unsqueeze(2).broadcast_to([P, NT, 2, HD])
                pool.tensor_copy(q_parts[:, :, 0:2, :], q).then_inc(s_pool, 1)
                pool.wait_ge(s_pool, own())
                pool.tensor_tensor(q_parts[:, :, 2:4, :], q, q_parts[:, :, 0:2, :].bitcast(F32), ALU.subtract)\
                    .then_inc(s_qp, 1)

            def value_parts(h):
                if h:
                    pool.wait_ge(s_pv, 3 * (HA + h))
                v = vb_n[:, :, h * P:(h + 1) * P]
                pool.tensor_copy(vb_hi[:, :, :], v).then_inc(s_pool, 1)
                pool.wait_ge(s_pool, own())
                pool.tensor_tensor(vb_lo[:, :, :], v, vb_hi[:, :, :].bitcast(F32), ALU.subtract).then_inc(s_vb, 1)

            pool.wait_ge(s_spill, 32)
            pool.wait_ge(s_half, HALVES_B)
            query_parts(0)
            pool.wait_ge(s_free_a, 3 * NT)
            pool.dma_start(new_diff_v[0, 0].rearrange("p h d -> p (h d)"), vb_n[:, 2 + NTL, :]).then_inc(s_out, 16)
            pool.wait_ge(s_vc, 16)
            value_parts(0)
            pool.wait_ge(s_kout, 32)
            query_parts(1)
            for s in range(1, NU + LAG + 3):
                for m in range(1, MAPS - 1):
                    if PREP[m] + 1 == s:
                        query_parts(m + 1)
                if s <= NU:
                    m, t = UNITS[s - 1]
                    n = KTL * P if t < NTL else P
                    second = m >= HA and (m - HA) % 2 == 1
                    if m < HA or second:
                        pool.wait_ge(s_rinv, s)
                        p = probs[:, (s - 1) % 4, 0:n]
                        pool.tensor_scalar(p, p, row_inv[:, (s - 1) % 8:(s - 1) % 8 + 1], None, ALU.mult)\
                            .then_inc(s_c1 if second else s_nrm, 1)
                for h in range(1, HB):
                    if PUS[NT * (HA + h) - 1][2] + 4 == s:
                        value_parts(h)
            pool.wait_ge(s_pv, len(BLOCKS))
            pool.dma_start(ht_hi[:, :, :].rearrange("p k t -> p (k t)"), ht_dram[:, 0, :]).then_inc(s_refill, 16)
            pool.dma_start(ht_lo[:, :, :].rearrange("p k t -> p (k t)"), ht_dram[:, 1, :]).then_inc(s_refill, 16)
            pool.wait_ge(s_half, FIRST[("gemm", 11)] + NHALF[("gemm", 11)])
            for gate, part, semaphore in ((gate1, 2, s_gb1), (gate2, 5, s_gb2)):
                for v in range(2):
                    pool.dma_start(gate[:, v, :], b_mod[:, part * D:(part + 1) * D].to_broadcast([P, D]))\
                        .then_inc(semaphore, 16)
            pool.wait_ge(s_half, FIRST[("gemm", 12)] + NHALF[("gemm", 12)])
            pool.dma_start(x_r[:, 0:NTL, :], x_sample[0].rearrange("(t p) d -> p t d", p=P)).then_inc(s_xr, 16)
            pool.dma_start(x_r[:, NTL, :], x_prompt[0]).then_inc(s_xr, 16)
            pool.wait_ge(s_half, DENSE_HALVES)
            pool.dma_start(router[:, :, :], w_router[0].rearrange("(k p) e -> p k e", p=P)).then_inc(s_router, 16)
            pool.wait_ge(s_ss2, NT)
            one_over_rms(rs[:, :], ss[:, :], D, s_rs2)
            pool.wait_ge(s_x1out, 16)
            pool.wait_ge(s_xf, NT)
            pool.memset(acc[:, :, :], 0.0).then_inc(s_add, 1)
            pool.wait_ge(s_affc, 1)
            pool.dma_start(aff_dram[:, :], aff_t[:, :]).then_inc(s_route, 16)
            pool.wait_ge(s_pos, 1)
            pool.dma_start(pos_dram[:, :], pos_t[:, :]).then_inc(s_route, 16)
            pool.wait_ge(s_xl, NT)
            pool.memset(yc_hi[:, :].bitcast(F32), 0.0).then_inc(s_pool, 1)
            pool.memset(yc_lo[:, :].bitcast(F32), 0.0).then_inc(s_yec, 1)
            pool.memset(gate_e[:, :], 0.0).then_inc(s_gate, 1)
            pool.memset(xe_hi[:, :, :].bitcast(F32), 0.0).then_inc(s_pool, 1)
            pool.wait_ge(s_route, 32)
            pool.wait_ge(s_pool, own(2))
            pool.wait_ge(s_add, 1)
            pool.wait_ge(s_yec, 1)
            pool.wait_ge(s_gate, 1)
            pool.memset(xe_lo[:, :, :].bitcast(F32), 0.0).then_inc(s_clear, 1)
            pool.wait_ge(s_clear, 1)

            def body(i, last):
                H0 = DENSE_HALVES
                pool.wait_ge(s_xc, KD)
                pool.wait_ge(s_yec, i * EG + 1)
                pool.wait_ge(s_half, i * GH + H0)
                pool.tensor_copy(xc_g[:, :, :], xc_f[:, :, bass.ds(i * EG * CAPC, EG * CAPC)]).then_inc(s_xcg, 1)
                pool.wait_ge(s_xcg, i + 1)
                for n, col in enumerate((CCOL[0], CCOL[2])):
                    src = xc_g[:, :, 2 * n * CAPC:2 * (n + 1) * CAPC]
                    pool.tensor_tensor(xe_hi[:, :, col:col + 2 * CAPC], src,
                                       one.unsqueeze(2).broadcast_to([P, KD, 2 * CAPC]), ALU.mult).then_inc(s_xech, 1)
                pool.wait_ge(s_xech, 2 * i + 2)
                for n, col in enumerate((CCOL[0], CCOL[2])):
                    src = xc_g[:, :, 2 * n * CAPC:2 * (n + 1) * CAPC]
                    pool.tensor_tensor(xe_lo[:, :, col:col + 2 * CAPC], src,
                                       xe_hi[:, :, col:col + 2 * CAPC].bitcast(F32), ALU.subtract)\
                        .then_inc(s_xeclo, 1)

                def spread(dst, src, e, rows, cols):
                    pool.dma_start(dst[rows, 0:cols.stop - cols.start],
                                   src[bass.ds(i * EG + e, 1), cols].to_broadcast(
                                       [rows.stop - rows.start, cols.stop - cols.start])).then_inc(s_pb, 16)

                for q in range(3):
                    pool.wait_ge(s_gate, i * 3 + q + 1)
                    for dst, src in ((pos_b, pos_dram), (aff_b, aff_dram)):
                        if q < 2:
                            for v in range(2):
                                spread(dst, src, 2 * q + v, slice(64 * v, 64 * v + 64), slice(0, LAT))
                        else:
                            for e in range(EG):
                                r = CROW[e]
                                spread(dst, src, e, slice(r, r + 32), slice(LAT, TOK))
                for e in range(EG):
                    rows = slice(CROW[e], CROW[e] + CAPC)
                    pool.wait_ge(s_yec, i * EG + e + 1)
                    pool.wait_ge(s_yef, i * EG + e + 1)
                    pool.tensor_tensor(yc_hi[rows, :], ye_f[rows, :], one[rows].broadcast_to([CAPC, D]), ALU.mult)\
                        .then_inc(s_ych, 1)
                    pool.wait_ge(s_ych, i * EG + e + 1)
                    pool.tensor_tensor(yc_lo[rows, :], ye_f[rows, :], yc_hi[rows, :].bitcast(F32), ALU.subtract)\
                        .then_inc(s_yec, 1)

            with pool.Fori(0, NG - 1) as i:
                body(i, False)
            pool.wait_ge(s_g, NG * KD)
            pool.dma_start(x_f[:, :, :], x1_dram[:, :, :]).then_inc(s_fin, 16)
            pool.dma_start(gate2_f[:, :, :], g2_dram[:, :, :]).then_inc(s_fin, 16)
            pool.dma_start(g_fin[:, :], g_final.rearrange("(a n) -> a n", a=1).to_broadcast([P, D]))\
                .then_inc(s_fin, 16)
            body(NG - 1, True)
            pool.wait_ge(s_yec, NE + 1)
            pool.wait_ge(s_fss, NT)
            one_over_rms(rs[:, :], ss[:, :], D, s_frs)
            ys = y_sample[0].rearrange("(t p) d -> t p d", p=P)
            for t in range(NT):
                pool.wait_ge(s_fy, t + 1)
                pool.dma_start(ys[t] if t < NTL else y_prompt[0], x_f[:, t, :]).then_inc(s_out, 16)
            pool.wait_ge(s_out, 16 * (2 + NT))


_INS = ["x_prompt", "x_sample", "cache_attn_k", "cache_attn_v", "cache_diff_k", "cache_diff_v", "c", "c_ctx",
        "w_mod", "b_mod", "g_attn_norm", "g_ffn_norm", "w_in", "g_q_norm", "g_k_norm", "lambda_q1", "lambda_k1",
        "lambda_q2", "lambda_k2", "g_diff_norm", "w_branch_a", "w_branch_b", "w_out", "w_router", "w_exp_gate",
        "w_exp_up", "w_exp_down", "g_final"]
_OUTS = [(1, CTX, D), (1, LAT, D), (1, 1, CTX, KVA, HD), (1, 1, CTX, KVA, HD), (1, 1, CTX, HB, 2, HD),
         (1, 1, CTX, HB, 2 * HD)]


def kernel(**inputs):
    import numpy as _np
    import concourse.bacc as _bacc
    from concourse import mybir as _mybir
    from concourse.bass_utils import run_bass_kernel_spmd as _run

    nc = _bacc.Bacc("TRN2", target_bir_lowering=False, num_devices=1)
    arrays, args = {}, []
    for name in _INS:
        a = _np.ascontiguousarray(inputs[name])
        arrays[f"in_{name}_dram"] = a
        args.append(nc.dram_tensor(f"in_{name}_dram", a.shape, _mybir.dt.from_np(a.dtype), kind="ExternalInput").ap())
    a = table_of_constants()
    arrays["in_constants_dram"] = a
    args.append(nc.dram_tensor("in_constants_dram", a.shape, _mybir.dt.float32, kind="ExternalInput").ap())
    for i, shape in enumerate(_OUTS):
        args.append(nc.dram_tensor(f"out_{i}_dram", shape, _mybir.dt.float32, kind="ExternalOutput").ap())
    build(nc, *args)
    r = _run(nc, [arrays], core_ids=[0])
    return tuple(r.results[0][f"out_{i}_dram"] for i in range(len(_OUTS)))
```

```python
from contextlib import ExitStack

import concourse.bass as bass
from concourse import mybir

F32 = mybir.dt.float32
F32R = mybir.dt.float32r
ALU = mybir.AluOpType
ACT = mybir.ActivationFunctionType
AX = mybir.AxisListType

P = 128
D = 1024
KD = D // P
LAT, CTX = 512, 128
TOK = LAT + CTX
NT = TOK // P
NTL = LAT // P
PAST = 256
HD = 64
HA, KVA = 8, 2
HB = 4
MAPS = HA + 2 * HB
KMAPS = KVA + 2 * HB
KEYS = PAST + TOK
KT = KEYS // P
KTL = (PAST + LAT) // P
NE = 16
CAPL, CAPC = 2 * LAT // NE, 2 * CTX // NE
LAM_INIT = 0.8 - 0.6 * 1.0
EPS = 1e-6
SCALE = HD ** -0.5
NW = 512
CH = 2048
HALF = CH // 2
NRAW, NHL = 4, 3
EG = 4
NG = NE // EG
PITCH = 416

WIN = [0, 80, 208, 288]
LCOL = [0, 144, 208, 352]
CROW = [64, 0, 96, 32]
CCOL = [WIN[e] + CROW[e] for e in range(EG)]

GEMMS = [("qa", 512, 8), ("qb", 512, 8), ("kv", 256, 8), ("kb", 512, 8), ("vb", 512, 8),
         ("ga0", 512, 8), ("wa0", 512, 4), ("gb0", 512, 8), ("wb0", 512, 4),
         ("ga1", 512, 8), ("wa1", 512, 4), ("gb1", 512, 8), ("wb1", 512, 4),
         ("out0", 512, 8), ("out1", 512, 8)]
W_IN_COL = {"qa": 0, "kv": 512, "qb": 768, "kb": 1280, "vb": 1792, "ga0": 2304, "ga1": 2816,
            "gb0": 3328, "gb1": 3840}
GN = [g[0] for g in GEMMS]
FREED_BY = {"qa": "dve", "qb": "act", "kv": "dve", "kb": "act", "vb": "act"}
for _n in GN[5:]:
    FREED_BY[_n] = "act" if _n[0] == "g" else "dve"
STREAM = [("mod", j) for j in range(4)] + [("gemm", j) for j in range(13)] + \
         [("mod", j) for j in range(4, 12)] + [("gemm", j) for j in (13, 14)]
FIRST = {}
NHALF = {}
_h = 0
for _e in STREAM:
    _n = 4 if _e[0] == "mod" else (GEMMS[_e[1]][1] * GEMMS[_e[1]][2]) // HALF
    FIRST[_e], NHALF[_e] = _h, _n
    _h += _n
DENSE_HALVES = _h
HALVES_B = FIRST[("gemm", 5)]
GH = 24 * EG
NB6 = 6

UNITS = [(m, t) for m in range(HA) for t in range(NT)] + \
        [(HA + 2 * h + i, t) for h in range(HB) for t in range(NT) for i in range(2)]
NU = len(UNITS)
U_FIRST = {m: min(s for s, u in enumerate(UNITS) if u[0] == m) for m in range(MAPS)}
U_LAST = {m: max(s for s, u in enumerate(UNITS) if u[0] == m) for m in range(MAPS)}
PREP = {m: 0 if m == 0 else U_FIRST[m] - (2 if m <= HA else 1) for m in range(MAPS)}
PU_OF, PUS = {}, []
for _s, (_m, _t) in enumerate(UNITS):
    if _m < HA or (_m - HA) % 2 == 1:
        PU_OF[_s] = len(PUS)
        PUS.append((_m if _m < HA else HA + (_m - HA) // 2, _t, _s))
BLOCKS = [(h, b) for h in range(HA + HB) for b in range(3)]
BLK_OF = {i: BLOCKS.index((h, min(t // 2, 2))) for i, (h, t, _) in enumerate(PUS)}
BLK_END = {BLK_OF[i]: i for i in range(len(PUS))}
LAG = 2

T_ID, T_IOTA, T_SLAT, T_SCTX, T_EPS, T_NH, T_ONES = 0, 128, 192, 193, 194, 195, 196
T_KEPT = 200
T_SEL, T_SB, T_MEAN, T_COS, T_SIN = 200, 202, 458, 586, 842
T_W = 1098


def table_of_constants():
    import numpy as np
    t = np.zeros((P, T_W), np.float32)
    p = np.arange(P)
    t[:, T_ID:T_ID + P] = np.eye(P)
    t[:, T_IOTA:T_IOTA + 64] = np.arange(64)
    t[:, T_SLAT] = p % 64
    t[:, T_SCTX] = p % 32
    t[:, T_EPS] = EPS
    t[:, T_NH] = -0.5
    t[:, T_ONES] = 1.0
    t[0:4:2, T_SEL] = 1.0
    t[1:4:2, T_SEL + 1] = 1.0
    t[0:4:2, T_SB:T_SB + P] = 1.0
    t[1:4:2, T_SB + P:T_SB + 2 * P] = 1.0
    t[:, T_MEAN:T_MEAN + P] = 1.0 / P
    n = np.arange(LAT)
    freqs = np.float32(10000.0) ** (-np.arange(16, dtype=np.float32) / np.float32(16))
    ang = np.stack([(n // 64).astype(np.float32)[:, None] * freqs,
                    (n % 64).astype(np.float32)[:, None] * freqs], 1)
    c, s = np.cos(ang), np.sin(ang)
    cos = np.stack([c, c], 2).reshape(NTL, P, 64)
    sin = np.stack([-s, s], 2).reshape(NTL, P, 64)
    t[:, T_COS:T_COS + 256] = cos.transpose(1, 0, 2).reshape(P, 256)
    t[:, T_SIN:T_SIN + 256] = sin.transpose(1, 0, 2).reshape(P, 256)
    return t


def build(nc, x_prompt, x_sample, cache_attn_k, cache_attn_v, cache_diff_k, cache_diff_v, c, c_ctx,
          w_mod, b_mod, g_attn_norm, g_ffn_norm, w_in, g_q_norm, g_k_norm, lambda_q1, lambda_k1,
          lambda_q2, lambda_k2, g_diff_norm, w_branch_a, w_branch_b, w_out, w_router, w_exp_gate,
          w_exp_up, w_exp_down, g_final, constants,
          y_prompt, y_sample, new_attn_k, new_attn_v, new_diff_k, new_diff_v):
    ctx = ExitStack()
    with ctx:
        def sb(name, shape, dt=F32):
            return ctx.enter_context(nc.sbuf_tensor(name, shape, dt))

        def sem(name):
            return ctx.enter_context(nc.semaphore(name))


        raw = sb("raw", [P, NRAW, CH])
        tab = sb("tab", [P, T_KEPT])
        mod_t = sb("mod_t", [P, 6 * KD, 2])
        scale1 = sb("scale1", [P, KD, 2])
        scale2 = sb("scale2", [P, KD, 2])
        vec_t = sb("vec_t", [P, 81])
        c_hi = sb("c_hi", [P, KD, 4], F32R)
        c_lo = sb("c_lo", [P, KD, 4], F32R)
        g_qk = sb("g_qk", [P, 2, HD])
        ss = sb("ss", [P, NT])
        rs = sb("rs", [P, NT])
        q_ss = sb("q_ss", [P, NT, HA])
        q_rs = sb("q_rs", [P, NT, HA])
        neg_max = sb("neg_max", [P, 8])
        row_sum = sb("row_sum", [P, 8])
        row_inv = sb("row_inv", [P, 8])
        lam = sb("lam", [P, 3 * HB])
        g_dif = sb("g_dif", [P, 1])
        aff_n = sb("aff_n", [P, NT, NE])
        pos_n = sb("pos_n", [P, NT, NE])
        gate_p = sb("gate_p", [P, 3])
        gate_e = sb("gate_e", [P, EG])
        base = nc.sbuf_base + (-nc.sbuf_base) % 32
        room = nc.sbuf_usable_end - base

        def at(name, offset, shape, dt=F32):
            size = 4
            for n in shape[1:]:
                size *= n
            assert offset + size <= room, (name, offset + size, room)
            return nc.alloc_sbuf_tensor_at(name, shape, dt, offset=base + offset)

        ident = tab[:, T_ID:T_ID + P]
        eps = tab[:, T_EPS:T_EPS + 1]
        minus_half = tab[:, T_NH:T_NH + 1]
        one = tab[:, T_ONES:T_ONES + 1]

        RING = 151584
        w_hi = at("w_hi", RING, [P, NHL, HALF], F32R)
        w_lo = at("w_lo", RING + 12288, [P, NHL, HALF], F32R)
        ht_hi = at("ht_hi", 0, [P, KD, TOK], F32R)
        ht_lo = at("ht_lo", 20480, [P, KD, TOK], F32R)
        keys_t = at("keys_t", 40960, [P, KMAPS, KEYS], F32R)
        squares = at("squares", 40960, [P, D])
        va_hi = at("va_hi", 76800, [P, KT, P], F32R)
        va_lo = at("va_lo", 80384, [P, KT, P], F32R)
        vb_n = at("vb_n", 83968, [P, KT, HB * P])
        x_n = at("x_n", 98304, [P, NT, D])
        q_n = at("q_n", 98304, [P, NT, MAPS, HD])
        T0 = 118784
        q_sq = at("q_sq", T0, [P, 2, NW])
        mod_row = at("mod_row", T0, [4, 2, NW])
        h_tmp = [at("h_tmp0", T0 + 4096, [P, TOK]), at("h_tmp1", T0, [P, TOK])]
        rope_d = at("rope_d", T0 + 4096, [P, NW])
        rope_p = at("rope_p", T0 + 6144, [P, NW])
        k_n = at("k_n", T0 + 8192, [P, NT, KMAPS, HD])
        vec = at("vec", T0 + 8192, [81, P])
        lam_w = at("lam_w", T0 + 8704, [P, 4, HB, HD])
        ka_parts = at("ka_parts", T0 + 20992, [P, KVA, 2, HD], F32R)
        kb_parts = at("kb_parts", T0 + 22016, [P, 2 * HB, 2, HD], F32R)
        k_cache = at("k_cache", T0 + 26112, [P, KMAPS, HD])
        va_cache = at("va_cache", T0 + 6656, [P, 2, P])
        va_ctx = at("va_ctx", T0 + 28672, [P, P])
        tab2 = at("tab2", T0 + 29184, [P, T_W - T_KEPT])
        probs = at("probs", 0, [P, 4, KTL * P])
        q_parts = at("q_parts", 12288, [P, NT, 4, HD], F32R)
        q_hi_t = at("q_hi_t", 17408, [P, 2, TOK], F32R)
        q_lo_t = at("q_lo_t", 22528, [P, 2, TOK], F32R)
        vb_hi = at("vb_hi", 27648, [P, KT, P], F32R)
        vb_lo = at("vb_lo", 31232, [P, KT, P], F32R)
        y_t = at("y_t", T0, [P, 8, TOK])
        p_hi = at("p_hi", RING, [P, 2, KTL, 2 * P], F32R)
        p_lo = at("p_lo", RING + 12288, [P, 2, KTL, 2 * P], F32R)
        y_sq = at("y_sq", 81920, [P, 2, TOK])
        y_rms = at("y_rms", 87040, [P, 2, TOK])
        yt_hi = at("yt_hi", 40960, [P, 8, TOK], F32R)
        yt_lo = at("yt_lo", 61440, [P, 8, TOK], F32R)
        mt_hi = at("mt_hi", 81920, [P, KD, TOK], F32R)
        mt_lo = at("mt_lo", 102400, [P, KD, TOK], F32R)
        sig = at("sig", 122880, [P, NT, NW])
        merged = at("merged", 133120, [P, NT, NW])
        gate1 = at("gate1", 0, [P, 2, D])
        gate2 = at("gate2", 8192, [P, 2, D])
        mod_row2 = at("mod_row2", 16384, [4, 2, NW])
        x_r = at("x_r", 40960, [P, NT, D])
        out_tmp = at("out_tmp", 61440, [P, 2, NW])
        xn_hi = at("xn_hi", 0, [P, NT, D], F32R)
        xn_lo = at("xn_lo", 20480, [P, NT, D], F32R)
        xn_f = at("xn_f", 122880, [P, NT, D])
        h2_t = at("h2_t", 61440, [P, KD, TOK])
        squares2 = at("squares2", 104448, [P, D])
        lg_t = at("lg_t", 88064, [NE, TOK])
        aff_t = at("aff_t", 108544, [NE, TOK])
        left = at("left", 111104, [NE, TOK])
        count = at("count", 113664, [NE, TOK])
        chosen = at("chosen", 116224, [NE, TOK])
        pos_t = at("pos_t", 118784, [NE, TOK])
        ones16 = at("ones16", 90624, [NE, LAT])
        soft = at("soft", 99328, [P, NT, NE])
        top8 = at("top8", 99648, [NE, 10, 8])
        router = at("router", 100352, [P, KD, NE])
        soft_s = at("soft_s", 100096, [P, 3, NT])
        acc = at("acc", 40960, [P, NT, D])
        xe_hi = at("xe_hi", 61440, [P, KD, PITCH], F32R)
        xe_lo = at("xe_lo", 74752, [P, KD, PITCH], F32R)
        xc_f = at("xc_f", 88064, [P, KD, NE * CAPC])
        xc_g = at("xc_g", 141312, [P, KD, EG * CAPC])
        ht2_hi = at("ht2_hi", 96256, [P, KD, P], F32R)
        ht2_lo = at("ht2_lo", 100352, [P, KD, P], F32R)
        h_act = at("h_act", 104448, [P, 2, NW])
        ye_hi = at("ye_hi", 108544, [P, 2, D], F32R)
        ye_lo = at("ye_lo", 116736, [P, 2, D], F32R)
        yc_hi = at("yc_hi", 124928, [P, D], F32R)
        yc_lo = at("yc_lo", 129024, [P, D], F32R)
        ye_f = at("ye_f", 133120, [P, D])
        sel_c = at("sel_c", 133120, [P, NE, CAPC], F32R)
        sel_g = at("sel_g", 137216, [P, NTL, EG * CAPL], F32R)
        pos_b = at("pos_b", 141312, [P, NW])
        aff_b = at("aff_b", 143360, [P, NW])
        sel_t = at("sel_t", 145408, [P, 2, LAT], F32R)
        sel_tc = at("sel_tc", 149504, [P, CTX], F32R)
        pos_c = at("pos_c", 150016, [P, CTX])
        aff_c = at("aff_c", 150528, [P, CTX])
        x_f = at("x_f", 0, [P, NT, D])
        gate2_f = at("gate2_f", 20480, [P, 2, D])
        g_fin = at("g_fin", 28672, [P, D])

        ht_dram = nc.dram_tensor("ht_dram", [P, 2, KD * TOK], F32R).ap()
        x1_dram = nc.dram_tensor("x1_dram", [P, NT, D], F32).ap()
        g2_dram = nc.dram_tensor("g2_dram", [P, 2, D], F32).ap()
        pos_dram = nc.dram_tensor("pos_dram", [NE, TOK], F32).ap()
        aff_dram = nc.dram_tensor("aff_dram", [NE, TOK], F32).ap()

        ps = ctx.enter_context(nc.psum_tensor("ps", [P, 8 * 512], F32))

        def bank(b, lo=0, hi=512, rows=slice(None)):
            return ps[rows, 512 * b + lo:512 * b + hi]

        s_tab = sem("s_tab"); s_tab2 = sem("s_tab2"); s_vec = sem("s_vec"); s_x = [sem(f"s_tokens{t}") for t in range(NT)]
        s_bc = sem("s_bc"); s_router = sem("s_router")
        s_raw = [sem(f"s_raw{n}") for n in range(NRAW)]
        s_hi = sem("s_hi"); s_lo = sem("s_lo"); s_half = sem("s_half")
        s_silu = sem("s_silu"); s_vect = sem("s_vect"); s_vec_cp = sem("s_vec_cp"); s_csplit = sem("s_csplit")
        s_row = sem("s_row"); s_post = sem("s_post"); s_mod = sem("s_mod"); s_scale = sem("s_scale")
        s_lamw = sem("s_lamw"); s_lame = sem("s_lame"); s_lam = sem("s_lam")
        s_ss = sem("s_ss"); s_rs = sem("s_rs"); s_xn = sem("s_xn"); s_xt = sem("s_xt")
        s_hth = sem("s_hth"); s_htl = sem("s_htl"); s_spill = sem("s_spill"); s_refill = sem("s_refill")
        s_acc = sem("s_acc"); s_free_d = sem("s_free_d"); s_free_a = sem("s_free_a")
        s_qsq = sem("s_qsq"); s_qss = sem("s_qss"); s_qrs = sem("s_qrs"); s_vah = sem("s_vah")
        s_dve = sem("s_dve"); s_pool = sem("s_pool"); s_act = sem("s_act")
        s_qn = sem("s_qn"); s_kparts = sem("s_kparts"); s_ktr = sem("s_ktr"); s_kev = sem("s_kev")
        s_kc = [sem("s_kc0"), sem("s_kc1")]; s_vc = sem("s_vc"); s_vac = sem("s_vac")
        s_qp = sem("s_qp"); s_qtr = sem("s_qtr"); s_qh = sem("s_qh"); s_ql = sem("s_ql")
        s_sc = sem("s_sc"); s_max = sem("s_max"); s_exp = sem("s_exp"); s_rinv = sem("s_rinv")
        s_nrm = sem("s_nrm"); s_c1 = sem("s_c1"); s_comb = sem("s_comb"); s_ptr = sem("s_ptr")
        s_ph = sem("s_ph"); s_pl = sem("s_pl"); s_pv = sem("s_pv"); s_oev = sem("s_oev"); s_vb = sem("s_vb")
        s_ysq = sem("s_ysq"); s_yms = sem("s_yms"); s_yrt = sem("s_yrt"); s_yn = sem("s_yn")
        s_yh = sem("s_yh"); s_yl = sem("s_yl")
        s_mrg = sem("s_mrg"); s_mtr = sem("s_mtr"); s_mth = sem("s_mth"); s_mtl = sem("s_mtl")
        s_gb1 = sem("s_gb1"); s_gb2 = sem("s_gb2"); s_g2out = sem("s_g2out"); s_xr = sem("s_xr")
        s_x1 = sem("s_x1"); s_x1out = sem("s_x1out"); s_ss2 = sem("s_ss2"); s_rs2 = sem("s_rs2")
        s_xf = sem("s_xf"); s_xh = sem("s_xh"); s_xl = sem("s_xl"); s_x2t = sem("s_x2t"); s_h2 = sem("s_h2")
        s_lgt = sem("s_lgt"); s_lgc = sem("s_lgc"); s_lgn = sem("s_lgn"); s_sub = sem("s_sub")
        s_sexp = sem("s_sexp"); s_affn = sem("s_affn"); s_afft = sem("s_afft"); s_affc = sem("s_affc")
        s_pos = sem("s_pos"); s_post2 = sem("s_post2"); s_posn = sem("s_posn"); s_route = sem("s_route")
        s_clear = sem("s_clear"); s_selc = sem("s_selc"); s_gc = sem("s_gc"); s_xc = sem("s_xc")
        s_selg = sem("s_selg"); s_g = sem("s_g"); s_xeh = sem("s_xeh"); s_xel = sem("s_xel")
        s_xeclo = sem("s_xeclo"); s_pb = sem("s_pb"); s_selt = sem("s_selt"); s_gate = sem("s_gate")
        s_silu2 = sem("s_silu2"); s_hm = sem("s_hm"); s_htr = sem("s_htr"); s_h2h = sem("s_h2h")
        s_h2l = sem("s_h2l"); s_yef = sem("s_yef"); s_yeh = sem("s_yeh"); s_yel = sem("s_yel")
        s_yec = sem("s_yec"); s_cmb = sem("s_cmb"); s_add = sem("s_add")
        s_fin = sem("s_fin"); s_fx = sem("s_fx"); s_fss = sem("s_fss"); s_frs = sem("s_frs"); s_fy = sem("s_fy")
        s_out = sem("s_out"); s_kout = sem("s_kout"); s_pbc = sem("s_pbc"); s_htf = sem("s_htf"); s_kn = sem("s_kn"); s_fg = sem("s_fg"); s_gm = sem("s_gm"); s_xet = sem("s_xet")
        s_xech = sem("s_xech"); s_xcg = sem("s_xcg"); s_gep = sem("s_gep"); s_ych = sem("s_ych")

        block = ctx.enter_context(nc.Block())

        def gain(eng, x, heads, which):
            return eng.tensor_tensor(x, x, g_qk[:, which, :].unsqueeze(1).broadcast_to([P, heads, HD]), ALU.mult)

        def rope(eng, x, heads, t, tmp):
            cos = tab2[:, T_COS - T_KEPT + 64 * t:T_COS - T_KEPT + 64 * t + 64]
            sin = tab2[:, T_SIN - T_KEPT + 64 * t:T_SIN - T_KEPT + 64 * t + 64]
            n = heads * HD
            b = tmp[:, 0:n].rearrange("p (h a f c) -> p h a f c", a=2, f=2, c=16)
            x4 = x.rearrange("p h (a f c) -> p h a f c", a=2, f=2)
            s4 = sin.rearrange("p (a f c) -> p a f c", a=2, f=2)
            for f in range(2):
                yield eng.tensor_tensor(b[:, :, :, f, :], x4[:, :, :, 1 - f, :],
                                        s4[:, :, f, :].unsqueeze(1).broadcast_to([P, heads, 2, 16]), ALU.mult)
            yield eng.tensor_tensor(x, x, cos.unsqueeze(1).broadcast_to([P, heads, HD]), ALU.mult)
            yield eng.tensor_tensor(x, x, tmp[:, 0:n].rearrange("p (h d) -> p h d", d=HD), ALU.add)

        def columns(w, col, n, k0, kn):
            return w[k0 * P:(k0 + kn) * P, col:col + n].rearrange("(k p) n -> p k n", p=P)

        chunks = []
        for kind, j in STREAM:
            if kind == "mod":
                for q in range(2):
                    chunks.append([(slice(0, P), columns(w_mod[0], NW * j, NW, 4 * q, 4))])
                continue
            name, n, kt = GEMMS[j]
            if name in W_IN_COL:
                per = CH // n
                for q in range(kt // per):
                    chunks.append([(slice(0, P), columns(w_in[0], W_IN_COL[name], n, per * q, per))])
            elif name[:2] == "wa":
                w = w_branch_a[0].rearrange("(v i p) n -> v p i n", v=2, p=HD)
                c0 = NW * int(name[2])
                chunks.append([(slice(64 * v, 64 * v + 64), w[v][:, :, c0:c0 + NW]) for v in range(2)])
            elif name[:2] == "wb":
                chunks.append([(slice(0, P), columns(w_branch_b[0], NW * int(name[2]), NW, 0, 4))])
            else:
                for q in range(2):
                    chunks.append([(slice(0, P), columns(w_out[0], NW * int(name[3]), NW, 4 * q, 4))])
        NCH = len(chunks)
        assert 2 * NCH == DENSE_HALVES
        raw_count = [0] * NCH
        seen = [0] * NRAW
        for n, parts in enumerate(chunks):
            seen[n % NRAW] += 16 * len(parts)
            raw_count[n] = seen[n % NRAW]

        def half_of(tensor, h, n):
            return tensor[:, h % NHL, :].rearrange("p (k n) -> p k n", n=n)

        def split_hi(act, h):
            if h % 2 == 0:
                act.wait_ge(s_raw[(h // 2) % NRAW], raw_count[h // 2] if h < DENSE_HALVES else expert_raw(0, 0))
            if h >= NHL:
                act.wait_ge(s_half, h - NHL + 1)
            n, q = h // 2 % NRAW, h % 2
            act.activation(w_hi[:, h % NHL, :], raw[:, n, q * HALF:(q + 1) * HALF], ACT.Copy).then_inc(s_hi, 1)

        def split_lo(dve, h):
            dve.wait_ge(s_hi, h + 1)
            n, q = h // 2 % NRAW, h % 2
            dve.tensor_tensor(w_lo[:, h % NHL, :], raw[:, n, q * HALF:(q + 1) * HALF],
                              w_hi[:, h % NHL, :].bitcast(F32), ALU.subtract).then_inc(s_lo, 1)

        def prob_part(dst, i):
            _, t, _ = PUS[i]
            if t == NTL:
                return dst[:, BLK_OF[i] % 2, 0, 0:P], bank(4, 0, P)
            o = (t % 2) * P
            return (dst[:, BLK_OF[i] % 2, :, o:o + P].rearrange("p (a b) c -> p a b c", a=2),
                    ps[:, 2048:3072].rearrange("p (a b) -> p a b", a=2)[:, :, 0:384]
                    .rearrange("p a (b c) -> p a b c", c=P))

        def latent_slots(xe, k):
            v = xe[:, k, LCOL[0]:LCOL[0] + CAPL]
            return bass.AP(tensor=v.tensor, offset=v.offset,
                           ap=[v.ap[0], [LCOL[2] - LCOL[0], 2], [LCOL[1] - LCOL[0], 2], [1, CAPL]])

        def four(x):
            return x.rearrange("p (a b s) -> p a b s", a=2, b=2)

        def product_bank(j, t):
            return (NT * j + t) % NB6

        def wait_product(eng, j, t):
            if t < NT - 1:
                eng.wait_ge(s_acc, (NT - 1) * j + t + 1)
            else:
                eng.wait_ge(s_half, FIRST[("gemm", j)] + NHALF[("gemm", j)])

        def freed_before(owner, q):
            return sum(1 for r in range(q + 1) if FREED_BY[GN[r // NT]] == owner)

        def expert_chunk(e, n):
            if n < 8:
                w = (w_exp_gate, w_exp_up)[n // 2 % 2]
                return w[0, e, (n % 2) * NW:(n % 2 + 1) * NW,
                         (n // 4) * NW:(n // 4 + 1) * NW].rearrange("(k p) n -> p k n", p=P)
            k, d = (n - 8) // 2, (n - 8) % 2
            return w_exp_down[0, e, k * NW:(k + 1) * NW, d * NW:(d + 1) * NW].rearrange("(k p) n -> p k n", p=P)

        def groups(eng, body):
            body(0, True, False)
            with eng.Fori(1, NG - 1) as i:
                body(i, False, False)
            body(NG - 1, False, True)

        EC = 12 * EG

        @block.sync
        def _(sp):
            sp.dma_start(tab[:, :], constants[:, 0:T_KEPT]).then_inc(s_tab, 16)
            for r, src, n in ((0, c[0], 8), (8, c_ctx, 8), (16, g_attn_norm[0], 8), (24, g_ffn_norm[0], 8),
                              (32, b_mod[0], 48), (80, g_diff_norm[0], 1)):
                sp.dma_start(vec[r:r + n, :], src.rearrange("(r n) -> r n", n=P)).then_inc(s_vec, 16)
            xs = x_sample[0].rearrange("(t p) d -> t p d", p=P)
            for n, parts in enumerate(chunks):
                if n >= NRAW:
                    sp.wait_ge(s_lo, 2 * (n - NRAW) + 2)
                for rows, src in parts:
                    k = src.shape[1]
                    sp.dma_start(raw[rows, n % NRAW, :].rearrange("p (k n) -> p k n", k=k), src)\
                      .then_inc(s_raw[n % NRAW], 16)
                if 1 <= n <= NT:
                    t = n - 1
                    sp.dma_start(x_n[:, t, :], xs[t] if t < NTL else x_prompt[0]).then_inc(s_x[t], 16)

            with sp.Fori(0, NG) as i:
                for e in range(EG):
                    for n in range(12):
                        q = 12 * e + n
                        g = NCH + q
                        sp.wait_ge(s_lo, 2 * (g - NRAW) + 2 + GH * i)
                        sp.dma_start(raw[:, g % NRAW, :].rearrange("p (k n) -> p k n", n=NW),
                                     expert_chunk(i * EG + e, n)).then_inc(s_raw[g % NRAW], 16)

        def expert_raw(c, i):
            g = NCH + c
            before = seen[g % NRAW] + 16 * sum(1 for m in range(c + 1) if (NCH + m) % NRAW == g % NRAW)
            return before + 16 * (EC // NRAW) * i

        @block.tensor
        def _(pe):
            def product(j, stat_hi, stat_lo, after_half=None):
                h0, nh = FIRST[("gemm", j)], NHALF[("gemm", j)]
                _, n, kt = GEMMS[j]
                per = HALF // n
                for hh in range(nh):
                    h = h0 + hh
                    pe.wait_ge(s_lo, h + 1)
                    hi, lo = half_of(w_hi, h, n), half_of(w_lo, h, n)
                    for t in range(NT):
                        b = bank(product_bank(j, t), 0, n)
                        q = NT * j + t - NB6
                        if hh == 0 and q >= 0:
                            owner = FREED_BY[GN[q // NT]]
                            pe.wait_ge(s_free_d if owner == "dve" else s_free_a, freed_before(owner, q))
                        for kk in range(per):
                            k = per * hh + kk
                            first, last = k == 0, k == kt - 1
                            tt = slice(t * P, (t + 1) * P)
                            pe.matmul(b, stat_hi(k, tt), hi[:, kk, :], start=first, stop=False)
                            pe.matmul(b, stat_hi(k, tt), lo[:, kk, :], start=False, stop=False)
                            mm = pe.matmul(b, stat_lo(k, tt), hi[:, kk, :], start=False, stop=last)
                        if hh == nh - 1 and t < NT - 1:
                            mm.then_inc(s_acc, 1)
                    mm.then_inc(s_half, 1)
                    if after_half:
                        after_half(hh)

            def mod_product(j, b):
                for hh in range(4):
                    h = FIRST[("mod", j)] + hh
                    pe.wait_ge(s_lo, h + 1)
                    for kk in range(2):
                        k = 2 * hh + kk
                        pe.matmul(bank(b, rows=slice(0, 4)), c_hi[:, k, :], half_of(w_hi, h, NW)[:, kk, :],
                                  start=(k == 0), stop=False)
                        mm = pe.matmul(bank(b, rows=slice(0, 4)), c_lo[:, k, :], half_of(w_lo, h, NW)[:, kk, :],
                                       start=False, stop=(k == KD - 1))
                    mm.then_inc(s_half, 1)

            def mod_turn(j, n, rows):
                pe.wait_ge(s_row, n + 1)
                if n:
                    pe.wait_ge(s_mod, n)
                for i in range(4):
                    mm = pe.matmul(bank(6, 2 * i, 2 * i + 2), rows[0:4, n % 2, i * P:(i + 1) * P],
                                   tab2[0:4, T_SEL - T_KEPT:T_SEL - T_KEPT + 2], start=True, stop=True)
                mm.then_inc(s_post, 1)

            def mod_spread(j, n, rows):
                pe.wait_ge(s_row, n + 1)
                pe.wait_ge(s_mod, n)
                for i in range(2):
                    o = T_SB - T_KEPT + i * P
                    mm = pe.matmul(bank(6 + i), tab2[0:4, o:o + P], rows[0:4, n % 2, :], start=True, stop=True)
                mm.then_inc(s_post, 1)

            pe.wait_ge(s_tab, 16)
            pe.wait_ge(s_silu, 1)
            pe.transpose(bank(5, 0, 81), vec[:, :], ident[0:81, 0:81]).then_inc(s_vect, 1)
            pe.wait_ge(s_csplit, 1)
            pe.wait_ge(s_tab2, 16)
            for j in range(4):
                if j >= 2:
                    pe.wait_ge(s_row, j - 1)
                mod_product(j, j % 2)
                if j:
                    mod_turn(j - 1, j - 1, mod_row)
            mod_turn(3, 3, mod_row)
            pe.wait_ge(s_xn, NT)
            pe.wait_ge(s_row, 4)
            pe.wait_ge(s_mod, 4)
            for k in range(KD):
                if k >= 4:
                    pe.wait_ge(s_htl, k - 3)
                for t in range(NTL):
                    pe.transpose(bank(2 * (k % 4), t * P, (t + 1) * P), x_n[:, t, k * P:(k + 1) * P], ident)
                pe.transpose(bank(2 * (k % 4) + 1, 0, P),
                             x_n[:, NTL, k * P:(k + 1) * P], ident).then_inc(s_xt, 1)
            pe.wait_ge(s_htl, KD)

            def hth(k, tt):
                return ht_hi[:, k, tt]

            def htl(k, tt):
                return ht_lo[:, k, tt]

            turned = [0]

            def turn_keys(n, parts):
                pe.wait_ge(s_kparts, n + 1)
                maps = parts.shape[1]
                for g in range(0, maps, 4):
                    if turned[0] >= 2:
                        pe.wait_ge(s_kev, turned[0] - 1)
                    b = 6 + turned[0] % 2
                    for m in range(min(4, maps - g)):
                        mm = pe.transpose(bank(b, m * P, (m + 1) * P),
                                          parts[:, g + m, :, :].rearrange("p a b -> p (a b)").bitcast(F32), ident)
                    mm.then_inc(s_ktr, 1)
                    turned[0] += 1

            product(0, hth, htl)
            turn_keys(0, ka_parts)
            turn_keys(1, kb_parts)
            turn_keys(2, ka_parts)
            turn_keys(3, kb_parts)
            product(1, hth, htl)
            product(2, hth, htl)
            product(3, hth, htl, lambda hh: turn_keys(4 + hh, ka_parts))
            turn_keys(4 + NTL, ka_parts)
            product(4, hth, htl, lambda hh: turn_keys(4 + NT + hh - 1, kb_parts) if hh else None)
            turn_keys(4 + NT + NTL - 1, kb_parts)
            turn_keys(4 + NT + NTL, kb_parts)

            turns = []

            def turn_banks_free():
                if not turns:
                    pe.wait_ge(s_kev, 3 * KT)
                    return
                kind, n, part = turns[-1]
                if kind == "p":
                    pe.wait_ge(s_pl, n + 1)
                elif part == 0:
                    pe.wait_ge(s_qh, n + 1)
                else:
                    pe.wait_ge(s_ql, n + 1)

            def turn_queries(m):
                pe.wait_ge(s_qp, m + 1)
                for part in range(2):
                    turn_banks_free()
                    for t in range(NT):
                        mm = pe.transpose(bank(4, t * P, (t + 1) * P),
                                          q_parts[:, t, 2 * part:2 * part + 2, :]
                                          .rearrange("p a b -> p (a b)").bitcast(F32), ident)
                    mm.then_inc(s_qtr, 1)
                    turns.append(("q", m, part))

            def scores(s):
                m, t = UNITS[s]
                x = m // (HA // KVA) if m < HA else KVA + m - HA
                if s == U_FIRST[m]:
                    pe.wait_ge(s_qh, m + 1)
                    pe.wait_ge(s_ql, m + 1)
                if s >= 2:
                    pe.wait_ge(s_exp, s - 1)
                b = 2 * (s % 2)
                cols = [(b, 0, 384), (b + 1, 384, 384)] if t < NTL else [(b, KTL * P, P)]
                for part, q in enumerate((q_hi_t, q_lo_t)):
                    for bb, c0, n in cols:
                        mm = pe.matmul(bank(bb, 0, n), q[:, m % 2, t * P:(t + 1) * P], keys_t[:, x, c0:c0 + n],
                                       start=(part == 0), stop=(part == 1))
                mm.then_inc(s_sc, 1)

            def turn_probs(i):
                h, t, s = PUS[i]
                if h < HA:
                    pe.wait_ge(s_nrm, i + 1)
                else:
                    pe.wait_ge(s_comb, i - HA * NT + 1)
                turn_banks_free()
                src = probs[:, (s if h < HA else s - 1) % 4, :]
                for kt in range(KTL if t < NTL else 1):
                    o = (kt % 3) * P
                    mm = pe.transpose(bank(4 + kt // 3, o, o + P), src[:, kt * P:(kt + 1) * P], ident)
                mm.then_inc(s_ptr, 1)
                turns.append(("p", i, 0))

            def values(blk):
                h, b = BLOCKS[blk]
                n = 2 * P if b < 2 else P
                pe.wait_ge(s_pl, BLK_END[blk] + 1)
                if blk >= 2:
                    pe.wait_ge(s_oev, blk - 1)
                if h >= HA and b == 0:
                    pe.wait_ge(s_vb, h - HA + 1)
                vh, vl = (va_hi, va_lo) if h < HA else (vb_hi, vb_lo)
                kts = range(KTL) if b < 2 else [KTL]
                for kt in kts:
                    src = kt if b < 2 else 0
                    o = bank(6 + blk % 2, 0, n)
                    pe.matmul(o, vh[:, kt, :], p_hi[:, blk % 2, src, 0:n], start=(kt == kts[0]), stop=False)
                    pe.matmul(o, vh[:, kt, :], p_lo[:, blk % 2, src, 0:n], start=False, stop=False)
                    mm = pe.matmul(o, vl[:, kt, :], p_hi[:, blk % 2, src, 0:n], start=False, stop=(kt == kts[-1]))
                mm.then_inc(s_pv, 1)

            for s in range(NU + LAG + 1):
                for m in range(MAPS):
                    if PREP[m] == s:
                        turn_queries(m)
                if s < NU:
                    scores(s)
                if s >= LAG and s - LAG in PU_OF:
                    turn_probs(PU_OF[s - LAG])
                if s - LAG - 1 in PU_OF and PU_OF[s - LAG - 1] in BLK_END.values():
                    values(BLK_OF[PU_OF[s - LAG - 1]])
            for h in range(HB):
                pe.wait_ge(s_ysq, h + 1)
                if h >= 2:
                    pe.wait_ge(s_yrt, h - 1)
                b = 2 * (h % 2)
                mean = tab2[:, T_MEAN - T_KEPT:T_MEAN - T_KEPT + P]
                pe.matmul(bank(b), mean, y_sq[:, h % 2, 0:512], start=True, stop=True)
                pe.matmul(bank(b + 1, 0, TOK - 512), mean, y_sq[:, h % 2, 512:TOK], start=True, stop=True)\
                  .then_inc(s_yms, 1)

            def turn_merged(nh):
                for t in range(NT):
                    n = nh * NT + t
                    pe.wait_ge(s_mrg, n + 1)
                    if n >= 2:
                        pe.wait_ge(s_mtl, n - 1)
                    for i in range(4):
                        mm = pe.transpose(bank(6 + n % 2, i * P, (i + 1) * P), merged[:, t, i * P:(i + 1) * P], ident)
                    mm.then_inc(s_mtr, 1)

            pe.wait_ge(s_refill, 32)
            for j in range(5, 13):
                name = GN[j]
                if name[0] == "g":
                    product(j, hth, htl)
                else:
                    if j == 6:
                        pe.wait_ge(s_yl, 8)
                    o = 0 if name[1] == "a" else 4
                    product(j, lambda k, tt: yt_hi[:, o + k, tt], lambda k, tt: yt_lo[:, o + k, tt])
                if j == 9:
                    turn_merged(0)
            for n in range(8):
                if n == 0:
                    pe.wait_ge(s_free_d, freed_before("dve", NT * 13 - 1))
                    pe.wait_ge(s_free_a, freed_before("act", NT * 13 - 1))
                if n >= 2:
                    pe.wait_ge(s_row, 4 + n - 1)
                mod_product(4 + n, n % 2)
                if n == 0:
                    turn_merged(1)
                    pe.wait_ge(s_mtl, 2 * NT)
                if n:
                    (mod_spread if n - 1 in (0, 1, 6, 7) else mod_turn)(4 + n - 1, 4 + n - 1, mod_row2)
            mod_spread(11, 11, mod_row2)
            for j in (13, 14):
                product(j, lambda k, tt: mt_hi[:, k, tt], lambda k, tt: mt_lo[:, k, tt])
            pe.wait_ge(s_free_d, freed_before("dve", NT * 15 - 1))
            for k in range(KD):
                if k == 0:
                    pe.wait_ge(s_xf, NT)
                if k >= 3:
                    pe.wait_ge(s_h2, k - 2)
                for t in range(NTL):
                    pe.transpose(bank(2 * (k % 3), t * P, (t + 1) * P), xn_f[:, t, k * P:(k + 1) * P], ident)
                pe.transpose(bank(2 * (k % 3) + 1, 0, P),
                             xn_f[:, NTL, k * P:(k + 1) * P], ident).then_inc(s_x2t, 1)
            pe.wait_ge(s_router, 16)
            e16 = slice(0, NE)
            for k in range(KD):
                pe.wait_ge(s_h2, k + 1)
                pe.matmul(bank(6, rows=e16), router[:, k, :], h2_t[:, k, 0:LAT], start=(k == 0), stop=(k == KD - 1))
                mm = pe.matmul(bank(7, 0, CTX, rows=e16), router[:, k, :], h2_t[:, k, LAT:TOK],
                               start=(k == 0), stop=(k == KD - 1))
            mm.then_inc(s_lgt, 1)
            pe.wait_ge(s_lgc, 1)
            for t in range(NT):
                mm = pe.transpose(bank(0, t * NE, (t + 1) * NE), lg_t[:, t * P:(t + 1) * P], ident[0:NE, 0:NE])
            mm.then_inc(s_lgn, 1)
            pe.wait_ge(s_affn, 1)
            for t in range(NT):
                mm = pe.transpose(ps[0:NE, 512 + t * P:512 + (t + 1) * P], aff_n[:, t, :], ident)
            mm.then_inc(s_afft, 1)
            pe.wait_ge(s_pos, 1)
            for t in range(NT):
                mm = pe.transpose(bank(3, t * NE, (t + 1) * NE), pos_t[:, t * P:(t + 1) * P], ident[0:NE, 0:NE])
            mm.then_inc(s_post2, 1)
            pe.wait_ge(s_selc, 1)
            pe.wait_ge(s_xl, NT)
            flat_c = sel_c[:, :, :].rearrange("p e s -> p (e s)")
            for k in range(KD):
                if k >= 2:
                    pe.wait_ge(s_xc, k - 1)
                b = bank(4 + k % 2, 0, NE * CAPC)
                pe.matmul(b, xn_hi[:, NTL, k * P:(k + 1) * P], flat_c, start=True, stop=False)
                pe.matmul(b, xn_lo[:, NTL, k * P:(k + 1) * P], flat_c, start=False, stop=True).then_inc(s_gc, 1)

            def gather(n, k):
                if k == 0:
                    pe.wait_ge(s_selg, n * NTL + NTL)
                if k >= 4:
                    pe.wait_ge(s_xel, n * KD + k - 3)
                b = bank(k % 4, 0, EG * CAPL)
                for t in range(NTL):
                    pe.matmul(b, xn_hi[:, t, k * P:(k + 1) * P], sel_g[:, t, :], start=(t == 0), stop=False)
                    mm = pe.matmul(b, xn_lo[:, t, k * P:(k + 1) * P], sel_g[:, t, :],
                                   start=False, stop=(t == NTL - 1))
                mm.then_inc(s_g, 1)

            def combine(g1, n):
                t, d = n // 2, n % 2
                if n == 0:
                    pe.wait_ge(s_yel, g1 * EG)
                    pe.wait_ge(s_gate, g1 * 3 + 1)
                if n == 2 * NTL:
                    pe.wait_ge(s_yec, g1 * EG + 1)
                if n >= 2:
                    pe.wait_ge(s_add, g1 * 2 * NT + (n - 2 * NT))
                b = bank(6 + n % 2)
                ds = slice(d * NW, (d + 1) * NW)
                if t < NTL:
                    for pr in range(2):
                        st = sel_t[:, pr, t * P:(t + 1) * P]
                        pe.matmul(b, st, ye_hi[:, pr, ds], start=(pr == 0), stop=False)
                        mm = pe.matmul(b, st, ye_lo[:, pr, ds], start=False, stop=(pr == 1))
                else:
                    pe.matmul(b, sel_tc[:, :], yc_hi[:, ds], start=True, stop=False)
                    mm = pe.matmul(b, sel_tc[:, :], yc_lo[:, ds], start=False, stop=True)
                mm.then_inc(s_cmb, 1)

            for k in range(KD):
                gather(0, k)

            def body(i, first, last):
                H0 = DENSE_HALVES

                def hidden(e, b, hh0):
                    for q in range(4):
                        h = H0 + 24 * e + hh0 + q
                        pe.wait_ge(s_lo, i * GH + h + 1)
                        hi, lo = half_of(w_hi, h, NW), half_of(w_lo, h, NW)
                        for kk in range(2):
                            k = 2 * q + kk
                            w = slice(WIN[e], WIN[e] + P)
                            pe.matmul(bank(b), xe_hi[:, k, w], hi[:, kk, :], start=(k == 0), stop=False)
                            pe.matmul(bank(b), xe_hi[:, k, w], lo[:, kk, :], start=False, stop=False)
                            mm = pe.matmul(bank(b), xe_lo[:, k, w], hi[:, kk, :], start=False, stop=(k == KD - 1))
                        mm.then_inc(s_half, 1)
                        if e == 0 and not first and 2 <= hh0 + q < 2 + 2 * NT:
                            combine(i, hh0 + q - 2)

                def turn_hidden(e, f):
                    pe.wait_ge(s_hm, i * 8 + 2 * e + f + 1)
                    if not (e == 0):
                        pe.wait_ge(s_h2l, i * 8 + 2 * e + f - 1)
                    for k in range(4):
                        mm = pe.transpose(bank(6 + f, k * P, (k + 1) * P), h_act[:, f, k * P:(k + 1) * P], ident)
                    mm.then_inc(s_htr, 1)

                def down(e, hh):
                    h = H0 + 24 * e + 16 + hh
                    d, k0 = (hh // 2) % 2, 4 * (hh // 4) + 2 * (hh % 2)
                    if hh % 4 == 0:
                        pe.wait_ge(s_h2l, i * 8 + 2 * e + hh // 4 + 1)
                    pe.wait_ge(s_lo, i * GH + h + 1)
                    hi, lo = half_of(w_hi, h, NW), half_of(w_lo, h, NW)
                    for kk in range(2):
                        k = k0 + kk
                        b = bank(4 + d)
                        pe.matmul(b, ht2_hi[:, k, :], hi[:, kk, :], start=(k == 0), stop=False)
                        pe.matmul(b, ht2_hi[:, k, :], lo[:, kk, :], start=False, stop=False)
                        mm = pe.matmul(b, ht2_lo[:, k, :], hi[:, kk, :], start=False, stop=(k == KD - 1))
                    mm.then_inc(s_half, 1)

                pe.wait_ge(s_xel, i * KD + KD)
                pe.wait_ge(s_xeclo, 2 * i + 2)
                for e in range(EG):
                    hidden(e, 0, 0)
                    hidden(e, 2, 4)
                    hidden(e, 1, 8)
                    if e == 0 and not first:
                        pe.wait_ge(s_add, i * 2 * NT + 1)
                    turn_hidden(e, 0)
                    hidden(e, 3, 12)
                    if e:
                        pe.wait_ge(s_yel, i * EG + e)
                    for hh in range(8):
                        down(e, hh)
                        if hh == 1:
                            turn_hidden(e, 1)
                        if e == EG - 1 and not last:
                            gather(i + 1, hh)

            groups(pe, body)
            for n in range(2 * NT):
                combine(NG, n)

        @block.scalar
        def _(act):
            act.wait_ge(s_vec, 16 * 6)
            act.activation(vec[0:16, :], vec[0:16, :], ACT.Silu).then_inc(s_silu, 1)
            split_hi(act, 0)
            split_hi(act, 1)
            end_b = HALVES_B
            for j in range(4):
                for hh in range(4):
                    split_hi(act, FIRST[("mod", j)] + hh + 2)
                    t = {(1, 0): 0, (1, 2): 1, (2, 0): 2, (2, 2): 3, (3, 0): 4}.get((j, hh))
                    if t is not None:
                        act.wait_ge(s_x[t], 16)
                        if t:
                            act.wait_ge(s_ss, t)
                        act.activation(squares[:, :], x_n[:, t, :], ACT.Square, accum_out=ss[:, t:t + 1])\
                           .then_inc(s_ss, 1)

            act.wait_ge(s_scale, 1)
            for k in range(KD):
                act.wait_ge(s_xt, k + 1)
                act.activation(ht_hi[:, k, 0:LAT], bank(2 * (k % 4)), ACT.Identity, scale=scale1[:, k, 0:1],
                               bias=mod_t[:, k, 0:1])
                act.activation(ht_hi[:, k, LAT:TOK], bank(2 * (k % 4) + 1, 0, P), ACT.Identity,
                               scale=scale1[:, k, 1:2], bias=mod_t[:, k, 1:2]).then_inc(s_hth, 1)
            act.wait_ge(s_htl, KD)
            act.dma_start(ht_dram[:, 0, :].bitcast(F32), ht_hi[:, :, :].rearrange("p k t -> p (k t)").bitcast(F32))\
               .then_inc(s_spill, 16)
            act.dma_start(ht_dram[:, 1, :].bitcast(F32), ht_lo[:, :, :].rearrange("p k t -> p (k t)").bitcast(F32))\
               .then_inc(s_spill, 16)

            turned = [0]

            def key_copies(maps, kt):
                for g in range(0, maps, 4):
                    n = min(4, maps - g)
                    x0 = 0 if maps == KVA else KVA + g
                    act.wait_ge(s_ktr, turned[0] + 1)
                    b = 6 + turned[0] % 2
                    act.activation(keys_t[:, x0:x0 + n, kt * P:(kt + 1) * P],
                                   bank(b, 0, n * P).rearrange("p (m c) -> p m c", c=P), ACT.Copy).then_inc(s_kev, 1)
                    turned[0] += 1

            def lead(j, stop):
                for hh in range(NHALF[("gemm", j)]):
                    h = FIRST[("gemm", j)] + hh + 2
                    if h < stop:
                        split_hi(act, h)

            n_sq = [0]

            def square_of(j, t, cols):
                wait_product(act, j, t)
                if n_sq[0] >= 2:
                    act.wait_ge(s_qss, n_sq[0] - 1)
                act.activation(q_sq[:, n_sq[0] % 2, 0:cols], bank(product_bank(j, t), 0, cols), ACT.Square)\
                   .then_inc(s_qsq, 1)
                n_sq[0] += 1

            lead(0, end_b)
            act.wait_ge(s_lamw, 1)
            act.activation(lam[:, 0:2 * HB], lam[:, 0:2 * HB], ACT.Exp).then_inc(s_lame, 1)
            for t in range(NT):
                square_of(0, t, NW)
            key_copies(KVA, 0)
            key_copies(2 * HB, 0)
            key_copies(KVA, 1)
            key_copies(2 * HB, 1)
            lead(1, end_b)
            for t in range(NT):
                wait_product(act, 1, t)
                act.activation(q_n[:, t, HA:MAPS, :], bank(product_bank(1, t)).rearrange("p (m c) -> p m c", c=HD),
                               ACT.Copy).then_inc(s_free_a, 1)
            lead(2, end_b)
            for t in range(NT):
                square_of(2, t, P)
                act.activation(va_hi[:, 2 + t, :], bank(product_bank(2, t), P, 2 * P), ACT.Copy).then_inc(s_vah, 1)
            for hh in range(4):
                split_hi(act, FIRST[("gemm", 3)] + hh + 2)
                key_copies(KVA, 2 + hh)
            for t in range(NT):
                wait_product(act, 3, t)
                act.activation(k_n[:, t, KVA:, :], bank(product_bank(3, t)).rearrange("p (m c) -> p m c", c=HD),
                               ACT.Copy).then_inc(s_free_a, 1)
            key_copies(KVA, 2 + NTL)
            lead(4, end_b)
            for t in range(NTL - 1):
                key_copies(2 * HB, 2 + t)
            for t in range(NT):
                wait_product(act, 4, t)
                act.activation(vb_n[:, 2 + t, :], bank(product_bank(4, t)), ACT.Copy).then_inc(s_free_a, 1)
            key_copies(2 * HB, 2 + NTL - 1)
            key_copies(2 * HB, 2 + NTL)

            act.wait_ge(s_half, HALVES_B)
            act.wait_ge(s_spill, 32)
            for s in range(NU + LAG + 1):
                for m in range(MAPS):
                    if PREP[m] == s:
                        act.wait_ge(s_qtr, 2 * m + 1)
                        if m >= 2:
                            act.wait_ge(s_sc, U_LAST[m - 2] + 1)
                        act.activation(q_hi_t[:, m % 2, :], ps[:, 4 * 512:4 * 512 + TOK], ACT.Copy).then_inc(s_qh, 1)
                if s >= LAG and s - LAG in PU_OF:
                    i = PU_OF[s - LAG]
                    act.wait_ge(s_ptr, i + 1)
                    dst, src = prob_part(p_hi, i)
                    if BLK_OF[i] >= 2:
                        act.wait_ge(s_pv, BLK_OF[i] - 1)
                    act.activation(dst, src, ACT.Copy).then_inc(s_ph, 1)
                if s < NU:
                    _, t = UNITS[s]
                    act.wait_ge(s_max, s + 1)
                    if s >= 4:
                        if UNITS[s - 4][0] < HA:
                            act.wait_ge(s_ptr, PU_OF[s - 4] + 1)
                        elif s - 4 in PU_OF:
                            act.wait_ge(s_comb, PU_OF[s - 4] - HA * NT + 1)
                        else:
                            act.wait_ge(s_ptr, PU_OF[s - 3] + 1)
                    n = KTL * P if t < NTL else P
                    dst, src = probs[:, s % 4, 0:n], bank(2 * (s % 2), 0, n)
                    if t < NTL:
                        dst = dst.rearrange("p (a b) -> p a b", a=2)
                        src = ps[:, 1024 * (s % 2):1024 * (s % 2) + 1024].rearrange("p (a b) -> p a b", a=2)[:, :, 0:384]
                    act.activation(dst, src, ACT.Exp, bias=neg_max[:, s % 8:s % 8 + 1], scale=SCALE,
                                   accum_out=row_sum[:, s % 8:s % 8 + 1]).then_inc(s_exp, 1)
                if s - LAG - 1 in PU_OF and PU_OF[s - LAG - 1] in BLK_END.values():
                    blk = BLK_OF[PU_OF[s - LAG - 1]]
                    h, b = BLOCKS[blk]
                    n = 2 * P if b < 2 else P
                    act.wait_ge(s_pv, blk + 1)
                    rows = slice(0, P) if h >= HA else slice(64 * (h // 4), 64 * (h // 4) + 64)
                    y = 4 + h - HA if h >= HA else h % 4
                    act.activation(y_t[rows, y, 2 * P * b:2 * P * b + n], bank(6 + blk % 2, 0, n, rows), ACT.Copy)\
                       .then_inc(s_oev, 1)
            act.wait_ge(s_oev, len(BLOCKS))
            for h in range(HB + 1):
                if h < HB:
                    if h >= 2:
                        act.wait_ge(s_yms, h - 1)
                    act.activation(y_sq[:, h % 2, :], y_t[:, 4 + h, :], ACT.Square).then_inc(s_ysq, 1)
                if h:
                    act.wait_ge(s_yms, h)
                    if h >= 3:
                        act.wait_ge(s_yn, h - 2)
                    b = 1024 * ((h - 1) % 2)
                    act.activation(y_rms[:, (h - 1) % 2, :], ps[:, b:b + TOK], ACT.Sqrt, bias=eps).then_inc(s_yrt, 1)
            for i in range(8):
                if i >= 4:
                    act.wait_ge(s_yn, i - 3)
                act.activation(yt_hi[:, i, :], y_t[:, i, :], ACT.Copy).then_inc(s_yh, 1)
            act.wait_ge(s_pv, len(BLOCKS))
            for h in (HALVES_B, HALVES_B + 1):
                split_hi(act, h)
            act.wait_ge(s_yl, 8)
            def merged_hi(n):
                nh, t = n // NT, n % NT
                act.wait_ge(s_mtr, n + 1)
                act.activation(mt_hi[:, 4 * nh:4 * nh + 4, t * P:(t + 1) * P],
                               bank(6 + n % 2).rearrange("p (k c) -> p k c", c=P), ACT.Copy).then_inc(s_mth, 1)

            for j in range(5, 13):
                lead(j, DENSE_HALVES)
                if GN[j][0] == "g":
                    for t in range(NT):
                        wait_product(act, j, t)
                        if j > 5:
                            n = j // 2 - 3 + 1
                            act.wait_ge(s_mrg if GN[j][:2] == "ga" else s_free_d,
                                        t + 1 if GN[j][:2] == "ga" else freed_before("dve", NT * (j - 1) + t))
                        act.activation(sig[:, t, :], bank(product_bank(j, t)), ACT.Sigmoid).then_inc(s_free_a, 1)
                if j == 9:
                    for t in range(NT):
                        merged_hi(t)
            for n in range(8):
                for hh in range(4):
                    split_hi(act, FIRST[("mod", 4 + n)] + hh + 2)
                if n == 0:
                    for t in range(NT):
                        merged_hi(NT + t)
            for j in (13, 14):
                for hh in range(4):
                    split_hi(act, FIRST[("gemm", j)] + hh + 2)
            act.wait_ge(s_mod, 12)
            act.dma_start(g2_dram[:, :, :], gate2[:, :, :]).then_inc(s_g2out, 16)
            for t in range(NT):
                act.wait_ge(s_x1, t + 1)
                if t:
                    act.wait_ge(s_ss2, t)
                act.activation(squares2[:, :], x_r[:, t, :], ACT.Square, accum_out=ss[:, t:t + 1]).then_inc(s_ss2, 1)
            act.dma_start(x1_dram[:, :, :], x_r[:, :, :]).then_inc(s_x1out, 16)
            act.wait_ge(s_g2out, 16)
            for t in range(NT):
                act.wait_ge(s_xf, t + 1)
                act.activation(xn_hi[:, t, :], xn_f[:, t, :], ACT.Copy).then_inc(s_xh, 1)
            for k in range(KD):
                act.wait_ge(s_x2t, k + 1)
                act.activation(h2_t[:, k, 0:LAT], bank(2 * (k % 3)), ACT.Identity, scale=scale2[:, k, 0:1],
                               bias=mod_t[:, 24 + k, 0:1])
                act.activation(h2_t[:, k, LAT:TOK], bank(2 * (k % 3) + 1, 0, P), ACT.Identity,
                               scale=scale2[:, k, 1:2], bias=mod_t[:, 24 + k, 1:2]).then_inc(s_h2, 1)
            act.wait_ge(s_sub, 1)
            act.activation(soft[:, :, :], soft[:, :, :], ACT.Exp).then_inc(s_sexp, 1)
            act.wait_ge(s_route, 32)
            for k in range(KD):
                act.wait_ge(s_gc, k + 1)
                act.activation(xc_f[:, k, :], bank(4 + k % 2, 0, NE * CAPC), ACT.Identity,
                               scale=scale2[:, k, 1:2], bias=mod_t[:, 24 + k, 1:2]).then_inc(s_xc, 1)

            def gathered(n, k):
                act.wait_ge(s_g, n * KD + k + 1)
                act.activation(latent_slots(xe_hi, k), four(bank(k % 4, 0, EG * CAPL)), ACT.Identity,
                               scale=scale2[:, k, 0:1], bias=mod_t[:, 24 + k, 0:1]).then_inc(s_xeh, 1)

            act.wait_ge(s_clear, 1)
            for k in range(KD):
                gathered(0, k)

            def body(i, first, last):
                H0 = DENSE_HALVES

                def expert_split(h):
                    if last and h >= GH:
                        return
                    g = H0 + h
                    if h % 2 == 0:
                        act.wait_ge(s_raw[g // 2 % NRAW], expert_raw(h // 2, i))
                    act.wait_ge(s_half, i * GH + g - NHL + 1)
                    act.activation(w_hi[:, g % NHL, :], raw[:, g // 2 % NRAW, (g % 2) * HALF:(g % 2 + 1) * HALF],
                                   ACT.Copy).then_inc(s_hi, 1)

                def silu(e, f):
                    act.wait_ge(s_half, i * GH + H0 + 24 * e + 8 * f + 4)
                    if e:
                        act.wait_ge(s_htr, i * 8 + 2 * e + f - 1)
                    act.activation(h_act[:, f, :], bank(f), ACT.Silu).then_inc(s_silu2, 1)

                def hidden_hi(e, f):
                    act.wait_ge(s_htr, i * 8 + 2 * e + f + 1)
                    if e:
                        act.wait_ge(s_half, i * GH + H0 + 24 * e)
                    act.activation(ht2_hi[:, 4 * f:4 * f + 4, :], bank(6 + f).rearrange("p (k c) -> p k c", c=P),
                                   ACT.Copy).then_inc(s_h2h, 1)

                def output_hi(e):
                    act.wait_ge(s_yef, i * EG + e + 1)
                    e %= EG
                    rows = slice(64 * (e % 2), 64 * (e % 2) + 64)
                    act.activation(ye_hi[rows, e // 2, :], ye_f[rows, :], ACT.Copy).then_inc(s_yeh, 1)

                for e in range(EG):
                    for hh in range(24):
                        expert_split(24 * e + hh + 2)
                        if hh == 3:
                            silu(e, 0)
                        if hh == 1 and (e or not first):
                            output_hi(e - 1)
                        if hh == 11:
                            silu(e, 1)
                            hidden_hi(e, 0)
                        if hh == 17:
                            hidden_hi(e, 1)
                        if e == EG - 1 and hh >= 16 and not last:
                            gathered(i + 1, hh - 16)
                if last:
                    act.wait_ge(s_yef, NE)
                    act.activation(ye_hi[64:P, EG // 2 - 1, :], ye_f[64:P, :], ACT.Copy).then_inc(s_yeh, 1)

            act.wait_ge(s_selc, 1)
            groups(act, body)
            for t in range(NT):
                act.wait_ge(s_fx, t + 1)
                if t:
                    act.wait_ge(s_fss, t)
                act.activation(squares2[:, :], x_f[:, t, :], ACT.Square, accum_out=ss[:, t:t + 1]).then_inc(s_fss, 1)

        @block.vector
        def _(dve):
            n_own = [0]

            def own(n=1):
                n_own[0] += n
                return n_own[0]

            dve.wait_ge(s_vect, 1)
            dve.tensor_copy(vec_t[:, :], bank(5, 0, 81)).then_inc(s_dve, 1)
            dve.wait_ge(s_dve, own())
            cv = vec_t[:, 0:2 * KD].rearrange("p (v k) -> p k v", v=2)
            dve.memset(c_lo[:, :, :].bitcast(F32), 0.0).then_inc(s_dve, 1)
            dve.tensor_copy(c_hi[:, :, 0:2], cv).then_inc(s_dve, 1)
            dve.tensor_scalar(g_dif[:, :], vec_t[:, 80:81], 1.0 - LAM_INIT, None, ALU.mult).then_inc(s_dve, 1)
            dve.wait_ge(s_dve, own(3))
            dve.tensor_copy(c_lo[:, :, 0:2], cv).then_inc(s_dve, 1)
            dve.wait_ge(s_dve, own())
            dve.tensor_tensor(c_hi[:, :, 2:4], cv, c_hi[:, :, 0:2].bitcast(F32), ALU.subtract).then_inc(s_csplit, 1)
            split_lo(dve, 0)
            split_lo(dve, 1)

            def copy_row(j, b, rows):
                dve.wait_ge(s_half, FIRST[("mod", j)] + 4)
                if j >= 2:
                    dve.wait_ge(s_post, j - 1)
                dve.tensor_copy(rows[0:4, j % 2, :], bank(b, rows=slice(0, 4))).then_inc(s_row, 1)

            def add_bias(j):
                dve.wait_ge(s_post, j + 1)
                dve.tensor_tensor(mod_t[:, 4 * j:4 * j + 4, :], bank(6, 0, 8).rearrange("p (i v) -> p i v", v=2),
                                  vec_t[:, 32 + 4 * j:36 + 4 * j].unsqueeze(2).broadcast_to([P, 4, 2]), ALU.add)\
                   .then_inc(s_mod, 1)

            def scale_of(scale, k0, g):
                dve.scalar_tensor_tensor(scale[:, :, :], mod_t[:, k0:k0 + KD, :], 1.0,
                                         vec_t[:, g:g + KD].unsqueeze(2).broadcast_to([P, KD, 2]), ALU.add, ALU.mult)\
                   .then_inc(s_scale, 1)

            for j in range(4):
                for hh in range(4):
                    split_lo(dve, FIRST[("mod", j)] + hh + 2)
                copy_row(j, j % 2, mod_row)
                if j:
                    add_bias(j - 1)
                if j == 3:
                    add_bias(3)
                    dve.wait_ge(s_mod, 4)
                    scale_of(scale1, 8, 16)
                for t in ((), (), (0, 1), (2, 3, 4))[j]:
                    dve.wait_ge(s_rs, t + 1)
                    dve.tensor_scalar(x_n[:, t, :], x_n[:, t, :], rs[:, t:t + 1], None, ALU.mult).then_inc(s_xn, 1)
            dve.wait_ge(s_scale, 1)
            for k in range(KD):
                dve.wait_ge(s_xt, k + 1)
                dve.wait_ge(s_hth, k + 1)
                if k >= 2:
                    dve.wait_ge(s_htl, k - 1)
                tmp = h_tmp[k % 2]
                dve.tensor_scalar(tmp[:, 0:LAT], bank(2 * (k % 4)), scale1[:, k, 0:1], mod_t[:, k, 0:1],
                                  ALU.mult, ALU.add).then_inc(s_htf, 1)
                dve.tensor_scalar(tmp[:, LAT:TOK], bank(2 * (k % 4) + 1, 0, P),
                                  scale1[:, k, 1:2], mod_t[:, k, 1:2], ALU.mult, ALU.add).then_inc(s_htf, 1)

            def lead(j, stop):
                for hh in range(NHALF[("gemm", j)]):
                    h = FIRST[("gemm", j)] + hh + 2
                    if h < stop:
                        split_lo(dve, h)

            n_sq = [0]

            def sums_of(t, heads):
                dve.wait_ge(s_qsq, n_sq[0] + 1)
                dve.tensor_reduce(q_ss[:, t, 0:heads],
                                  q_sq[:, n_sq[0] % 2, 0:heads * HD].rearrange("p (m c) -> p m c", c=HD),
                                  AX.X, ALU.add).then_inc(s_qss, 1)
                n_sq[0] += 1

            def over_rms(dst, j, t, heads):
                src = bank(product_bank(j, t), 0, heads * HD).rearrange("p (m c) -> p m c", c=HD)
                return dve.tensor_tensor(dst, src, q_rs[:, t, 0:heads].unsqueeze(2).broadcast_to([P, heads, HD]),
                                         ALU.mult)

            dve.wait_ge(s_bc, 16 * 6)
            pairs = lam_w[:, :, :, :].rearrange("p (a b) h d -> p a b h d", b=2)
            dve.tensor_tensor(pairs[:, :, 0], pairs[:, :, 0], pairs[:, :, 1], ALU.mult).then_inc(s_dve, 1)
            dve.wait_ge(s_dve, own())
            dve.tensor_reduce(lam[:, 0:2 * HB].rearrange("p (a h) -> p a h", a=2), pairs[:, :, 0], AX.X, ALU.add)\
               .then_inc(s_lamw, 1)
            lead(0, HALVES_B)
            dve.wait_ge(s_lame, 1)
            dve.tensor_tensor(lam[:, 2 * HB:], lam[:, 0:HB], lam[:, HB:2 * HB], ALU.subtract).then_inc(s_dve, 1)
            dve.wait_ge(s_dve, own())
            dve.tensor_scalar(lam[:, 2 * HB:], lam[:, 2 * HB:], LAM_INIT, None, ALU.add).then_inc(s_dve, 1)
            dve.wait_ge(s_dve, own())
            for t in range(NT):
                sums_of(t, HA)
            for t in range(NT):
                dve.wait_ge(s_qrs, t + 1)
                over_rms(q_n[:, t, 0:HA, :], 0, t, HA).then_inc(s_free_d, 1)

            def by_position(x, t, heads):
                for step in rope(dve, x, heads, t, rope_d):
                    step.then_inc(s_dve, 1)
                    dve.wait_ge(s_dve, own())

            def finish_query(t):
                gain(dve, q_n[:, t, 0:HA, :], HA, 0).then_inc(s_dve, 1)
                dve.wait_ge(s_dve, own())
                if t < NTL:
                    by_position(q_n[:, t, 0:HA, :], t, HA)
                dve.sem_inc(s_qn, 1)

            dve.wait_ge(s_tab2, 16)
            dve.wait_ge(s_free_d, NT)
            for t in range(NT):
                if t < 4:
                    split_lo(dve, FIRST[("gemm", 1)] + t + 2)
                finish_query(t)
            lead(2, HALVES_B)
            for t in range(NT):
                sums_of(t, KVA)
            for t in range(NT):
                wait_product(dve, 2, t)
                dve.wait_ge(s_vah, t + 1)
                dve.wait_ge(s_qrs, NT + t + 1)
                over_rms(k_n[:, t, 0:KVA, :], 2, t, KVA).then_inc(s_dve, 1)
                own()
                v = bank(product_bank(2, t), P, 2 * P)
                if t == NTL:
                    dve.tensor_copy(va_ctx[:, :], v).then_inc(s_dve, 1)
                    own()
                dve.wait_ge(s_dve, own(0))
                dve.tensor_tensor(va_lo[:, 2 + t, :], v, va_hi[:, 2 + t, :].bitcast(F32), ALU.subtract)\
                   .then_inc(s_free_d, 1)
            for hh in range(4):
                split_lo(dve, FIRST[("gemm", 3)] + hh + 2)
                dve.wait_ge(s_free_a, hh + 1)
                by_position(q_n[:, hh, HA:MAPS, :], hh, 2 * HB)
                dve.sem_inc(s_qn, 1)
            lead(4, HALVES_B)
            for t in range(NTL):
                dve.wait_ge(s_free_a, NT + t + 1)
                by_position(k_n[:, t, KVA:, :], t, 2 * HB)
                dve.sem_inc(s_kn, 1)
            dve.wait_ge(s_spill, 32)
            dve.wait_ge(s_half, HALVES_B)
            dve.wait_ge(s_qn, NT)
            q = q_n[:, :, 0, :].unsqueeze(2).broadcast_to([P, NT, 2, HD])
            dve.tensor_copy(q_parts[:, :, 0:2, :], q).then_inc(s_dve, 1)
            dve.wait_ge(s_dve, own())
            dve.tensor_tensor(q_parts[:, :, 2:4, :], q, q_parts[:, :, 0:2, :].bitcast(F32), ALU.subtract)\
               .then_inc(s_qp, 1)

            for s in range(NU + LAG + 1):
                for m in range(MAPS):
                    if PREP[m] == s:
                        dve.wait_ge(s_qtr, 2 * m + 2)
                        if m >= 2:
                            dve.wait_ge(s_sc, U_LAST[m - 2] + 1)
                        dve.tensor_copy(q_lo_t[:, m % 2, :], ps[:, 4 * 512:4 * 512 + TOK]).then_inc(s_ql, 1)
                if s >= LAG and s - LAG in PU_OF:
                    i = PU_OF[s - LAG]
                    h, t, _ = PUS[i]
                    if h >= HA:
                        dve.wait_ge(s_c1, i - HA * NT + 1)
                        dve.wait_ge(s_rinv, s - LAG)
                        n = KTL * P if t < NTL else P
                        u = s - LAG - 1
                        dve.scalar_tensor_tensor(probs[:, u % 4, 0:n], probs[:, u % 4, 0:n],
                                                 row_inv[:, u % 8:u % 8 + 1], probs[:, (u + 1) % 4, 0:n],
                                                 ALU.mult, ALU.subtract).then_inc(s_comb, 1)
                if s < NU:
                    _, t = UNITS[s]
                    dve.wait_ge(s_sc, s + 1)
                    nm = neg_max[:, s % 8:s % 8 + 1]
                    if t < NTL:
                        src = ps[:, 1024 * (s % 2):1024 * (s % 2) + 1024].rearrange("p (a b) -> p a b", a=2)
                        dve.tensor_reduce(nm, src[:, :, 0:384], AX.XY, ALU.max).then_inc(s_dve, 1)
                    else:
                        dve.tensor_reduce(nm, bank(2 * (s % 2), 0, P), AX.X, ALU.max).then_inc(s_dve, 1)
                    dve.wait_ge(s_dve, own())
                    dve.tensor_scalar(nm, nm, -SCALE, None, ALU.mult).then_inc(s_max, 1)
                if 1 <= s <= NU:
                    m, n = UNITS[s - 1][0], (s - 1) % 8
                    dve.wait_ge(s_exp, s)
                    if m >= HA and (m - HA) % 2 == 1:
                        h = (m - HA) // 2
                        dve.reciprocal(row_inv[:, n:n + 1], row_sum[:, n:n + 1]).then_inc(s_dve, 1)
                        dve.wait_ge(s_dve, own())
                        dve.tensor_tensor(row_inv[:, n:n + 1], row_inv[:, n:n + 1],
                                          lam[:, 2 * HB + h:2 * HB + h + 1], ALU.mult).then_inc(s_rinv, 1)
                    else:
                        dve.reciprocal(row_inv[:, n:n + 1], row_sum[:, n:n + 1]).then_inc(s_rinv, 1)
                    second = m >= HA and (m - HA) % 2 == 1
                    if m < HA or second:
                        dve.wait_ge(s_rinv, s)
                        p = probs[:, (s - 1) % 4, 0:KTL * P if UNITS[s - 1][1] < NTL else P]
                        dve.tensor_scalar(p, p, row_inv[:, n:n + 1], None, ALU.mult)\
                           .then_inc(s_c1 if second else s_nrm, 1)
                if s >= LAG and s - LAG in PU_OF:
                    i = PU_OF[s - LAG]
                    h, t, _ = PUS[i]
                    dve.wait_ge(s_ph, i + 1)
                    dst, src = prob_part(p_lo, i)
                    hi, _ = prob_part(p_hi, i)
                    dve.tensor_tensor(dst, src, hi.bitcast(F32), ALU.subtract).then_inc(s_pl, 1)
            for h in range(HB):
                dve.wait_ge(s_yrt, h + 1)
                dve.reciprocal(y_rms[:, h % 2, :], y_rms[:, h % 2, :]).then_inc(s_dve, 1)
                dve.wait_ge(s_dve, own())
                dve.scalar_tensor_tensor(y_t[:, 4 + h, :], y_t[:, 4 + h, :], g_dif[:, 0:1], y_rms[:, h % 2, :],
                                         ALU.mult, ALU.mult).then_inc(s_yn, 1)
            dve.wait_ge(s_yn, HB)
            for i in range(8):
                dve.wait_ge(s_yh, i + 1)
                dve.tensor_tensor(yt_lo[:, i, :], y_t[:, i, :], yt_hi[:, i, :].bitcast(F32), ALU.subtract)\
                   .then_inc(s_yl, 1)
            for h in (HALVES_B, HALVES_B + 1):
                split_lo(dve, h)

            def merged_lo(n):
                nh, t = n // NT, n % NT
                dve.wait_ge(s_mth, n + 1)
                o = (slice(None), slice(4 * nh, 4 * nh + 4), slice(t * P, (t + 1) * P))
                dve.tensor_tensor(mt_lo[o], bank(6 + n % 2).rearrange("p (k c) -> p k c", c=P),
                                  mt_hi[o].bitcast(F32), ALU.subtract).then_inc(s_mtl, 1)

            for j in range(5, 13):
                lead(j, DENSE_HALVES)
                name = GN[j]
                for t in range(NT):
                    if name[0] == "w":
                        wait_product(dve, j, t)
                        b = bank(product_bank(j, t))
                        if j == 10:
                            dve.wait_ge(s_mtr, t + 1)
                        if name[1] == "a":
                            dve.tensor_tensor(merged[:, t, :], b, sig[:, t, :], ALU.mult).then_inc(s_free_d, 1)
                        else:
                            dve.tensor_tensor(sig[:, t, :], b, sig[:, t, :], ALU.mult).then_inc(s_free_d, 1)
                            dve.wait_ge(s_free_d, freed_before("dve", NT * j + t))
                            dve.tensor_tensor(merged[:, t, :], merged[:, t, :], sig[:, t, :], ALU.add)\
                               .then_inc(s_mrg, 1)
                if j == 9:
                    for t in range(NT):
                        merged_lo(t)
            for n in range(8):
                for hh in range(4):
                    split_lo(dve, FIRST[("mod", 4 + n)] + hh + 2)
                if n == 0:
                    for t in range(NT):
                        merged_lo(NT + t)
                copy_row(4 + n, n % 2, mod_row2)
                for i in ([n - 1] if n else []) + ([7] if n == 7 else []):
                    if i in (0, 1, 6, 7):
                        gate, g = (gate1, s_gb1) if i < 4 else (gate2, s_gb2)
                        dve.wait_ge(s_post, 4 + i + 1)
                        dve.wait_ge(g, 32)
                        cols = slice((i % 2) * NW, (i % 2 + 1) * NW)
                        dve.tensor_tensor(gate[:, :, cols], gate[:, :, cols],
                                          ps[:, 6 * 512:8 * 512].rearrange("p (v c) -> p v c", v=2), ALU.add)\
                           .then_inc(s_mod, 1)
                    else:
                        add_bias(4 + i)
                    if i == 5:
                        dve.wait_ge(s_mod, 10)
                        scale_of(scale2, 32, 24)
                        dve.wait_ge(s_scale, 2)
            dve.wait_ge(s_mod, 12)
            for j in (13, 14):
                for hh in range(4):
                    h = FIRST[("gemm", j)] + hh + 2
                    if h < DENSE_HALVES:
                        split_lo(dve, h)
                    else:
                        split_lo(dve, h)
                dve.wait_ge(s_xr, 32)
                cols = slice((j - 13) * NW, (j - 12) * NW)
                for t in range(NT):
                    wait_product(dve, j, t)
                    dve.tensor_tensor(out_tmp[:, t % 2, :], bank(product_bank(j, t)), gate1[:, t // NTL, cols],
                                      ALU.mult).then_inc(s_free_d, 1)
                    dve.wait_ge(s_free_d, freed_before("dve", NT * j + t))
                    dve.tensor_tensor(x_r[:, t, cols], x_r[:, t, cols], out_tmp[:, t % 2, :], ALU.add)\
                       .then_inc(s_x1 if j == 14 else s_dve, 1)
                if j == 13:
                    dve.wait_ge(s_dve, own(NT))

            dve.wait_ge(s_x1, NT)
            dve.wait_ge(s_rs2, 1)
            for t in range(NT):
                dve.tensor_scalar(xn_f[:, t, :], x_r[:, t, :], rs[:, t:t + 1], None, ALU.mult).then_inc(s_xf, 1)
            dve.wait_ge(s_xf, NT)
            e16 = slice(0, NE)
            dve.wait_ge(s_lgt, 1)
            dve.tensor_copy(lg_t[:, 0:LAT], bank(6, rows=e16)).then_inc(s_dve, 1)
            dve.tensor_copy(lg_t[:, LAT:TOK], bank(7, 0, CTX, rows=e16)).then_inc(s_lgc, 1)
            dve.wait_ge(s_dve, own())
            dve.wait_ge(s_lgn, 1)
            logits = bank(0, 0, NT * NE).rearrange("p (t e) -> p t e", e=NE)

            def over_experts(i):
                return soft_s[:, i, :].unsqueeze(2).broadcast_to([P, NT, NE])

            dve.tensor_reduce(soft_s[:, 0, :], logits, AX.X, ALU.max).then_inc(s_dve, 1)
            dve.wait_ge(s_dve, own())
            dve.tensor_tensor(soft[:, :, :], logits, over_experts(0), ALU.subtract).then_inc(s_sub, 1)
            dve.wait_ge(s_sexp, 1)
            dve.tensor_reduce(soft_s[:, 1, :], soft[:, :, :], AX.X, ALU.add).then_inc(s_dve, 1)
            dve.wait_ge(s_dve, own())
            dve.reciprocal(soft_s[:, 2, :], soft_s[:, 1, :]).then_inc(s_dve, 1)
            dve.wait_ge(s_dve, own())
            dve.tensor_tensor(aff_n[:, :, :], soft[:, :, :], over_experts(2), ALU.mult).then_inc(s_affn, 1)
            dve.wait_ge(s_afft, 1)
            dve.tensor_copy(aff_t[:, :], ps[e16, 512:512 + TOK]).then_inc(s_affc, 1)
            dve.wait_ge(s_affc, 1)
            dve.memset(ones16[:, :], 1.0).then_inc(s_dve, 1)
            dve.tensor_copy(left[:, :], aff_t[:, :]).then_inc(s_dve, 1)
            dve.wait_ge(s_dve, own(2))
            sets = ((slice(0, LAT), CAPL), (slice(LAT, TOK), CAPC))
            n_top = 0
            for cols, cap in sets:
                for _ in range(cap // 8):
                    dve.max(top8[:, n_top, :], left[:, cols]).then_inc(s_dve, 1)
                    dve.wait_ge(s_dve, own())
                    dve.match_replace(left[:, cols], top8[:, n_top, :], left[:, cols], -1.0).then_inc(s_dve, 1)
                    dve.wait_ge(s_dve, own())
                    n_top += 1
            dve.tensor_scalar(chosen[:, :], left[:, :], 0.0, None, ALU.is_lt).then_inc(s_dve, 1)
            dve.wait_ge(s_dve, own())
            for cols, cap in sets:
                n = cols.stop - cols.start
                dve.tensor_tensor_scan(count[:, cols], ones16[:, 0:n], chosen[:, cols], 0.0, ALU.mult, ALU.add)\
                   .then_inc(s_dve, 1)
            dve.wait_ge(s_dve, own(2))
            dve.tensor_tensor(count[:, :], count[:, :], chosen[:, :], ALU.mult).then_inc(s_dve, 1)
            dve.wait_ge(s_dve, own())
            dve.tensor_scalar(pos_t[:, :], count[:, :], -1.0, None, ALU.add).then_inc(s_pos, 1)
            dve.wait_ge(s_post2, 1)
            dve.tensor_copy(pos_n[:, :, :], bank(3, 0, NT * NE).rearrange("p (t e) -> p t e", e=NE))\
               .then_inc(s_posn, 1)
            dve.wait_ge(s_posn, 1)
            dve.wait_ge(s_x2t, KD)
            dve.wait_ge(s_xl, NT)
            dve.tensor_tensor(sel_c[:, :, :], tab[:, T_IOTA:T_IOTA + CAPC].unsqueeze(1).broadcast_to([P, NE, CAPC]),
                              pos_n[:, NTL, :].unsqueeze(2).broadcast_to([P, NE, CAPC]), ALU.is_equal)\
               .then_inc(s_selc, 1)

            def select_group(n):
                for t in range(NTL):
                    dve.tensor_tensor(sel_g[:, t, :].rearrange("p (e s) -> p e s", s=CAPL),
                                      tab[:, T_IOTA:T_IOTA + CAPL].unsqueeze(1).broadcast_to([P, EG, CAPL]),
                                      pos_n[:, t, bass.ds(n * EG, EG)].unsqueeze(2).broadcast_to([P, EG, CAPL]),
                                      ALU.is_equal).then_inc(s_selg, 1)

            def gathered(n, k):
                dve.wait_ge(s_g, n * KD + k + 1)
                dve.wait_ge(s_xeh, n * KD + k + 1)
                tmp = h_act[:, k % 2, 0:EG * CAPL]
                dve.tensor_scalar(tmp, bank(k % 4, 0, EG * CAPL), scale2[:, k, 0:1], mod_t[:, 24 + k, 0:1],
                                  ALU.mult, ALU.add).then_inc(s_xet, 1)
                dve.wait_ge(s_xet, n * KD + k + 1)
                dve.tensor_tensor(latent_slots(xe_lo, k), four(tmp), latent_slots(xe_hi, k).bitcast(F32),
                                  ALU.subtract).then_inc(s_xel, 1)

            def add_outputs(g1, n):
                t, cols = n // 2, slice(n % 2 * NW, (n % 2 + 1) * NW)
                if n == 0:
                    dve.wait_ge(s_add, g1 * 2 * NT + (1 - 2 * NT))
                dve.wait_ge(s_cmb, g1 * 2 * NT + (n + 1 - 2 * NT))
                dve.tensor_tensor(acc[:, t, cols], acc[:, t, cols], bank(6 + n % 2), ALU.add).then_inc(s_add, 1)

            select_group(0)
            dve.wait_ge(s_clear, 1)
            for k in range(KD):
                gathered(0, k)

            def body(i, first, last):
                H0 = DENSE_HALVES

                def expert_split(h):
                    if last and h >= GH:
                        return
                    g = H0 + h
                    dve.wait_ge(s_hi, i * GH + g + 1)
                    dve.tensor_tensor(w_lo[:, g % NHL, :], raw[:, g // 2 % NRAW, (g % 2) * HALF:(g % 2 + 1) * HALF],
                                      w_hi[:, g % NHL, :].bitcast(F32), ALU.subtract).then_inc(s_lo, 1)

                def select_slots(q):
                    order = (0, 2, 1)[q]
                    if q < 2:
                        dve.wait_ge(s_pb, 128 * i + (64, 128)[q])
                    else:
                        dve.wait_ge(s_pbc, 128 * i + 128)
                    n = LAT if q < 2 else CTX
                    dst = sel_t[:, q, :] if q < 2 else sel_tc[:, :]
                    places, gates = (pos_b, aff_b) if q < 2 else (pos_c, aff_c)
                    slot = T_SLAT if q < 2 else T_SCTX
                    dve.tensor_scalar(dst, places[:, 0:n], tab[:, slot:slot + 1], None, ALU.is_equal)\
                       .then_inc(s_selt, 1)
                    dve.wait_ge(s_selt, 3 * i + order + 1)
                    dve.tensor_tensor(gates[:, 0:n], gates[:, 0:n], dst.bitcast(F32), ALU.mult).then_inc(s_gm, 1)
                    dve.wait_ge(s_gm, 3 * i + order + 1)
                    dve.tensor_reduce(gate_p[:, q:q + 1], gates[:, 0:n], AX.X, ALU.add).then_inc(s_gate, 1)

                def gates_of_rows():
                    dve.wait_ge(s_gate, 3 * i + 4)
                    dve.wait_ge(s_clear, 1)
                    for v in range(2):
                        rows = slice(64 * v, 64 * v + 64)
                        by_pair = gate_e[rows, :].rearrange("p (a b) -> p b a", b=2)
                        dve.tensor_copy(by_pair[:, v, :], gate_p[rows, 0:2]).then_inc(s_gep, 1)
                    for e in range(EG):
                        rows = slice(CROW[e], CROW[e] + 32)
                        dve.tensor_copy(gate_e[rows, e:e + 1], gate_p[rows, 2:3]).then_inc(s_gep, 1)

                def hidden(e, f):
                    dve.wait_ge(s_half, i * GH + H0 + 24 * e + 8 * f + 8)
                    dve.wait_ge(s_silu2, i * 8 + 2 * e + f + 1)
                    dve.tensor_tensor(h_act[:, f, :], h_act[:, f, :], bank(2 + f), ALU.mult).then_inc(s_hm, 1)

                def hidden_lo(e, f):
                    dve.wait_ge(s_h2h, i * 8 + 2 * e + f + 1)
                    o = slice(4 * f, 4 * f + 4)
                    dve.tensor_tensor(ht2_lo[:, o, :], bank(6 + f).rearrange("p (k c) -> p k c", c=P),
                                      ht2_hi[:, o, :].bitcast(F32), ALU.subtract).then_inc(s_h2l, 1)

                def output(e):
                    dve.wait_ge(s_half, i * GH + H0 + 24 * e + 24)
                    dve.wait_ge(s_gep, 6 * i + (6 if e >= 0 else 0))
                    dve.wait_ge(s_yec, i * EG + e + 1)
                    dve.tensor_scalar(ye_f[:, :], ps[:, 4 * 512:6 * 512], gate_e[:, e % EG:e % EG + 1], None, ALU.mult)\
                       .then_inc(s_yef, 1)

                def output_lo(e):
                    dve.wait_ge(s_yef, i * EG + e + 1)
                    dve.wait_ge(s_yeh, i * EG + e + 1)
                    e %= EG
                    rows = slice(64 * (e % 2), 64 * (e % 2) + 64)
                    dve.tensor_tensor(ye_lo[rows, e // 2, :], ye_f[rows, :], ye_hi[rows, e // 2, :].bitcast(F32),
                                      ALU.subtract).then_inc(s_yel, 1)

                for e in range(EG):
                    for hh in range(24):
                        expert_split(24 * e + hh + 2)
                        if e == 0 and hh in (13, 15, 20):
                            select_slots({13: 0, 15: 2, 20: 1}[hh])
                        if e == 0 and hh == 22:
                            gates_of_rows()
                        if e == 0 and hh == 4 and not last:
                            select_group(i + 1)
                        if hh == 0 and (e or not first):
                            output(e - 1)
                        if hh == 2 and (e or not first):
                            output_lo(e - 1)
                        if e == 0 and not first and 2 <= hh < 2 + 2 * NT:
                            add_outputs(i, hh - 2)
                        if hh in (7, 15):
                            hidden(e, hh // 8)
                        if hh in (11, 17):
                            hidden_lo(e, hh // 17)
                        if e == EG - 1 and hh >= 16 and not last:
                            gathered(i + 1, hh - 16)
                if last:
                    output(EG - 1)
                    output_lo(EG - 1)

            def finish(t):
                if t < NT:
                    dve.wait_ge(s_add, (NG - 1) * 2 * NT + 2 * t + 3)
                    if t == 0:
                        dve.wait_ge(s_fin, 48)
                    dve.tensor_tensor(acc[:, t, :], acc[:, t, :], gate2_f[:, t // NTL, :], ALU.mult).then_inc(s_fg, 1)
                    dve.wait_ge(s_fg, t + 1)
                    dve.tensor_tensor(x_f[:, t, :], x_f[:, t, :], acc[:, t, :], ALU.add).then_inc(s_fx, 1)
                if t:
                    dve.wait_ge(s_frs, t)
                    dve.scalar_tensor_tensor(x_f[:, t - 1, :], x_f[:, t - 1, :], rs[:, t - 1:t], g_fin[:, :],
                                             ALU.mult, ALU.mult).then_inc(s_fy, 1)

            groups(dve, body)
            for t in range(NT):
                add_outputs(NG, 2 * t)
                add_outputs(NG, 2 * t + 1)
                finish(t)
            finish(NT)

        @block.gpsimd
        def _(pool):
            n_own = [0]

            def own(n=1):
                n_own[0] += n
                return n_own[0]

            pool.dma_start(tab2[:, :], constants[:, T_KEPT:T_W]).then_inc(s_tab2, 16)
            for n, src in enumerate((lambda_q1, lambda_k1, lambda_q2, lambda_k2)):
                flat = src.rearrange("a h d -> a (h d)")
                pool.dma_start(lam_w[:, n, :, :].rearrange("p h d -> p (h d)"), flat.to_broadcast([P, HB * HD]))\
                    .then_inc(s_bc, 16)
            pool.dma_start(g_qk[:, 0, :], g_q_norm.to_broadcast([P, HD])).then_inc(s_bc, 16)
            pool.dma_start(g_qk[:, 1, :], g_k_norm.to_broadcast([P, HD])).then_inc(s_bc, 16)

            def load_key_cache(n):
                rows = slice(n * P, (n + 1) * P)
                pool.dma_start(k_cache[:, 0:KVA, :], cache_attn_k[0, 0, rows]).then_inc(s_kc[n], 16)
                pool.dma_start(k_cache[:, KVA:, :].rearrange("p m d -> p (m d)"),
                               cache_diff_k[0, 0, rows].rearrange("p h i d -> p (h i d)")).then_inc(s_kc[n], 16)

            load_key_cache(0)
            pool.dma_start(va_cache[:, :, :], cache_attn_v[0, 0].rearrange("(t p) h d -> p t (h d)", p=P))\
                .then_inc(s_vac, 16)
            pool.dma_start(vb_n[:, 0:2, :], cache_diff_v[0, 0].rearrange("(t p) h d -> p t (h d)", p=P))\
                .then_inc(s_vc, 16)

            def one_over_rms(dst, sums, count_of, semaphore):
                pool.tensor_scalar(dst, sums, 1.0 / count_of, EPS, ALU.mult, ALU.add).then_inc(s_pool, 1)
                pool.wait_ge(s_pool, own())
                n = dst.shape[1]
                pool.tensor_tensor(dst, dst, minus_half.broadcast_to([P, n]), ALU.pow).then_inc(semaphore, 1)

            pool.wait_ge(s_tab, 16)
            pool.wait_ge(s_tab2, 16)
            for t in range(NT):
                pool.wait_ge(s_ss, t + 1)
                one_over_rms(rs[:, t:t + 1], ss[:, t:t + 1], D, s_rs)
            pool.wait_ge(s_vac, 16)
            pool.tensor_copy(va_hi[:, 0:2, :], va_cache[:, :, :]).then_inc(s_pool, 1)
            pool.wait_ge(s_pool, own())
            pool.tensor_tensor(va_lo[:, 0:2, :], va_cache[:, :, :], va_hi[:, 0:2, :].bitcast(F32), ALU.subtract)\
                .then_inc(s_pool, 1)
            pool.wait_ge(s_pool, own())

            turned = [0, 0]

            def make_parts(kind, src):
                parts = (ka_parts, kb_parts)[kind]
                if turned[kind]:
                    pool.wait_ge(s_ktr, turned[kind])
                turned[kind] = max(turned) + 1 + kind
                pool.tensor_copy(parts[:, :, 0, :], src).then_inc(s_pool, 1)
                pool.wait_ge(s_pool, own())
                pool.tensor_tensor(parts[:, :, 1, :], src, parts[:, :, 0, :].bitcast(F32), ALU.subtract)\
                    .then_inc(s_kparts, 1)

            for k in range(KD):
                pool.wait_ge(s_htf, 2 * k + 2)
                pool.tensor_tensor(ht_lo[:, k, :], h_tmp[k % 2][:, :], ht_hi[:, k, :].bitcast(F32), ALU.subtract)\
                    .then_inc(s_htl, 1)
            pool.wait_ge(s_kc[0], 32)
            make_parts(0, k_cache[:, 0:KVA, :])
            make_parts(1, k_cache[:, KVA:, :])
            pool.wait_ge(s_kparts, 2)
            load_key_cache(1)
            for t in range(NT):
                pool.wait_ge(s_qss, t + 1)
                one_over_rms(q_rs[:, t, :], q_ss[:, t, :], HD, s_qrs)
            pool.wait_ge(s_kc[1], 32)
            make_parts(0, k_cache[:, 0:KVA, :])
            make_parts(1, k_cache[:, KVA:, :])

            def rope_own(x, heads, t):
                for step in rope(pool, x, heads, t, rope_p):
                    step.then_inc(s_pool, 1)
                    pool.wait_ge(s_pool, own())

            def gain_own(x, heads, which):
                gain(pool, x, heads, which).then_inc(s_pool, 1)
                pool.wait_ge(s_pool, own())

            pool.wait_ge(s_bc, 16 * 6)
            for t in range(NT):
                pool.wait_ge(s_qss, NT + t + 1)
                one_over_rms(q_rs[:, t, 0:KVA], q_ss[:, t, 0:KVA], HD, s_qrs)
            for t in range(NT):
                pool.wait_ge(s_free_d, NT + t + 1)
                gain_own(k_n[:, t, 0:KVA, :], KVA, 1)
                if t < NTL:
                    rope_own(k_n[:, t, 0:KVA, :], KVA, t)
                make_parts(0, k_n[:, t, 0:KVA, :])
            for t in range(NT):
                if t < NTL:
                    pool.wait_ge(s_kn, t + 1)
                else:
                    pool.wait_ge(s_free_a, NT + t + 1)
                make_parts(1, k_n[:, t, KVA:, :])
            pool.dma_start(new_attn_k[0, 0], k_n[:, NTL, 0:KVA, :]).then_inc(s_kout, 16)
            pool.dma_start(new_diff_k[0, 0].rearrange("p h i d -> p (h i d)"),
                           k_n[:, NTL, KVA:, :].rearrange("p m d -> p (m d)")).then_inc(s_kout, 16)
            pool.dma_start(new_attn_v[0, 0].rearrange("p h d -> p (h d)"), va_ctx[:, :]).then_inc(s_out, 16)
            def query_parts(m):
                pool.wait_ge(s_qtr, 2 * m)
                pool.wait_ge(s_qn, NT if m < HA else NT + NTL)
                q = q_n[:, :, m, :].unsqueeze(2).broadcast_to([P, NT, 2, HD])
                pool.tensor_copy(q_parts[:, :, 0:2, :], q).then_inc(s_pool, 1)
                pool.wait_ge(s_pool, own())
                pool.tensor_tensor(q_parts[:, :, 2:4, :], q, q_parts[:, :, 0:2, :].bitcast(F32), ALU.subtract)\
                    .then_inc(s_qp, 1)

            def value_parts(h):
                if h:
                    pool.wait_ge(s_pv, 3 * (HA + h))
                v = vb_n[:, :, h * P:(h + 1) * P]
                pool.tensor_copy(vb_hi[:, :, :], v).then_inc(s_pool, 1)
                pool.wait_ge(s_pool, own())
                pool.tensor_tensor(vb_lo[:, :, :], v, vb_hi[:, :, :].bitcast(F32), ALU.subtract).then_inc(s_vb, 1)

            pool.wait_ge(s_free_a, 3 * NT)
            pool.dma_start(new_diff_v[0, 0].rearrange("p h d -> p (h d)"), vb_n[:, 2 + NTL, :]).then_inc(s_out, 16)
            pool.wait_ge(s_kout, 32)
            query_parts(1)
            for s in range(1, NU + LAG + 3):
                for m in range(1, MAPS - 1):
                    if PREP[m] + 1 == s:
                        query_parts(m + 1)
                if s == U_FIRST[2]:
                    pool.wait_ge(s_vc, 16)
                    value_parts(0)
                for h in range(1, HB):
                    if PUS[NT * (HA + h) - 1][2] + 4 == s:
                        value_parts(h)
            pool.wait_ge(s_pv, len(BLOCKS))
            pool.dma_start(ht_hi[:, :, :].rearrange("p k t -> p (k t)"), ht_dram[:, 0, :]).then_inc(s_refill, 16)
            pool.dma_start(ht_lo[:, :, :].rearrange("p k t -> p (k t)"), ht_dram[:, 1, :]).then_inc(s_refill, 16)
            pool.wait_ge(s_half, FIRST[("gemm", 11)] + NHALF[("gemm", 11)])
            for gate, part, semaphore in ((gate1, 2, s_gb1), (gate2, 5, s_gb2)):
                for v in range(2):
                    pool.dma_start(gate[:, v, :], b_mod[:, part * D:(part + 1) * D].to_broadcast([P, D]))\
                        .then_inc(semaphore, 16)
            pool.wait_ge(s_half, FIRST[("gemm", 12)] + NHALF[("gemm", 12)])
            pool.dma_start(x_r[:, 0:NTL, :], x_sample[0].rearrange("(t p) d -> p t d", p=P)).then_inc(s_xr, 16)
            pool.dma_start(x_r[:, NTL, :], x_prompt[0]).then_inc(s_xr, 16)
            pool.wait_ge(s_half, DENSE_HALVES)
            pool.dma_start(router[:, :, :], w_router[0].rearrange("(k p) e -> p k e", p=P)).then_inc(s_router, 16)
            pool.wait_ge(s_ss2, NT)
            one_over_rms(rs[:, :], ss[:, :], D, s_rs2)
            for t in range(NT):
                pool.wait_ge(s_xh, t + 1)
                pool.tensor_tensor(xn_lo[:, t, :], xn_f[:, t, :], xn_hi[:, t, :].bitcast(F32), ALU.subtract)\
                    .then_inc(s_xl, 1)
            pool.wait_ge(s_x1out, 16)
            pool.wait_ge(s_xf, NT)
            pool.memset(acc[:, :, :], 0.0).then_inc(s_add, 1)
            pool.wait_ge(s_xl, NT)
            pool.wait_ge(s_x2t, KD)
            pool.memset(yc_hi[:, :].bitcast(F32), 0.0).then_inc(s_pool, 1)
            pool.memset(yc_lo[:, :].bitcast(F32), 0.0).then_inc(s_yec, 1)
            pool.memset(gate_e[:, :], 0.0).then_inc(s_gate, 1)
            pool.wait_ge(s_lgt, 1)
            pool.memset(xe_hi[:, :, :].bitcast(F32), 0.0).then_inc(s_pool, 1)
            pool.wait_ge(s_pool, own(2))
            pool.wait_ge(s_add, 1)
            pool.wait_ge(s_yec, 1)
            pool.wait_ge(s_gate, 1)
            pool.memset(xe_lo[:, :, :].bitcast(F32), 0.0).then_inc(s_clear, 1)
            pool.wait_ge(s_clear, 1)
            pool.wait_ge(s_affc, 1)
            pool.dma_start(aff_dram[:, :], aff_t[:, :]).then_inc(s_route, 16)
            pool.wait_ge(s_pos, 1)
            pool.dma_start(pos_dram[:, :], pos_t[:, :]).then_inc(s_route, 16)
            pool.wait_ge(s_route, 32)

            H0 = DENSE_HALVES

            def context_columns(n, before):
                pool.wait_ge(s_xc, KD)
                pool.wait_ge(s_half, before)
                pool.tensor_copy(xc_g[:, :, :], xc_f[:, :, bass.ds(n * EG * CAPC, EG * CAPC)]).then_inc(s_xcg, 1)
                pool.wait_ge(s_xcg, n + 1)
                for v, col in enumerate((CCOL[0], CCOL[2])):
                    src = xc_g[:, :, 2 * v * CAPC:2 * (v + 1) * CAPC]
                    pool.tensor_tensor(xe_hi[:, :, col:col + 2 * CAPC], src,
                                       one.unsqueeze(2).broadcast_to([P, KD, 2 * CAPC]), ALU.mult).then_inc(s_xech, 1)
                pool.wait_ge(s_xech, 2 * n + 2)
                for v, col in enumerate((CCOL[0], CCOL[2])):
                    src = xc_g[:, :, 2 * v * CAPC:2 * (v + 1) * CAPC]
                    pool.tensor_tensor(xe_lo[:, :, col:col + 2 * CAPC], src,
                                       xe_hi[:, :, col:col + 2 * CAPC].bitcast(F32), ALU.subtract)\
                        .then_inc(s_xeclo, 1)

            context_columns(0, H0)

            def body(i, first, last):
                def spread(dst, src, e, rows, cols, semaphore):
                    pool.dma_start(dst[rows, 0:cols.stop - cols.start],
                                   src[bass.ds(i * EG + e, 1), cols].to_broadcast(
                                       [rows.stop - rows.start, cols.stop - cols.start])).then_inc(semaphore, 16)

                pool.wait_ge(s_xeclo, 2 * i + 2)
                for q in (0, 2, 1):
                    pool.wait_ge(s_gate, i * 3 + (2 if q == 1 else 1))
                    if q < 2:
                        for dst, src in ((pos_b, pos_dram), (aff_b, aff_dram)):
                            for v in range(2):
                                spread(dst, src, 2 * q + v, slice(64 * v, 64 * v + 64), slice(0, LAT),
                                       s_pb)
                    else:
                        for dst, src in ((pos_c, pos_dram), (aff_c, aff_dram)):
                            for e in range(EG):
                                r = CROW[e]
                                spread(dst, src, e, slice(r, r + 32), slice(LAT, TOK), s_pbc)
                for e in range(EG):
                    rows = slice(CROW[e], CROW[e] + CAPC)
                    if e == EG - 1 and not last:
                        pool.wait_ge(s_yec, i * EG + e + 1)
                        context_columns(i + 1, i * GH + (H0 + 24 * e + 16))
                        pool.wait_ge(s_xeclo, 2 * i + 4)
                    pool.wait_ge(s_yec, i * EG + e + 1)
                    pool.wait_ge(s_yef, i * EG + e + 1)
                    pool.tensor_tensor(yc_hi[rows, :], ye_f[rows, :], one[rows].broadcast_to([CAPC, D]), ALU.mult)\
                        .then_inc(s_ych, 1)
                    pool.wait_ge(s_ych, i * EG + e + 1)
                    pool.tensor_tensor(yc_lo[rows, :], ye_f[rows, :], yc_hi[rows, :].bitcast(F32), ALU.subtract)\
                        .then_inc(s_yec, 1)

            body(0, True, False)
            with pool.Fori(1, NG - 1) as i:
                body(i, False, False)
            pool.wait_ge(s_g, NG * KD)
            pool.dma_start(x_f[:, :, :], x1_dram[:, :, :]).then_inc(s_fin, 16)
            pool.dma_start(gate2_f[:, :, :], g2_dram[:, :, :]).then_inc(s_fin, 16)
            pool.dma_start(g_fin[:, :], g_final.rearrange("(a n) -> a n", a=1).to_broadcast([P, D]))\
                .then_inc(s_fin, 16)
            body(NG - 1, False, True)
            pool.wait_ge(s_yec, NE + 1)
            ys = y_sample[0].rearrange("(t p) d -> t p d", p=P)
            for t in range(NT + 1):
                if t < NT:
                    pool.wait_ge(s_fss, t + 1)
                    one_over_rms(rs[:, t:t + 1], ss[:, t:t + 1], D, s_frs)
                if t == 0:
                    continue
                t -= 1
                pool.wait_ge(s_fy, t + 1)
                pool.dma_start(ys[t] if t < NTL else y_prompt[0], x_f[:, t, :]).then_inc(s_out, 16)
            pool.wait_ge(s_out, 16 * (2 + NT))


_INS = ["x_prompt", "x_sample", "cache_attn_k", "cache_attn_v", "cache_diff_k", "cache_diff_v", "c", "c_ctx",
        "w_mod", "b_mod", "g_attn_norm", "g_ffn_norm", "w_in", "g_q_norm", "g_k_norm", "lambda_q1", "lambda_k1",
        "lambda_q2", "lambda_k2", "g_diff_norm", "w_branch_a", "w_branch_b", "w_out", "w_router", "w_exp_gate",
        "w_exp_up", "w_exp_down", "g_final"]
_OUTS = [(1, CTX, D), (1, LAT, D), (1, 1, CTX, KVA, HD), (1, 1, CTX, KVA, HD), (1, 1, CTX, HB, 2, HD),
         (1, 1, CTX, HB, 2 * HD)]


def kernel(**inputs):
    import numpy as _np
    import concourse.bacc as _bacc
    from concourse import mybir as _mybir
    from concourse.bass_utils import run_bass_kernel_spmd as _run

    nc = _bacc.Bacc("TRN2", target_bir_lowering=False, num_devices=1)
    arrays, args = {}, []
    for name in _INS:
        a = _np.ascontiguousarray(inputs[name])
        arrays[f"in_{name}_dram"] = a
        args.append(nc.dram_tensor(f"in_{name}_dram", a.shape, _mybir.dt.from_np(a.dtype), kind="ExternalInput").ap())
    a = table_of_constants()
    arrays["in_constants_dram"] = a
    args.append(nc.dram_tensor("in_constants_dram", a.shape, _mybir.dt.float32, kind="ExternalInput").ap())
    for i, shape in enumerate(_OUTS):
        args.append(nc.dram_tensor(f"out_{i}_dram", shape, _mybir.dt.float32, kind="ExternalOutput").ap())
    build(nc, *args)
    r = _run(nc, [arrays], core_ids=[0])
    return tuple(r.results[0][f"out_{i}_dram"] for i in range(len(_OUTS)))
```
